# Optimizing a Trainium2 kernel written in Bass

```python
import jax, jax.numpy as jnp
from jax import lax
import numpy as np
import math

D_MODEL = 1024
BATCH = 1
SEQ = 512
DEPTH = 1

SB_HEADS = 8
SB_HEAD_DIM = 64
SB_WIDTH = SB_HEADS * SB_HEAD_DIM
Q_BLOCK = 128
CONV_GROUPS = 8
CONV_GROUP_DIM = 64
CONV_WIDTH = CONV_GROUPS * CONV_GROUP_DIM
CONV_KSIZE = 3
N_BRANCHES = 2
N_GROUPS = 4
EXPERTS_PER_GROUP = 8
N_EXPERTS = N_GROUPS * EXPERTS_PER_GROUP
TOP_K_IN_GROUP = 2
D_EXPERT = 256
NORM_EPS = 1e-6
IN_SIZES = (SB_WIDTH, SB_WIDTH, SB_WIDTH, CONV_WIDTH, CONV_WIDTH, CONV_WIDTH, D_MODEL, D_MODEL)
IN_PROJ_WIDTH = sum(IN_SIZES)
IN_SPLITS = tuple(int(s) for s in np.cumsum(IN_SIZES)[:-1])


def rms_norm(x, g):
    xf = x.astype(jnp.float32)
    y = xf * lax.rsqrt(jnp.mean(xf * xf, axis=-1, keepdims=True) + NORM_EPS)
    return (y * g.astype(jnp.float32)).astype(x.dtype)

def stick_breaking_attention(q, k, v):
    B, H, S, dh = q.shape
    n_blocks = S // Q_BLOCK
    scale = SB_HEAD_DIM ** -0.5
    kf = k.astype(jnp.float32)
    vf = v.astype(jnp.float32)
    key_pos = jnp.arange(S)

    def one_block(i):
        start = i * Q_BLOCK
        qb = lax.dynamic_slice_in_dim(q, start, Q_BLOCK, axis=2).astype(jnp.float32)
        z = jnp.einsum('bhqd,bhkd->bhqk', qb, kf) * scale
        q_pos = start + jnp.arange(Q_BLOCK)
        mask = key_pos[None, :] < q_pos[:, None]
        neg_log_1m_beta = jnp.where(mask, jax.nn.softplus(z), 0.0)
        tail = lax.cumsum(neg_log_1m_beta, axis=3, reverse=True) - neg_log_1m_beta
        a = jnp.where(mask, jnp.exp(jax.nn.log_sigmoid(z) - tail), 0.0)
        return jnp.einsum('bhqk,bhkd->bhqd', a, vf)

    out = lax.map(one_block, jnp.arange(n_blocks))
    out = jnp.transpose(out, (1, 0, 3, 2, 4)).reshape(B, S, H * dh)
    return out.astype(q.dtype)

def short_conv_mixer(b_gate, c_gate, u, conv_w):
    S = u.shape[1]
    cu = c_gate * u
    cu_pad = jnp.pad(cu, ((0, 0), (CONV_KSIZE - 1, 0), (0, 0)))
    y = conv_w[0] * cu_pad[:, 0:S]
    for j in range(1, CONV_KSIZE):
        y = y + conv_w[j] * cu_pad[:, j:j + S]
    return b_gate * y

def hierarchical_moe(h, w_rg, b_rg, w_re, b_re, w_gate, w_up, w_down):
    N = h.shape[0]
    hf = h.astype(jnp.float32)
    g_logits = hf @ w_rg.astype(jnp.float32) + b_rg.astype(jnp.float32)
    g_prob = jax.nn.softmax(g_logits, axis=-1)
    _, g_idx = lax.top_k(g_logits, 1)
    g_w = jnp.take_along_axis(g_prob, g_idx, axis=-1)
    e_logits = (hf @ w_re.astype(jnp.float32) + b_re.astype(jnp.float32)).reshape(N, N_GROUPS, EXPERTS_PER_GROUP)
    e_in_group = jnp.take_along_axis(e_logits, g_idx[:, :, None], axis=1)[:, 0]
    top_v, top_i = lax.top_k(e_in_group, TOP_K_IN_GROUP)
    top_w = jax.nn.softmax(top_v, axis=-1)
    within = jnp.sum(jax.nn.one_hot(top_i, EXPERTS_PER_GROUP, dtype=jnp.float32) * top_w[..., None], axis=1)
    combine = (jax.nn.one_hot(g_idx[:, 0], N_GROUPS, dtype=jnp.float32)[:, :, None]
               * within[:, None, :] * g_w[:, :, None]).astype(h.dtype)
    y = jnp.zeros_like(h)
    for g in range(N_GROUPS):
        sl = slice(g * EXPERTS_PER_GROUP, (g + 1) * EXPERTS_PER_GROUP)
        act = jax.nn.silu(jnp.einsum('nd,edf->nef', h, w_gate[sl])) * jnp.einsum('nd,edf->nef', h, w_up[sl])
        act = act * combine[:, g, :, None]
        y = y + jnp.einsum('nef,efd->nd', act, w_down[sl])
    return y

def first_inputs(seed: int = 0) -> dict:
    key = jax.random.key(seed)
    ks = jax.random.split(key, 20)
    f32 = jnp.float32
    nrm = lambda k, shape, fan_in: jax.random.normal(k, shape, f32) * (fan_in ** -0.5)
    gain = lambda k, shape: 1.0 + 0.05 * jax.random.normal(k, shape, f32)
    return {
        "x": jax.random.normal(ks[0], (BATCH, SEQ, D_MODEL), f32),
        "norm_mix_g": gain(ks[1], (DEPTH, D_MODEL)),
        "w_in": nrm(ks[2], (DEPTH, D_MODEL, IN_PROJ_WIDTH), D_MODEL),
        "q_norm_g": gain(ks[3], (DEPTH, SB_HEAD_DIM)),
        "k_norm_g": gain(ks[4], (DEPTH, SB_HEAD_DIM)),
        "conv_w": nrm(ks[5], (DEPTH, CONV_KSIZE, CONV_WIDTH), CONV_KSIZE),
        "w_sb_branch": nrm(ks[6], (DEPTH, SB_WIDTH, D_MODEL), SB_WIDTH),
        "w_conv_branch": nrm(ks[7], (DEPTH, CONV_WIDTH, D_MODEL), CONV_WIDTH),
        "w_out": nrm(ks[8], (DEPTH, D_MODEL, D_MODEL), D_MODEL),
        "norm_ffn_g": gain(ks[9], (DEPTH, D_MODEL)),
        "w_router_group": nrm(ks[10], (DEPTH, D_MODEL, N_GROUPS), D_MODEL),
        "b_router_group": 0.01 * jax.random.normal(ks[11], (DEPTH, N_GROUPS), f32),
        "w_router_expert": nrm(ks[12], (DEPTH, D_MODEL, N_EXPERTS), D_MODEL),
        "b_router_expert": 0.01 * jax.random.normal(ks[13], (DEPTH, N_EXPERTS), f32),
        "w_gate_e": nrm(ks[14], (DEPTH, N_EXPERTS, D_MODEL, D_EXPERT), D_MODEL),
        "w_up_e": nrm(ks[15], (DEPTH, N_EXPERTS, D_MODEL, D_EXPERT), D_MODEL),
        "w_down_e": nrm(ks[16], (DEPTH, N_EXPERTS, D_EXPERT, D_MODEL), D_EXPERT),
    }

def first_block(x, norm_mix_g, w_in, q_norm_g, k_norm_g, conv_w, w_sb_branch, w_conv_branch,
              w_out, norm_ffn_g, w_router_group, b_router_group, w_router_expert,
              b_router_expert, w_gate_e, w_up_e, w_down_e):
    B, S, D = x.shape
    for l in range(DEPTH):
        h = rms_norm(x, norm_mix_g[l])
        proj = h @ w_in[l]
        q, k, v, c_b, c_c, c_u, g_a, g_b = jnp.split(proj, IN_SPLITS, axis=-1)
        q = rms_norm(q.reshape(B, S, SB_HEADS, SB_HEAD_DIM), q_norm_g[l]).transpose(0, 2, 1, 3)
        k = rms_norm(k.reshape(B, S, SB_HEADS, SB_HEAD_DIM), k_norm_g[l]).transpose(0, 2, 1, 3)
        v = v.reshape(B, S, SB_HEADS, SB_HEAD_DIM).transpose(0, 2, 1, 3)
        branch_a = stick_breaking_attention(q, k, v) @ w_sb_branch[l]
        branch_b = short_conv_mixer(c_b, c_c, c_u, conv_w[l]) @ w_conv_branch[l]
        merged = jax.nn.sigmoid(g_a) * branch_a + jax.nn.sigmoid(g_b) * branch_b
        x = x + merged @ w_out[l]
        h2 = rms_norm(x, norm_ffn_g[l]).reshape(B * S, D)
        y = hierarchical_moe(h2, w_router_group[l], b_router_group[l], w_router_expert[l],
                             b_router_expert[l], w_gate_e[l], w_up_e[l], w_down_e[l])
        x = x + y.reshape(B, S, D)
    return x


GRID_W = 64
CTX_LEN = 256
EPS = 1e-6

N_HEADS = 8
N_KV_HEADS = 2
HEAD_DIM = 64
AXIS_ROPE_DIM = HEAD_DIM // 2
ROPE_THETA = 10000.0

HY_DIM = D_MODEL // 2
HY_ORDER = 2
HY_SHORT = 3
HY_EMB_BANDS = 16
HY_EMB_DIM = 1 + 2 * HY_EMB_BANDS
HY_FFN = 64
HY_FAST_DECAY = 0.3
HY_SLOW_DECAY = 1.5
HY_TARGET = 1e-2

Q_DIM = N_HEADS * HEAD_DIM
KV_DIM = N_KV_HEADS * HEAD_DIM
HY_COLS = (HY_ORDER + 1) * HY_DIM
GATE_COLS = 2 * D_MODEL
IN_COLS = Q_DIM + 2 * KV_DIM + HY_COLS + GATE_COLS

PEER_HEADS = 8
PEER_N_KEYS = 128
PEER_N_EXPERTS = PEER_N_KEYS * PEER_N_KEYS
PEER_DK = 256
PEER_TOPK = 16
PEER_CHUNK = 128


def rmsnorm(x, g):
    xf = x.astype(jnp.float32)
    y = xf * lax.rsqrt(jnp.mean(xf * xf, axis=-1, keepdims=True) + EPS)
    return (y * g.astype(jnp.float32)).astype(x.dtype)

def modulate(h, shift, scale):
    return h * (1.0 + scale) + shift

def axial_rope(rows):
    t = jnp.arange(rows * GRID_W)
    row = (t // GRID_W).astype(jnp.float32)
    col = (t % GRID_W).astype(jnp.float32)
    inv = ROPE_THETA ** (-jnp.arange(0, AXIS_ROPE_DIM, 2, dtype=jnp.float32) / AXIS_ROPE_DIM)
    ar = row[:, None] * inv
    ac = col[:, None] * inv
    ang = jnp.concatenate([ar, ar, ac, ac], axis=-1)
    return jnp.cos(ang), jnp.sin(ang)

def apply_rope(x, cos, sin):
    xf = x.astype(jnp.float32)
    half = AXIS_ROPE_DIM // 2

    def rot(a):
        return jnp.concatenate([-a[..., half:], a[..., :half]], axis=-1)

    xr = jnp.concatenate([rot(xf[..., :AXIS_ROPE_DIM]), rot(xf[..., AXIS_ROPE_DIM:])], axis=-1)
    return (xf * cos[:, None] + xr * sin[:, None]).astype(x.dtype)

def gqa_blocks(q, k, v):
    B, L, _, _ = q.shape
    G = N_HEADS // N_KV_HEADS
    nb = L // Q_BLOCK
    qb = jnp.moveaxis(q.reshape(B, nb, Q_BLOCK, N_KV_HEADS, G, HEAD_DIM), 1, 0)
    scale = HEAD_DIM ** -0.5

    def one_block(qblk):
        s = jnp.einsum('bqkgd,btkd->bkgqt', qblk, k) * scale
        p = jax.nn.softmax(s.astype(jnp.float32), axis=-1).astype(v.dtype)
        return jnp.einsum('bkgqt,btkd->bqkgd', p, v)

    o = lax.map(one_block, qb)
    return jnp.moveaxis(o, 0, 1).reshape(B, L, Q_DIM)

def short_conv(z, w, b):
    zp = jnp.pad(z, ((0, 0), (1, 1), (0, 0)))
    return zp[:, :-2] * w[0] + zp[:, 1:-1] * w[1] + zp[:, 2:] * w[2] + b

def implicit_filters(L, w1, b1, w2, b2, w3, b3, w4, freq):
    t01 = jnp.linspace(0.0, 1.0, L, dtype=jnp.float32)[:, None]
    w = 2.0 * math.pi * jnp.arange(L, dtype=jnp.float32)[:, None] / L
    f = jnp.linspace(1e-4, HY_EMB_BANDS - 1, HY_EMB_BANDS, dtype=jnp.float32)[None]
    z = jnp.concatenate([t01, jnp.cos(f * w), -jnp.sin(f * w)], axis=-1)
    act = lambda a: jnp.sin(freq * a)
    hmid = act(z @ w1 + b1)
    hmid = act(hmid @ w2 + b2)
    hmid = act(hmid @ w3 + b3)
    h = (hmid @ w4).astype(jnp.float32).reshape(L, HY_ORDER, 2, HY_DIM)
    max_decay = math.log(HY_TARGET) / HY_FAST_DECAY
    min_decay = math.log(HY_TARGET) / HY_SLOW_DECAY
    deltas = jnp.abs(jnp.linspace(min_decay, max_decay, HY_DIM, dtype=jnp.float32))
    h = h * jnp.exp(-t01[:, :, None, None] * deltas)
    fwd = h[:, :, 0]
    bwd = h[:, :, 1]
    k = jnp.concatenate([fwd, jnp.zeros_like(fwd[:1]), bwd[:0:-1]], axis=0)
    k = k / (jnp.sum(jnp.abs(k), axis=0, keepdims=True) + EPS)
    return jnp.fft.rfft(k, axis=0)

def fftconv(u, kf, d):
    L = u.shape[1]
    uf = u.astype(jnp.float32)
    U = jnp.fft.rfft(uf, n=2 * L, axis=1)
    y = jnp.fft.irfft(U * kf[None], n=2 * L, axis=1)[:, :L]
    return y + uf * d.astype(jnp.float32)

def hyena(z_hy, conv_w, conv_b, kf, skip):
    zs = short_conv(z_hy, conv_w, conv_b)
    v, x1, x2 = jnp.split(zs, 3, axis=-1)
    y = x1.astype(jnp.float32) * fftconv(v, kf[:, 0], skip[0])
    y = x2.astype(jnp.float32) * fftconv(y, kf[:, 1], skip[1])
    return y.astype(z_hy.dtype)

def mix(h, p, rope, kv_ext):
    B, L, _ = h.shape
    z = h @ p["w_in"]
    q, k, v, z_hy, gates = jnp.split(
        z, [Q_DIM, Q_DIM + KV_DIM, Q_DIM + 2 * KV_DIM, Q_DIM + 2 * KV_DIM + HY_COLS], axis=-1)
    q = rmsnorm(q.reshape(B, L, N_HEADS, HEAD_DIM), p["q_norm_g"])
    k = rmsnorm(k.reshape(B, L, N_KV_HEADS, HEAD_DIM), p["k_norm_g"])
    v = v.reshape(B, L, N_KV_HEADS, HEAD_DIM)
    if rope is not None:
        q = apply_rope(q, rope[0], rope[1])
        k = apply_rope(k, rope[0], rope[1])
    k_self, v_self = k, v
    if kv_ext is not None:
        k = jnp.concatenate([k, kv_ext[0]], axis=1)
        v = jnp.concatenate([v, kv_ext[1]], axis=1)
    attn = gqa_blocks(q, k, v)
    kf = implicit_filters(L, p["hf_w1"], p["hf_b1"], p["hf_w2"], p["hf_b2"],
                          p["hf_w3"], p["hf_b3"], p["hf_w4"], p["hf_freq"])
    hy = hyena(z_hy, p["hy_conv_w"], p["hy_conv_b"], kf, p["hy_skip"])
    g_attn, g_hy = jnp.split(gates, 2, axis=-1)
    merged = (jax.nn.sigmoid(g_attn) * (attn @ p["w_attn_out"])
              + jax.nn.sigmoid(g_hy) * (hy @ p["w_hy_out"]))
    return merged @ p["w_out"], k_self, v_self

def context_kv(hc, p):
    B, L, _ = hc.shape
    z = hc @ p["w_in"][:, Q_DIM:Q_DIM + 2 * KV_DIM]
    k, v = jnp.split(z, 2, axis=-1)
    k = rmsnorm(k.reshape(B, L, N_KV_HEADS, HEAD_DIM), p["k_norm_g"])
    return k, v.reshape(B, L, N_KV_HEADS, HEAD_DIM)

def peer(h, wq, keys1, keys2, u_tab, v_tab):
    B, L, D = h.shape
    xt = h.reshape(B * L // PEER_CHUNK, PEER_CHUNK, D)
    half = PEER_DK // 2

    def chunk(xc):
        q = (xc @ wq).reshape(PEER_CHUNK, PEER_HEADS, 2, half)
        s1 = jnp.einsum('chd,hnd->chn', q[:, :, 0], keys1).astype(jnp.float32)
        s2 = jnp.einsum('chd,hnd->chn', q[:, :, 1], keys2).astype(jnp.float32)
        v1, i1 = lax.top_k(s1, PEER_TOPK)
        v2, i2 = lax.top_k(s2, PEER_TOPK)
        cand = (v1[..., :, None] + v2[..., None, :]).reshape(PEER_CHUNK, PEER_HEADS, PEER_TOPK * PEER_TOPK)
        cidx = (i1[..., :, None] * PEER_N_KEYS + i2[..., None, :]).reshape(PEER_CHUNK, PEER_HEADS, PEER_TOPK * PEER_TOPK)
        best, pos = lax.top_k(cand, PEER_TOPK)
        eidx = jnp.take_along_axis(cidx, pos, axis=-1)
        g = jax.nn.softmax(best, axis=-1)
        a = jnp.einsum('chkd,cd->chk', u_tab[eidx], xc)
        wgt = (jax.nn.gelu(a.astype(jnp.float32)) * g).astype(xc.dtype)
        return jnp.einsum('chk,chkd->cd', wgt, v_tab[eidx])

    return lax.map(chunk, xt).reshape(B, L, D)

def second_inputs(seed: int = 0) -> dict:
    key = jax.random.key(seed)
    ks = iter(jax.random.split(key, 40))

    def nrm(shape, scale):
        return jax.random.normal(next(ks), shape, jnp.float32) * scale

    L = DEPTH
    return {
        "x": nrm((BATCH, SEQ, D_MODEL), 1.0),
        "c": nrm((BATCH, D_MODEL), 1.0),
        "ctx": nrm((BATCH, CTX_LEN, D_MODEL), 1.0),
        "c_ctx": nrm((D_MODEL,), 1.0),
        "ada_w": nrm((L, D_MODEL, 6 * D_MODEL), D_MODEL ** -0.5),
        "ada_b": nrm((L, 6 * D_MODEL), 0.02),
        "norm_mix_g": 1.0 + nrm((L, D_MODEL), 0.02),
        "norm_ffn_g": 1.0 + nrm((L, D_MODEL), 0.02),
        "w_in": nrm((L, D_MODEL, IN_COLS), D_MODEL ** -0.5),
        "q_norm_g": 1.0 + nrm((L, HEAD_DIM), 0.02),
        "k_norm_g": 1.0 + nrm((L, HEAD_DIM), 0.02),
        "hy_conv_w": nrm((L, HY_SHORT, HY_COLS), HY_SHORT ** -0.5),
        "hy_conv_b": nrm((L, HY_COLS), 0.02),
        "hf_w1": nrm((L, HY_EMB_DIM, HY_FFN), HY_EMB_DIM ** -0.5),
        "hf_b1": nrm((L, HY_FFN), 0.02),
        "hf_w2": nrm((L, HY_FFN, HY_FFN), HY_FFN ** -0.5),
        "hf_b2": nrm((L, HY_FFN), 0.02),
        "hf_w3": nrm((L, HY_FFN, HY_FFN), HY_FFN ** -0.5),
        "hf_b3": nrm((L, HY_FFN), 0.02),
        "hf_w4": nrm((L, HY_FFN, HY_ORDER * 2 * HY_DIM), HY_FFN ** -0.5),
        "hf_freq": 1.0 + nrm((L, HY_FFN), 0.02),
        "hy_skip": nrm((L, HY_ORDER, HY_DIM), 0.5),
        "w_attn_out": nrm((L, Q_DIM, D_MODEL), Q_DIM ** -0.5),
        "w_hy_out": nrm((L, HY_DIM, D_MODEL), HY_DIM ** -0.5),
        "w_out": nrm((L, D_MODEL, D_MODEL), D_MODEL ** -0.5),
        "peer_wq": nrm((L, D_MODEL, PEER_HEADS * PEER_DK), D_MODEL ** -0.5),
        "peer_keys1": nrm((L, PEER_HEADS, PEER_N_KEYS, PEER_DK // 2), (PEER_DK // 2) ** -0.5),
        "peer_keys2": nrm((L, PEER_HEADS, PEER_N_KEYS, PEER_DK // 2), (PEER_DK // 2) ** -0.5),
        "peer_u": nrm((L, PEER_N_EXPERTS, D_MODEL), D_MODEL ** -0.5),
        "peer_v": nrm((L, PEER_N_EXPERTS, D_MODEL), PEER_HEADS ** -0.5),
        "final_norm_g": 1.0 + nrm((D_MODEL,), 0.02),
    }

def second_block(x, c, ctx, c_ctx, ada_w, ada_b, norm_mix_g, norm_ffn_g, w_in, q_norm_g, k_norm_g,
              hy_conv_w, hy_conv_b, hf_w1, hf_b1, hf_w2, hf_b2, hf_w3, hf_b3, hf_w4, hf_freq, hy_skip,
              w_attn_out, w_hy_out, w_out, peer_wq, peer_keys1, peer_keys2, peer_u, peer_v, final_norm_g):
    ROWS = x.shape[1] // GRID_W
    rope = axial_rope(ROWS)
    sc = jax.nn.silu(c)
    scc = jax.nn.silu(c_ctx)
    for i in range(DEPTH):
        p = dict(w_in=w_in[i], q_norm_g=q_norm_g[i], k_norm_g=k_norm_g[i],
                 hy_conv_w=hy_conv_w[i], hy_conv_b=hy_conv_b[i],
                 hf_w1=hf_w1[i], hf_b1=hf_b1[i], hf_w2=hf_w2[i], hf_b2=hf_b2[i],
                 hf_w3=hf_w3[i], hf_b3=hf_b3[i], hf_w4=hf_w4[i], hf_freq=hf_freq[i],
                 hy_skip=hy_skip[i], w_attn_out=w_attn_out[i], w_hy_out=w_hy_out[i], w_out=w_out[i])
        mod = (sc @ ada_w[i] + ada_b[i])[:, None, :]
        mod_c = scc @ ada_w[i] + ada_b[i]
        sh1, sc1, g1, sh2, sc2, g2 = jnp.split(mod, 6, axis=-1)
        csh1, csc1, cg1, csh2, csc2, cg2 = jnp.split(mod_c, 6, axis=-1)

        h = modulate(rmsnorm(x, norm_mix_g[i]), sh1, sc1)
        hc = modulate(rmsnorm(ctx, norm_mix_g[i]), csh1, csc1)
        if i < DEPTH - 1:
            out_c, kc, vc = mix(hc, p, None, None)
        else:
            kc, vc = context_kv(hc, p)
        out, _, _ = mix(h, p, rope, (kc, vc))
        x = x + g1 * out
        x = x + g2 * peer(modulate(rmsnorm(x, norm_ffn_g[i]), sh2, sc2),
                          peer_wq[i], peer_keys1[i], peer_keys2[i], peer_u[i], peer_v[i])
        if i < DEPTH - 1:
            ctx = ctx + cg1 * out_c
            ctx = ctx + cg2 * peer(modulate(rmsnorm(ctx, norm_ffn_g[i]), csh2, csc2),
                                   peer_wq[i], peer_keys1[i], peer_keys2[i], peer_u[i], peer_v[i])
    return rmsnorm(x, final_norm_g)


def setup_inputs(seed=0):
    out = dict(first_inputs(seed))
    for name, value in second_inputs(seed + 1).items():
        if name != "x":
            out[name + "_2"] = value
    return out


def reference(
    x, norm_mix_g, w_in, q_norm_g, k_norm_g, conv_w, w_sb_branch, w_conv_branch, w_out,
    norm_ffn_g, w_router_group, b_router_group, w_router_expert, b_router_expert, w_gate_e,
    w_up_e, w_down_e, c_2, ctx_2, c_ctx_2, ada_w_2, ada_b_2, norm_mix_g_2, norm_ffn_g_2, w_in_2,
    q_norm_g_2, k_norm_g_2, hy_conv_w_2, hy_conv_b_2, hf_w1_2, hf_b1_2, hf_w2_2, hf_b2_2,
    hf_w3_2, hf_b3_2, hf_w4_2, hf_freq_2, hy_skip_2, w_attn_out_2, w_hy_out_2, w_out_2,
    peer_wq_2, peer_keys1_2, peer_keys2_2, peer_u_2, peer_v_2, final_norm_g_2,
):
    x = first_block(
        x, norm_mix_g, w_in, q_norm_g, k_norm_g, conv_w, w_sb_branch, w_conv_branch, w_out,
        norm_ffn_g, w_router_group, b_router_group, w_router_expert, b_router_expert, w_gate_e,
        w_up_e, w_down_e,
    )
    return second_block(
        x, c_2, ctx_2, c_ctx_2, ada_w_2, ada_b_2, norm_mix_g_2, norm_ffn_g_2, w_in_2,
        q_norm_g_2, k_norm_g_2, hy_conv_w_2, hy_conv_b_2, hf_w1_2, hf_b1_2, hf_w2_2, hf_b2_2,
        hf_w3_2, hf_b3_2, hf_w4_2, hf_freq_2, hy_skip_2, w_attn_out_2, w_hy_out_2, w_out_2,
        peer_wq_2, peer_keys1_2, peer_keys2_2, peer_u_2, peer_v_2, final_norm_g_2,
    )


_drawn_inputs = setup_inputs


def setup_inputs(seed=0):
    import zlib

    import numpy as np

    out = dict(_drawn_inputs(seed))
    spreads = {}
    factors = {'k_norm_g': 3.023,
     'b_router_group': 3.774,
     'b_router_expert': 2.779,
     'ctx_2': 3.385,
     'ada_b_2': 2.683,
     'norm_mix_g_2': 6.455,
     'norm_ffn_g_2': 28.336,
     'q_norm_g_2': 36.821,
     'k_norm_g_2': 38.227,
     'hy_conv_b_2': 6.514,
     'hf_b1_2': 7.449,
     'hf_b2_2': 6.213,
     'hf_b3_2': 4.853,
     'hf_freq_2': 8.0,
     'final_norm_g_2': 7.887}
    for name, (base, spread) in spreads.items():
        noise = np.random.default_rng([zlib.crc32(name.encode()), seed]).standard_normal(out[name].shape)
        drawn = base * np.exp(spread * noise) if base else spread * noise
        out[name] = __import__('jax').numpy.asarray(drawn.astype(out[name].dtype))
    for name, factor in factors.items():
        out[name] = (out[name] * factor).astype(out[name].dtype)
    return out
```

```python
import math

import numpy as np

import concourse.bass as bass
from concourse import mybir

S = 512
D = 1024
EPS = 1e-6
BIG = 1.0e30

PCOLS = {}
_n = 0
for _name, _w in [("g1", 8), ("gf1", 8), ("qg1", 1), ("kg1", 1), ("cw", 12), ("rb", 36), ("ab", 48),
                  ("g2", 8), ("gf2", 8), ("gfin", 8), ("qg2", 1), ("kg2", 1), ("hcw", 36), ("hcb", 12),
                  ("hb1", 1), ("hb2", 1), ("hb3", 1), ("hfr", 1), ("cc", 16)]:
    PCOLS[_name] = (_n, _n + _w)
    _n += _w
PTOTAL = _n
CNAMES = ["ident", "ones", "blk", "linc", "smask", "nmask", "iota", "rot"]


class Engine:

    def __init__(self, sem):
        self.sem, self.n, self.items, self.seen = sem, 0, [], {}

    def wait(self, *toks):
        for t in toks:
            if t is None:
                continue
            if isinstance(t, list):
                self.wait(*t)
                continue
            sem, val = t
            if self.seen.get(id(sem), 0) < val:
                self.seen[id(sem)] = val
                self.items.append((None, sem, val))

    def do(self, fn, *after, sig=True):
        self.wait(*after)
        if not sig:
            self.items.append((fn, None, 0))
            return None
        self.n += 1
        self.items.append((fn, self.sem, 1))
        return (self.sem, self.n)

    def last(self):
        return (self.sem, self.n) if self.n else None

    def run(self, eng):
        for fn, sem, val in self.items:
            if fn is None:
                eng.wait_ge(sem, val)
            else:
                ins = fn()
                if sem is not None:
                    ins.then_inc(sem, val)


class Counter:
    def __init__(self, sem):
        self.sem, self.n = sem, 0


class Place:

    def __init__(self, ap, sem=None):
        self.ap, self.free, self.counter = ap, [], Counter(sem)


class Pool:
    def __init__(self, places):
        self.q = list(places)

    def get(self):
        return self.q.pop(0)

    def put(self, place, *toks):
        place.free = list(toks)
        self.q.append(place)


def program(nc, A, out):
    f32 = mybir.dt.float32
    u32 = mybir.dt.uint32
    ALU = mybir.AluOpType
    ACT = mybir.ActivationFunctionType
    AX = mybir.AxisListType
    from contextlib import ExitStack
    ctx = ExitStack()
    with ctx:
        def sb(name, cols, dt=f32):
            return ctx.enter_context(nc.sbuf_tensor(name, [128, cols], dt))

        def sem(name):
            return ctx.enter_context(nc.semaphore(name))

        def dsem(name):
            return Counter(sem(name))

        v, a, t = nc.vector, nc.scalar, nc.tensor
        PE, DVE, SC, GP, SP = (Engine(sem(n)) for n in ("s_pe", "s_dve", "s_act", "s_pool", "s_sp"))

        def dma(queue, eng, counter, dst, src, *after):
            counter.n += 16
            sem_ = counter.sem
            queue.wait(*after)
            queue.items.append((lambda: eng.dma_start(dst, src), sem_, 16))
            return (sem_, counter.n)

        X = sb("X", 8 * S)[:, :].rearrange("p (k n) -> p k n", k=8)
        H = sb("H", 8 * S)[:, :].rearrange("p (k n) -> p k n", k=8)
        NSLOT = 4
        slots = Pool([Place(sb(f"W{i}", 4096)[:, :], sem(f"s_w{i}")) for i in range(NSLOT)])
        NA = 46
        arena = sb("arena", NA * S)
        TMP = sb("tmp", 5 * S)
        CST = sb("cst", len(CNAMES) * 128)
        PAR = sb("par", PTOTAL)
        banks = Pool([Place(ctx.enter_context(nc.psum_tensor(f"P{i}", [128, 512], f32))[:, :]) for i in range(8)])
        Wd = nc.dram_tensor("w_scratch", [8, 128, 128 * 64], f32).ap()

        def reg(at, n):
            assert at + n <= NA
            return arena[:, at * S:(at + n) * S]

        def tiles(at, n):
            return reg(at, n).rearrange("p (k n) -> p k n", k=n)

        def cst(name):
            i = CNAMES.index(name)
            return CST[:, i * 128:(i + 1) * 128]

        def par(name, i=None):
            lo, hi = PCOLS[name]
            return PAR[:, lo:hi] if i is None else PAR[:, lo + i:lo + i + 1]

        ident, ones, blk = cst("ident"), cst("ones"), cst("blk")
        tmp = [TMP[:, i * S:(i + 1) * S] for i in range(5)]

        def tt(out_, in0, in1, op, *after):
            return DVE.do(lambda: v.tensor_tensor(out=out_, in0=in0, in1=in1, op=op), *after)

        def ts(out_, in0, s1, s2, op0, op1, *after):
            if op1 is None:
                return DVE.do(lambda: v.tensor_scalar(out=out_, in0=in0, scalar1=s1, scalar2=None, op0=op0), *after)
            return DVE.do(lambda: v.tensor_scalar(out=out_, in0=in0, scalar1=s1, scalar2=s2, op0=op0, op1=op1), *after)

        def stt(out_, in0, s, in1, op0, op1, *after):
            return DVE.do(lambda: v.scalar_tensor_tensor(out=out_, in0=in0, scalar=s, in1=in1, op0=op0, op1=op1), *after)

        def vcopy(out_, in_, *after):
            return DVE.do(lambda: v.tensor_copy(out_, in_), *after)

        def act(out_, in_, fn, *after, bias=None, scale=None, acc=None):
            kw = {}
            if bias is not None:
                kw["bias"] = bias
            if scale is not None:
                kw["scale"] = scale
            if acc is not None:
                kw["accum_out"] = acc
            return SC.do(lambda: a.activation(out_, in_, fn, **kw), *after)

        def mms(out_, pairs, *after, start=True, stop=True):
            PE.wait(*after)
            n = len(pairs)
            tok = None
            for i, (l, r) in enumerate(pairs):
                st, sp = start and i == 0, stop and i == n - 1
                tok = PE.do(lambda l=l, r=r, st=st, sp=sp: t.matmul(out_, l, r, start=st, stop=sp), sig=i == n - 1)
            return tok

        def transpose(out_, in_, *after, sig=True):
            return PE.do(lambda: t.transpose(out_, in_, ident), *after, sig=sig)

        MUL, ADD, SUB = ALU.mult, ALU.add, ALU.subtract

        def load(pieces, *after):
            s = slots.get()
            tok = None
            for lo, hi, view, src in pieces:
                dst = s.ap[:, lo:hi]
                if view:
                    dst = view(dst)
                tok = dma(SP, nc.sync, s.counter, dst, src, s.free, *after)
            s.ready = tok
            return s

        k8 = lambda ap: ap.rearrange("p (k n) -> p k n", k=8)
        k4 = lambda ap: ap.rearrange("p (k n) -> p k n", k=4)
        k2 = lambda ap: ap.rearrange("p (k n) -> p k n", k=2)

        def load_cols(w, lo, hi):
            n = hi - lo
            return load([(0, 8 * n, k8, w[:, lo:hi].rearrange("(k p) n -> p k n", p=128))])

        def load_half(w):
            return load([(0, 4096, k4, w.rearrange("(k p) n -> p k n", p=128))])

        d_x, d_c, d_p, d_o = dsem("d_x"), dsem("d_c"), dsem("d_p"), dsem("d_o")
        t_c = dma(SC, nc.scalar, d_c, CST[:, :], A["consts"])
        t_p = dma(SC, nc.scalar, d_p, PAR[:, :], A["params"])
        t_x = dma(SP, nc.sync, d_x, X, A["x"].rearrange("(k p) n -> p k n", p=128))
        for e in (PE, DVE, SC, GP):
            e.wait(t_c, t_p)

        last_r = [None]

        def factor(srcs, lhs, inv, n, *after):
            b = banks.get()
            PE.wait(b.free)
            sq_free = factor_sq
            tok = None
            for i, s in enumerate(srcs):
                j = i % 2
                q = tmp[j][:, 0:n]
                tk = act(q, s, ACT.Square, sq_free[j], *after)
                tok = PE.do(lambda q=q, i=i: t.matmul(b.ap[:, 0:n], lhs, q, start=i == 0, stop=i == len(srcs) - 1), tk)
                sq_free[j] = tok
            m, r, w = tmp[2][:, 0:n], tmp[3][:, 0:n], tmp[4][:, 0:n]
            t1 = ts(m, b.ap[:, 0:n], inv, EPS, MUL, ADD, tok, last_r[0])
            banks.put(b, t1)
            t2 = act(r, m, ACT.Sqrt, t1)
            t3 = DVE.do(lambda: v.reciprocal(w, r), t2)
            t4 = tt(r, w, w, MUL, t3)
            t5 = tt(r, r, m, MUL, t4)
            t6 = ts(r, r, -0.5, 1.5, MUL, ADD, t5)
            t7 = tt(r, r, w, MUL, t6)
            return r, t7

        factor_sq = [None, None]

        def norm(src, gain, *after):
            r, tr = factor([src[:, k, :] for k in range(8)], ones, 1.0 / D, S, *after)
            toks = []
            for k in range(8):
                toks.append(stt(H[:, k, :], src[:, k, :], gain(k), r, MUL, MUL, tr))
            last_r[0] = toks[-1]
            return toks[-1]

        def proj(slot, c, h_tok, width=512):
            b = banks.get()
            w = slot.ap[:, 0:8 * width].rearrange("p (k n) -> p k n", k=8)
            tok = mms(b.ap, [(w[:, k, c * 128:(c + 1) * 128], H[:, k, :]) for k in range(8)], b.free, slot.ready, h_tok)
            return b, tok

        def drain(gen):
            for _ in gen:
                pass

        def mix(*gens):
            gens = list(gens)
            while gens:
                for g in list(gens):
                    try:
                        next(g)
                    except StopIteration:
                        gens.remove(g)

        t_h = norm(X, lambda k: par("g1", k), t_x)
        Q, K, V, AT = tiles(0, 4), tiles(4, 4), tiles(8, 4), tiles(12, 4)
        CB, CC, CU = tiles(16, 4), tiles(20, 4), tiles(24, 4)
        GA, GB = tiles(28, 8), tiles(36, 8)
        w_in = A["w_in"]

        def head_norm(dst, b, tok, gain):
            t0 = act(dst, b.ap, ACT.Copy, tok)
            r, tr = factor([dst], blk, 1.0 / 64, S, t0)
            banks.put(b, t0)
            t1 = stt(dst, dst, gain, r, MUL, MUL, tr)
            last_r[0] = t1
            return t1

        t_q, t_k, t_v = [None] * 4, [None] * 4, [None] * 4

        def project_qkv():
            for which, dst, gain, toks in ((0, Q, "qg1", t_q), (1, K, "kg1", t_k)):
                s = load_cols(w_in, which * 512, which * 512 + 512)
                held = []
                for c in range(4):
                    held.append(proj(s, c, t_h))
                slots.put(s, held[-1][1])
                for c in range(4):
                    toks[c] = head_norm(dst[:, c, :], *held[c], par(gain, 0))
            s = load_cols(w_in, 1024, 1536)
            w = k8(s.ap)
            for c in range(4):
                b = banks.get()
                tok = mms(b.ap, [(H[:, k, c * 128:(c + 1) * 128], w[:, k, :]) for k in range(8)], b.free, s.ready, t_h)
                t_v[c] = act(V[:, c, :], b.ap, ACT.Copy, tok)
                banks.put(b, t_v[c])
            slots.put(s, tok)

        project_qkv()

        OFF = [0, 512, 896, 1152]
        ZB = [reg(36, 10)[:, 0:1280], reg(36, 10)[:, 1280:2560]]
        EB = [reg(36, 10)[:, 2560:3840], reg(36, 10)[:, 3840:5120]]
        pv_tok = [None] * 8
        t_at = [None] * 8
        in_free = [None] * 8

        def attention():
            for h in range(8):
                j, po = h // 2, 64 * (h % 2)
                Z, E = ZB[h % 2], EB[h % 2]
                tz = None
                for i in range(4):
                    n = 512 - 128 * i
                    b = banks.get()
                    tok = mms(b.ap[:, 0:n], [(K[po:po + 64, j, i * 128:(i + 1) * 128], Q[po:po + 64, j, i * 128:512])],
                              b.free, t_q[j], t_k[j])
                    tz = act(Z[:, OFF[i]:OFF[i] + n], b.ap[:, 0:n], ACT.Copy, tok, pv_tok[h - 2] if h >= 2 else None, scale=0.125)
                    banks.put(b, tz)
                t1 = act(E, Z, ACT.Abs, tz, in_free[h - 2] if h >= 2 else None)
                t2 = act(E, E, ACT.Exp, t1, scale=-1.0)
                t3 = act(E, E, ACT.Ln, t2, bias=1.0)
                t4 = stt(E, Z, 0.0, E, ALU.max, ADD, t3)
                for i in range(4):
                    d = E[:, OFF[i]:OFF[i] + 128]
                    t5 = tt(d, d, cst("smask"), MUL, t4)
                yield
                te = None
                for i in range(4):
                    n = 512 - 128 * i
                    b = banks.get()
                    PE.wait(b.free, t5)
                    for jj in range(i, 4):
                        l = cst("linc") if jj == i else ones
                        o = (jj - i) * 128
                        tok = PE.do(lambda b=b, l=l, o=o, jj=jj, i=i, n=n, E=E: t.matmul(
                            b.ap[:, o:n], l, E[:, OFF[jj]:OFF[jj] + 512 - 128 * jj], start=jj == i, stop=jj == 3),
                            sig=jj == 3)
                    z = Z[:, OFF[i]:OFF[i] + n]
                    t6 = tt(z, z, b.ap[:, 0:n], SUB, tok, tz)
                    banks.put(b, t6)
                    t7 = tt(z[:, 0:128], z[:, 0:128], cst("nmask"), ADD, t6)
                in_free[h] = tok
                te = act(Z, Z, ACT.Exp, t7)
                yield
                b = banks.get()
                PE.wait(b.free, te, t_v)
                for i in range(4):
                    tok = PE.do(lambda i=i, b=b, Z=Z, h=h, po=po: t.matmul(
                        b.ap[po:po + 64, 128 * i:512], V[:, i, h * 64:(h + 1) * 64],
                        Z[:, OFF[i]:OFF[i] + 512 - 128 * i], start=i == 0, stop=i == 3), sig=i == 3)
                pv_tok[h] = tok
                t_at[h] = act(AT[po:po + 64, j, :], b.ap[po:po + 64, :], ACT.Copy, tok)
                banks.put(b, t_at[h])
                yield

        t_cv = [None] * 4
        t_ga = [None] * 8

        def conv_gates():
            t_cb, t_cc = [None] * 4, [None] * 4
            for dst, lo, toks in ((CB, 1536, t_cb), (CC, 2048, t_cc)):
                s = load_cols(w_in, lo, lo + 512)
                for c in range(4):
                    b, tok = proj(s, c, t_h)
                    toks[c] = act(dst[:, c, :], b.ap, ACT.Copy, tok)
                    banks.put(b, toks[c])
                    yield
                slots.put(s, tok)
            s = load_cols(w_in, 2560, 3072)
            for c in range(4):
                b, tok = proj(s, c, t_h)
                cu, y = CC[:, c, :], CU[:, c, :]
                cw = lambda j, c=c: par("cw", j * 4 + c)
                t1 = tt(cu, cu, b.ap, MUL, tok, t_cc[c])
                banks.put(b, t1)
                t2 = ts(y, cu, cw(2), None, MUL, None, t1)
                t3 = stt(y[:, 1:S], cu[:, 0:S - 1], cw(1), y[:, 1:S], MUL, ADD, t2)
                t4 = stt(y[:, 2:S], cu[:, 0:S - 2], cw(0), y[:, 2:S], MUL, ADD, t3)
                t_cv[c] = tt(y, y, CB[:, c, :], MUL, t4, t_cb[c])
                yield
            slots.put(s, tok)
            for half in range(2):
                s = load_cols(w_in, 3072 + half * 512, 3584 + half * 512)
                for c in range(4):
                    b, tok = proj(s, c, t_h)
                    i = half * 4 + c
                    t_ga[i] = act(GA[:, i, :], b.ap, ACT.Sigmoid, tok)
                    banks.put(b, t_ga[i])
                    yield
                slots.put(s, tok)

        mix(attention(), conv_gates())

        t_gb = [None] * 8

        def gates(dst, w, lo, toks, *after):
            for half in range(2):
                s = load_cols(w, lo + half * 512, lo + half * 512 + 512)
                for c in range(4):
                    b, tok = proj(s, c, t_h)
                    i = half * 4 + c
                    toks[i] = act(dst[:, i, :], b.ap, ACT.Sigmoid, tok, *after)
                    banks.put(b, toks[i])
                    yield
                slots.put(s, tok)

        drain(gates(GB, w_in, 4096, t_gb, pv_tok[6], pv_tok[7], in_free[6], in_free[7]))

        def merge(wa, wb, ATT, CONV, t_att, t_conv, t_g1, t_g2, ga, gb):
            toks = []
            for w, src, ready, g, tg in ((wa, ATT, t_att, ga, t_g1), (wb, CONV, t_conv, gb, t_g2)):
                s = load_half(w)
                wv = k4(s.ap)
                for c in range(8):
                    b = banks.get()
                    tok = mms(b.ap, [(wv[:, k, c * 128:(c + 1) * 128], src[:, k, :]) for k in range(4)], b.free, s.ready, ready)
                    t1 = tt(g[:, c, :], g[:, c, :], b.ap, MUL, tok, tg[c])
                    banks.put(b, t1)
                    if g is gb:
                        toks.append(tt(ga[:, c, :], ga[:, c, :], g[:, c, :], ADD, t1))
                slots.put(s, tok)
            return toks

        t_m = merge(A["w_sb"], A["w_conv"], AT, CU, t_at, t_cv, t_ga, t_gb, GA, GB)

        def out_proj(w, M, t_m, add):
            for half in range(2):
                s = load_cols(w, half * 512, half * 512 + 512)
                wv = k8(s.ap)
                for c in range(4):
                    b = banks.get()
                    tok = mms(b.ap, [(wv[:, k, c * 128:(c + 1) * 128], M[:, k, :]) for k in range(8)], b.free, s.ready, t_m)
                    t1 = add(half * 4 + c, b, tok)
                    banks.put(b, t1)
                slots.put(s, tok)
            return t1

        t_x = out_proj(A["w_out"], GA, t_m, lambda c, b, tok: tt(X[:, c, :], X[:, c, :], b.ap, ADD, tok))

        t_h = norm(X, lambda k: par("gf1", k), t_x)
        base = [0]
        scr = reg(0, 8)

        def small(n):
            base[0] += n
            return scr[:, base[0] - n:base[0]]

        WR = small(8 * 36).rearrange("p (k n) -> p k n", k=8)
        d_r = dsem("d_r")
        t_r = dma(SC, nc.scalar, d_r, WR, A["w_router"].rearrange("(k p) n -> p k n", p=128), t_x)
        COMB = small(4 * 32).rearrange("p (k n) -> p k n", k=4)
        CT = reg(8, 1)
        t_ct = None
        b = banks.get()
        for q in range(4):
            tok = mms(b.ap[:, q * 36:(q + 1) * 36], [(H[:, k, q * 128:(q + 1) * 128], WR[:, k, :]) for k in range(8)],
                      b.free, t_r, t_h)
        LG = small(4 * 36).rearrange("p (k n) -> p k n", k=4)
        rb = par("rb").unsqueeze(1).broadcast_to([128, 4, 36])
        t_lg = tt(LG, b.ap[:, 0:144].rearrange("p (k n) -> p k n", k=4), rb, ADD, tok)
        banks.put(b, t_lg)
        L8 = small(32).rearrange("p (k n) -> p k n", k=4)
        t1 = DVE.do(lambda: v.memset(L8, -BIG), t_lg)
        t_l8 = vcopy(L8[:, :, 0:4], LG[:, :, 0:4], t1)
        M8, E8, V8, WI, NM, SM, EX, ND, W0, W1, OG, I8f, J8f = (
            small(32).rearrange("p (k n) -> p k n", k=4) for _ in range(13))
        UI = small(32).bitcast(u32).rearrange("p (k n) -> p k n", k=4)
        UJ = small(32).bitcast(u32).rearrange("p (k n) -> p k n", k=4)
        iota = cst("iota")
        R4 = range(4)

        def each(f, *after):
            return [f(q) for q in R4]

        ta = [DVE.do(lambda q=q: v.max(M8[:, q, :], L8[:, q, :]), t_l8) for q in R4]
        tb = [DVE.do(lambda q=q: v.max_index(UI[:, q, :], M8[:, q, :], L8[:, q, :]), ta[q]) for q in R4]
        tc = vcopy(I8f, UI, tb)
        td = ts(NM, M8, -1.0, None, MUL, None, ta)
        tex = [act(EX[:, q, 0:4], L8[:, q, 0:4], ACT.Exp, td, bias=NM[:, q, 0:1], acc=SM[:, q, 0:1]) for q in R4]
        tgw = DVE.do(lambda: v.reciprocal(SM[:, :, 1:2], SM[:, :, 0:1]), tex)
        tog = [ts(OG[:, q, 0:4], iota[:, 0:4], I8f[:, q, 0:1], None, ALU.is_equal, None, tc) for q in R4]
        te = [ts(E8[:, q, :], LG[:, q, 4:12], OG[:, q, 0:1], None, MUL, None, tog) for q in R4]
        for g in range(1, 4):
            te = [stt(E8[:, q, :], LG[:, q, 4 + 8 * g:12 + 8 * g], OG[:, q, g:g + 1], E8[:, q, :], MUL, ADD, te[q]) for q in R4]
        ta = [DVE.do(lambda q=q: v.max(V8[:, q, :], E8[:, q, :]), te[q]) for q in R4]
        tb = [DVE.do(lambda q=q: v.max_index(UJ[:, q, :], V8[:, q, :], E8[:, q, :]), ta[q]) for q in R4]
        tc = vcopy(J8f, UJ, tb)
        td = tt(ND[:, :, 0:1], V8[:, :, 1:2], V8[:, :, 0:1], SUB, ta)
        te = act(ND[:, :, 1:2], ND[:, :, 0:1], ACT.Exp, td)
        tf = ts(ND[:, :, 2:3], ND[:, :, 1:2], 1.0, None, ADD, None, te)
        tg = DVE.do(lambda: v.reciprocal(ND[:, :, 3:4], ND[:, :, 2:3]), tf)
        th = tt(ND[:, :, 4:5], ND[:, :, 3:4], ND[:, :, 1:2], MUL, tg)
        tw0 = [ts(W0[:, q, :], iota[:, 0:8], J8f[:, q, 0:1], ND[:, q, 3:4], ALU.is_equal, MUL, tc, tg) for q in R4]
        tw1 = [ts(W1[:, q, :], iota[:, 0:8], J8f[:, q, 1:2], ND[:, q, 4:5], ALU.is_equal, MUL, th) for q in R4]
        ti = tt(WI, W0, W1, ADD, tw0, tw1)
        ti = [ts(WI[:, q, :], WI[:, q, :], SM[:, q, 1:2], None, MUL, None, ti, tgw) for q in R4]
        tcb = []
        for q in R4:
            for g in range(4):
                tcb.append(ts(COMB[:, q, 8 * g:8 * g + 8], WI[:, q, :], OG[:, q, g:g + 1], None, MUL, None, ti))
        b = banks.get()
        PE.wait(b.free)
        for q in R4:
            tok = transpose(b.ap[0:32, q * 128:(q + 1) * 128], COMB[:, q, :], tcb)
        t_ct = act(CT[0:32, :], b.ap[0:32, :], ACT.Copy, tok)
        banks.put(b, t_ct)

        AC = [tiles(10, 4), tiles(14, 4)]
        SG = [reg(18, 1), reg(19, 1)]
        SU = [reg(20, 1), reg(21, 1)]
        ac_free = [None, None]

        def moe_up(pr):
            toks = []
            for e in (2 * pr, 2 * pr + 1):
                s = load([(0, 2048, k8, A["w_gate"][e].rearrange("(k p) n -> p k n", p=128)),
                          (2048, 4096, k8, A["w_up"][e].rearrange("(k p) n -> p k n", p=128))])
                wg, wu = k8(s.ap[:, 0:2048]), k8(s.ap[:, 2048:4096])
                held = []
                for w in (wg, wu):
                    for f in range(2):
                        b = banks.get()
                        tok = mms(b.ap, [(w[:, k, f * 128:(f + 1) * 128], H[:, k, :]) for k in range(8)], b.free, s.ready, t_h)
                        held.append((b, tok))
                slots.put(s, tok)
                bw = banks.get()
                tw = mms(bw.ap, [(ident[0:32, e:e + 1].to_broadcast([32, 128]), CT[0:32, :])], bw.free, t_ct)
                for f in range(2):
                    dst = AC[pr % 2][:, (e % 2) * 2 + f, :]
                    (bg, tg_), (bu, tu_) = held[f], held[2 + f]
                    t1 = act(SG[f], bg.ap, ACT.Silu, tg_, sg_free[f])
                    banks.put(bg, t1)
                    t2 = tt(SU[f], SG[f], bu.ap, MUL, t1, tu_)
                    sg_free[f] = t2
                    banks.put(bu, t2)
                    t3 = tt(dst, SU[f], bw.ap, MUL, t2, tw, ac_free[pr % 2])
                    toks.append(t3)
                banks.put(bw, t3)
            return toks

        sg_free = [None, None]

        def moe_down(pr, ready):
            s = load([(0, 4096, lambda ap: ap.rearrange("p (e k n) -> p (e k) n", e=2, k=2),
                       A["w_down"][2 * pr:2 * pr + 2].rearrange("e (k p) n -> p (e k) n", p=128))])
            w = k4(s.ap)
            for c in range(8):
                b = banks.get()
                tok = mms(b.ap, [(w[:, k, c * 128:(c + 1) * 128], AC[pr % 2][:, k, :]) for k in range(4)], b.free, s.ready, ready)
                t1 = tt(X[:, c, :], X[:, c, :], b.ap, ADD, tok)
                banks.put(b, t1)
            ac_free[pr % 2] = tok
            slots.put(s, tok)
            return t1

        ready = moe_up(0)
        for pr in range(16):
            nxt = moe_up(pr + 1) if pr < 15 else None
            t_x = moe_down(pr, ready)
            ready = nxt

        MOD = reg(0, 1)[:, 0:96].rearrange("p (k n) -> p k n", n=2)
        SCC = reg(0, 1)[:, 96:112].rearrange("p (k n) -> p k n", n=2)
        G2 = reg(0, 1)[:, 112:128]
        GF2 = reg(0, 1)[:, 128:136]
        t_sc = act(SCC, par("cc").rearrange("p (k n) -> p k n", n=2), ACT.Silu, t_ct)
        b = banks.get()
        PE.wait(b.free, t_sc)
        for i in range(12):
            s = load_cols(A["ada_w"], i * 512, i * 512 + 512)
            w = k8(s.ap)
            for c in range(4):
                j = i * 4 + c
                tok = mms(b.ap[:, 2 * j:2 * j + 2], [(w[:, k, c * 128:(c + 1) * 128], SCC[:, k, :]) for k in range(8)], s.ready)
            slots.put(s, tok)
        t_mod = tt(MOD, b.ap[:, 0:96].rearrange("p (k n) -> p k n", n=2), par("ab").unsqueeze(2).broadcast_to([128, 48, 2]),
                   ADD, tok, t_ct)
        banks.put(b, t_mod)
        for w in range(2):
            t_g2 = stt(G2[:, 8 * w:8 * w + 8], MOD[:, 8:16, w], 1.0, par("g2"), ADD, MUL, t_mod)
        t_g2 = stt(GF2, MOD[:, 32:40, 0], 1.0, par("gf2"), ADD, MUL, t_mod, t_g2)

        def modulated(src, dst, n, gain, shift, *after):
            r, tr = factor([src[:, k, :] for k in range(8)], ones, 1.0 / D, n, *after)
            for k in range(8):
                t1 = stt(dst[:, k, :], src[:, k, :], gain(k), r, MUL, MUL, tr)
                t2 = ts(dst[:, k, :], dst[:, k, :], shift(k), None, ADD, None, t1)
            last_r[0] = t1
            return t2

        t_h = modulated(X, H, S, lambda k: G2[:, k:k + 1], lambda k: MOD[:, k, 0:1], t_x, t_g2)
        CX = reg(1, 4).rearrange("p (k n) -> p k n", k=8)
        HC = reg(5, 4).rearrange("p (k n) -> p k n", k=8)
        d_cx = dsem("d_cx")
        t_cx = dma(SC, nc.scalar, d_cx, CX, A["ctx"].rearrange("(k p) n -> p k n", p=128), t_x, t_ct)
        t_hc = modulated(CX, HC, 256, lambda k: G2[:, 8 + k:9 + k], lambda k: MOD[:, k, 1:2], t_cx, t_g2)

        w2 = A["w_in_2"]
        KK = reg(9, 2)[:, 0:768]
        VV = reg(11, 2)[:, 0:768].rearrange("p (k n) -> p k n", n=128)
        QQ = tiles(13, 4)
        COS, SIN = reg(17, 1), reg(18, 1)
        d_cs = dsem("d_cs")
        dma(SC, nc.scalar, d_cs, COS, A["rope"][0], t_x)
        t_cs = dma(SC, nc.scalar, d_cs, SIN, A["rope"][1], t_x)
        s = load_cols(w2, 4096, 4352)
        w = s.ap[:, 0:2048].rearrange("p (k n) -> p k n", k=8)

        def head_norm2(dst, b, tok, n, gain, rope):
            t0 = act(dst, b.ap[:, 0:n], ACT.Copy, tok)
            banks.put(b, t0)
            r, tr = factor([dst], blk, 1.0 / 64, n, t0)
            t1 = stt(dst, dst, gain, r, MUL, MUL, tr)
            last_r[0] = t1
            if rope:
                br = banks.get()
                tok = mms(br.ap, [(cst("rot"), dst)], br.free, t1)
                rt = tmp[0]
                t2 = tt(rt, br.ap, SIN, MUL, tok, t_cs, factor_sq[0])
                banks.put(br, t2)
                t3 = tt(dst, dst, COS, MUL, t2)
                t1 = tt(dst, dst, rt, ADD, t3)
                factor_sq[0] = t1
            return t1

        b = banks.get()
        tok = mms(b.ap, [(w[:, k, 0:128], H[:, k, :]) for k in range(8)], b.free, s.ready, t_h)
        t_k1 = head_norm2(KK[:, 0:512], b, tok, 512, par("kg2", 0), True)
        b = banks.get()
        tok = mms(b.ap[:, 0:256], [(w[:, k, 0:128], HC[:, k, :]) for k in range(8)], b.free, t_hc)
        t_k2 = head_norm2(KK[:, 512:768], b, tok, 256, par("kg2", 0), False)
        t_kk = [t_k1, t_k2]
        b = banks.get()
        b2 = banks.get()
        PE.wait(b.free, b2.free)
        for c in range(4):
            tok = mms(b.ap[:, c * 128:(c + 1) * 128], [(H[:, k, c * 128:(c + 1) * 128], w[:, k, 128:256]) for k in range(8)])
        for c in range(2):
            tok = mms(b2.ap[:, c * 128:(c + 1) * 128], [(HC[:, k, c * 128:(c + 1) * 128], w[:, k, 128:256]) for k in range(8)])
        slots.put(s, tok)
        t1 = act(VV[:, 0:4, :], b.ap.rearrange("p (k n) -> p k n", n=128), ACT.Copy, tok)
        t_vv = act(VV[:, 4:6, :], b2.ap[:, 0:256].rearrange("p (k n) -> p k n", n=128), ACT.Copy, tok)
        banks.put(b, t1)
        banks.put(b2, t_vv)
        t_qq = [None] * 4
        s = load_cols(w2, 1536, 2048)
        held = [proj(s, c, t_h) for c in range(4)]
        slots.put(s, held[-1][1])
        for c in range(4):
            t_qq[c] = head_norm2(QQ[:, c, :], *held[c], 512, par("qg2", 0), True)

        A2 = tiles(1, 4)
        PR = [reg(5, 2)[:, 0:768], reg(7, 2)[:, 0:768]]
        PT = reg(19, 6).rearrange("p (k n) -> p k n", k=6)
        STT = reg(25, 1)
        t_a2 = [None] * 8

        def attention2():
            pt_free = None
            pr_free = [None, None]
            it = 0
            for j in range(4):
                for g in range(2):
                    po = 64 * g
                    h = j * 2 + g
                    ready = []
                    for q in range(4):
                        c = (it % 2) * 8
                        st = lambda i, c=c: STT[:, c + i:c + i + 1]
                        Pb = PR[it % 2]
                        lq = QQ[po:po + 64, j, q * 128:(q + 1) * 128]
                        ba, bb = banks.get(), banks.get()
                        PE.wait(ba.free, bb.free)
                        t0 = mms(ba.ap, [(lq, KK[po:po + 64, 0:512])], t_qq[j], t_kk)
                        t1 = mms(bb.ap[:, 0:256], [(lq, KK[po:po + 64, 512:768])])
                        m0 = DVE.do(lambda st=st, ba=ba: v.tensor_reduce(out=st(0), in_=ba.ap, axis=AX.X, op=ALU.max), t0, pr_free[it % 2])
                        m1 = DVE.do(lambda st=st, bb=bb: v.tensor_reduce(out=st(1), in_=bb.ap[:, 0:256], axis=AX.X, op=ALU.max), t1)
                        m2 = tt(st(2), st(0), st(1), ALU.max, m0, m1)
                        m3 = ts(st(3), st(2), -0.125, None, MUL, None, m2)
                        e0 = act(Pb[:, 0:512], ba.ap, ACT.Exp, m3, pr_free[it % 2], t_hc, bias=st(3), scale=0.125, acc=st(4))
                        e1 = act(Pb[:, 512:768], bb.ap[:, 0:256], ACT.Exp, m3, bias=st(3), scale=0.125, acc=st(5))
                        banks.put(ba, e0)
                        banks.put(bb, e1)
                        m4 = tt(st(6), st(4), st(5), ADD, e0, e1)
                        m5 = DVE.do(lambda st=st: v.reciprocal(st(7), st(6)), m4)
                        m6 = ts(Pb, Pb, st(7), None, MUL, None, m5)
                        yield
                        ba, bb = banks.get(), banks.get()
                        PE.wait(ba.free, bb.free, m6)
                        for i in range(6):
                            o = (ba, bb)[i // 4].ap[:, (i % 4) * 128:(i % 4) * 128 + 128]
                            tok = transpose(o, Pb[:, i * 128:(i + 1) * 128], sig=i == 5)
                        pr_free[it % 2] = tok
                        r0 = act(PT[:, 0:4, q * 128:(q + 1) * 128], ba.ap.rearrange("p (k n) -> p k n", k=4), ACT.Copy, tok, pt_free)
                        r1 = vcopy(PT[:, 4:6, q * 128:(q + 1) * 128], bb.ap[:, 0:256].rearrange("p (k n) -> p k n", k=2), tok, pt_free)
                        banks.put(ba, r0)
                        banks.put(bb, r1)
                        ready += [r0, r1]
                        it += 1
                        yield
                    b = banks.get()
                    pt_free = mms(b.ap[po:po + 64, :], [(VV[:, i, po:po + 64], PT[:, i, :]) for i in range(6)], b.free, ready, t_vv)
                    t_a2[h] = act(A2[po:po + 64, j, :], b.ap[po:po + 64, :], ACT.Copy, pt_free, t_hc)
                    banks.put(b, t_a2[h])

        KF = tiles(26, 18)
        SB_, DB_ = tiles(10, 4), tiles(14, 4)
        DEC = None

        drain(attention2())
        PE_att = t_a2
        HM = reg(5, 1)
        FW = reg(19, 7)
        ZF, FW1, FW2, FW3, FW4, SKB = FW[:, 0:512], FW[:, 512:576], FW[:, 576:640], FW[:, 640:704], FW[:, 768:2816], FW[:, 2816 - 256:3584]
        SKB = reg(8, 2)
        d_f = dsem("d_f")
        dma(SP, nc.sync, d_f, ZF[0:33, :], A["zf"], t_a2, pt_last := PE.last())
        dma(SP, nc.sync, d_f, FW1[0:33, :], A["hf_w1"])
        dma(SP, nc.sync, d_f, FW2[0:64, :], A["hf_w2"])
        dma(SP, nc.sync, d_f, FW3[0:64, :], A["hf_w3"])
        dma(SP, nc.sync, d_f, FW4[0:64, :], A["hf_w4"])
        t_f = dma(SP, nc.sync, d_f, SKB, A["skip"])
        s_f1 = load([(0, 4096, lambda ap: ap.rearrange("p (t k n) -> p t k n", t=2, k=4), A["dft"][0:2].rearrange("t (k p) n -> p t k n", p=128))])
        s_f2 = load([(0, 4096, lambda ap: ap.rearrange("p (t k n) -> p t k n", t=2, k=4), A["dft"][2:4].rearrange("t (k p) n -> p t k n", p=128))])
        FC, FS = k4(s_f1.ap[:, 0:2048]), k4(s_f1.ap[:, 2048:4096])
        FST, DEC = k4(s_f2.ap[:, 0:2048]), k4(s_f2.ap[:, 2048:4096])
        MAGIC = 12582912.0
        C1, C2 = 6.28125, 2.0 * math.pi - 6.28125
        C2h = float(np.float32(np.round(C2 * 2 ** 21) / 2 ** 21))
        C3 = 2.0 * math.pi - C1 - C2h
        src, tok_s = ZF[0:33, :], t_f
        last_act = t_a2
        for li, (w, kk, bn) in enumerate(((FW1, 33, "hb1"), (FW2, 64, "hb2"), (FW3, 64, "hb3"))):
            b = banks.get()
            tok = mms(b.ap[0:64, :], [(w[0:kk, :], src)], b.free, t_f, tok_s)
            u, n_ = tmp[2][0:64, :], tmp[3][0:64, :]
            t1 = ts(u, b.ap[0:64, :], par(bn, 0)[0:64, :], par("hfr", 0)[0:64, :], ADD, MUL, tok, last_r[0])
            banks.put(b, t1)
            t2 = ts(n_, u, 1.0 / (2.0 * math.pi), MAGIC, MUL, ADD, t1)
            t3 = ts(n_, n_, -MAGIC, None, ADD, None, t2)
            t4 = stt(u, n_, -C1, u, MUL, ADD, t3)
            t5 = stt(u, n_, -C2h, u, MUL, ADD, t4)
            t6 = stt(u, n_, -C3, u, MUL, ADD, t5)
            t7 = ts(u, u, 3.1415925, -3.1415925, ALU.min, ALU.max, t6)
            hm = HM[0:64, :]
            tok_s = act(hm, u, ACT.Sin, t7, tok, t_a2)
            src = hm
        last_r[0] = t7
        t_hm = tok_s
        kf_tok = []
        sb_free = None
        for o in range(2):
            td = [None] * 4
            for c in range(4):
                bf, bb = banks.get(), banks.get()
                lh = HM[0:64, c * 128:(c + 1) * 128]
                t0 = mms(bf.ap, [(lh, FW4[0:64, o * 1024:o * 1024 + 512])], bf.free, t_hm)
                t1 = mms(bb.ap, [(lh, FW4[0:64, o * 1024 + 512:o * 1024 + 1024])], bb.free)
                fw, bw = SB_[:, c, :], DB_[:, c, :]
                t2 = tt(fw, bf.ap, DEC[:, c, :], MUL, t0, s_f2.ready, sb_free, t_hm)
                t3 = tt(bw, bb.ap, DEC[:, c, :], MUL, t1, sb_free)
                banks.put(bf, t2)
                banks.put(bb, t3)
                if c == 0:
                    t3 = DVE.do(lambda bw=bw: v.memset(bw[0:1, :], 0.0), t3)
                td[c] = [t2, t3]
            b = banks.get()
            PE.wait(b.free)
            nn = 0
            for c in range(4):
                for x in (SB_, DB_):
                    ab = tmp[nn % 2]
                    tk = act(ab, x[:, c, :], ACT.Abs, td[c], factor_sq[nn % 2])
                    factor_sq[nn % 2] = tok = PE.do(lambda ab=ab, nn=nn, b=b: t.matmul(b.ap, ones, ab, start=nn == 0, stop=nn == 7), tk)
                    nn += 1
            inv = tmp[2]
            t1 = ts(tmp[3], b.ap, EPS, None, ADD, None, tok, last_r[0])
            banks.put(b, t1)
            t_inv = DVE.do(lambda: v.reciprocal(tmp[2], tmp[3]), t1)
            last_r[0] = t_inv
            tsd = []
            for c in range(4):
                df = tmp[4]
                t1 = tt(df, SB_[:, c, :], DB_[:, c, :], SUB, td[c], tk, tsd[-1] if tsd else last_r[0])
                t2 = tt(SB_[:, c, :], SB_[:, c, :], DB_[:, c, :], ADD, t1, tk)
                t3 = vcopy(DB_[:, c, :], df, t2)
                tsd.append(t3)
            kc0 = 9 * o
            skip = SKB[:, o * 512:(o + 1) * 512]
            for f in range(4):
                b = banks.get()
                tok = mms(b.ap, [(FC[:, k, f * 128:(f + 1) * 128], SB_[:, k, :]) for k in range(4)], b.free, tsd, s_f1.ready)
                kc = KF[:, kc0 + f, :]
                t1 = tt(kc, b.ap, inv, MUL, tok, t_inv)
                banks.put(b, t1)
                t2 = tt(kc, kc, skip, ADD, t1)
                t3 = ts(kc, kc, 2.0 / 1024, None, MUL, None, t2)
                kf_tok.append(t3)
                b = banks.get()
                tok = mms(b.ap, [(FS[:, k, f * 128:(f + 1) * 128], DB_[:, k, :]) for k in range(4)], b.free)
                ks = KF[:, kc0 + 4 + f, :]
                t4 = tt(ks, b.ap, inv, MUL, tok)
                banks.put(b, t4)
                t5 = ts(ks, ks, 2.0 / 1024, None, MUL, None, t4)
                kf_tok.append(t5)
                if f == 0:
                    b = banks.get()
                    tok = mms(b.ap, [(FS[:, k, 0:128], SB_[:, k, :]) for k in range(4)], b.free)
                    kx = KF[:, kc0 + 8, :]
                    t6 = vcopy(kx, kc, t3)
                    t7 = ts(kc[0:1, :], kc[0:1, :], 0.5, None, MUL, None, t6)
                    t8 = DVE.do(lambda ks=ks: v.memset(ks[0:1, :], 0.0), t5)
                    t9 = tt(kx[0:1, :], b.ap[0:1, :], inv[0:1, :], MUL, tok, t6)
                    banks.put(b, t9)
                    t9 = tt(kx[0:1, :], kx[0:1, :], skip[0:1, :], ADD, t9)
                    t9 = ts(kx[0:1, :], kx[0:1, :], 1.0 / 1024, None, MUL, None, t9)
                    kf_tok += [t7, t8, t9]
            sb_free = tok
            last_r[0] = t5

        VF, X1, X2 = tiles(10, 4), tiles(14, 4), tiles(22, 4)
        UT, YC, YS = tiles(18, 4), tiles(5, 4), tiles(22, 4)

        def short(dst, c, tile, b, tok, *after):
            w = lambda j: par("hcw", j * 12 + c)
            raw = tmp[c % 2]
            t0 = act(raw, b.ap, ACT.Copy, tok, factor_sq[c % 2])
            banks.put(b, t0)
            t1 = ts(dst, raw, w(1), par("hcb", c), MUL, ADD, t0, *after)
            t2 = stt(dst[:, 1:S], raw[:, 0:S - 1], w(0), dst[:, 1:S], MUL, ADD, t1)
            t3 = stt(dst[:, 0:S - 1], raw[:, 1:S], w(2), dst[:, 0:S - 1], MUL, ADD, t2)
            factor_sq[c % 2] = t3
            return t3

        def hy_part(dst, i, *after):
            s = load_cols(w2, i * 512, i * 512 + 512)
            toks = []
            for c in range(4):
                b, tok = proj(s, c, t_h)
                toks.append(short(dst[:, c, :], i * 4 + c, c, b, tok, *after))
            slots.put(s, tok)
            return toks

        def to_tokens(dst, src, ready, *after):
            toks = []
            for q in range(4):
                b = banks.get()
                PE.wait(b.free, ready)
                for c in range(4):
                    tok = transpose(b.ap[:, c * 128:(c + 1) * 128], src[:, c, q * 128:(q + 1) * 128], sig=c == 3)
                toks.append(act(dst[:, q, :], b.ap, ACT.Copy, tok, *after))
                banks.put(b, toks[-1])
            return toks, tok

        def spectrum(U, ready, o, *after):
            toks = []
            for f in range(4):
                bc, bs = banks.get(), banks.get()
                tc_ = mms(bc.ap, [(FC[:, k, f * 128:(f + 1) * 128], U[:, k, :]) for k in range(4)], bc.free, ready)
                ts_ = mms(bs.ap, [(FS[:, k, f * 128:(f + 1) * 128], U[:, k, :]) for k in range(4)], bs.free)
                kc, ks = KF[:, 9 * o + f, :], KF[:, 9 * o + 4 + f, :]
                kx = KF[:, 9 * o + 8, :] if f == 0 else kc
                yc, ys, p = YC[:, f, :], YS[:, f, :], tmp[4]
                t1 = tt(yc, bc.ap, kc, MUL, tc_, kf_tok, *after)
                t2 = tt(p, bs.ap, ks, MUL, ts_, last_p[0])
                t3 = tt(yc, yc, p, SUB, t1, t2)
                t4 = tt(ys, bc.ap, ks, MUL, t3)
                t5 = tt(p, bs.ap, kx, MUL, t4)
                banks.put(bc, t4)
                banks.put(bs, t5)
                t6 = tt(ys, ys, p, ADD, t5)
                last_p[0] = t6
                toks += [t3, t6]
            return toks, ts_

        last_p = [last_r[0]]
        t_vf = hy_part(VF, 0, sb_free)
        t_x1 = hy_part(X1, 1, sb_free)
        t_ut, _ = to_tokens(UT, VF, t_vf, sb_free)
        t_y, t_u_free = spectrum(UT, t_ut, 0, sb_free)
        t_x1t, t_x1free = to_tokens(VF, X1, t_x1, t_ut[-1])
        t_y1 = []
        for q in range(4):
            b = banks.get()
            tok = mms(b.ap, [(FC[:, k, q * 128:(q + 1) * 128], YC[:, k, :]) for k in range(4)] +
                      [(FST[:, k, q * 128:(q + 1) * 128], YS[:, k, :]) for k in range(4)], b.free, t_y)
            t1 = tt(UT[:, q, :], b.ap, VF[:, q, :], MUL, tok, t_x1t, t_u_free)
            banks.put(b, t1)
            t_y1.append(t1)
        t_inv0 = tok
        t_y, t_u_free = spectrum(UT, t_y1, 1, t_inv0)
        t_x2 = hy_part(X1, 2, t_x1free)
        HY = X1
        t_hy = []
        for c in range(4):
            b = banks.get()
            tok = mms(b.ap, [(YC[:, k, c * 128:(c + 1) * 128], FC[:, k, :]) for k in range(4)] +
                      [(YS[:, k, c * 128:(c + 1) * 128], FST[:, k, :]) for k in range(4)], b.free, t_y)
            t1 = tt(HY[:, c, :], HY[:, c, :], b.ap, MUL, tok, t_x2[c])
            banks.put(b, t1)
            t_hy.append(t1)
        slots.put(s_f1, tok)
        slots.put(s_f2, tok)

        GA2, GB2 = tiles(18, 8), tiles(26, 8)
        t_ga2, t_gb2 = [None] * 8, [None] * 8
        drain(gates(GA2, w2, 2048, t_ga2, tok, t_hy))
        drain(gates(GB2, w2, 3072, t_gb2))
        t_m = merge(A["w_attn"], A["w_hy"], A2, HY, t_a2, t_hy, t_ga2, t_gb2, GA2, GB2)
        t_x = out_proj(A["w_out_2"], GA2, t_m,
                       lambda c, b, tok: stt(X[:, c, :], b.ap, MOD[:, 16 + c, 0:1], X[:, c, :], MUL, ADD, tok))
        t_h = modulated(X, H, S, lambda k: GF2[:, k:k + 1], lambda k: MOD[:, 24 + k, 0:1], t_x)

        QP = tiles(1, 16)
        t_qp = [None] * 16
        for i in range(4):
            s = load_cols(A["wq"], i * 512, i * 512 + 512)
            for c in range(4):
                b, tok = proj(s, c, t_h)
                t_qp[i * 4 + c] = act(QP[:, i * 4 + c, :], b.ap, ACT.Copy, tok, t_x)
                banks.put(b, t_qp[i * 4 + c])
            slots.put(s, tok)
        s_key = load([(0, 2048, None, A["keys"])])
        KEY = s_key.ap[:, 0:2048].rearrange("p (i n) -> p i n", i=16)
        SC1, SC2 = reg(17, 4).rearrange("p (i n) -> p i n", i=16), reg(21, 4).rearrange("p (i n) -> p i n", i=16)
        CD1, CD2 = reg(25, 4).rearrange("p (h k j) -> p h k j", h=8, k=16), reg(29, 4).rearrange("p (h k j) -> p h k j", h=8, k=16)
        EQ = reg(33, 4).rearrange("p (h k j) -> p h k j", h=8, k=16)
        SMALL = reg(37, 6)
        VAL = SMALL[:, 0:256].rearrange("p (i k) -> p i k", i=16)
        IDX = SMALL[:, 256:512].bitcast(u32).rearrange("p (i k) -> p i k", i=16)
        IDF = SMALL[:, 512:768].rearrange("p (i k) -> p i k", i=16)
        BST = SMALL[:, 768:896].rearrange("p (h k) -> p h k", h=8)
        POS = SMALL[:, 896:1024].bitcast(u32).rearrange("p (h k) -> p h k", h=8)
        PHI = SMALL[:, 1024:1152].bitcast(u32).rearrange("p (h k) -> p h k", h=8)
        PLO = SMALL[:, 1152:1280].bitcast(u32).rearrange("p (h k) -> p h k", h=8)
        PHF = SMALL[:, 1280:1408].rearrange("p (h k) -> p h k", h=8)
        PLF = SMALL[:, 1408:1536].rearrange("p (h k) -> p h k", h=8)
        I1 = SMALL[:, 1536:1664].rearrange("p (h k) -> p h k", h=8)
        I2 = SMALL[:, 1664:1792].rearrange("p (h k) -> p h k", h=8)
        GW = SMALL[:, 1792:1920].rearrange("p (h k) -> p h k", h=8)
        GS = SMALL[:, 1920:1928]
        GR = SMALL[:, 1928:1936]
        I1T, I2T, GT = reg(43, 1), reg(44, 1), reg(45, 1)
        IT = [(I1, I1T), (I2, I2T), (GW, GT)]
        iota16 = iota[:, 0:16].unsqueeze(1).broadcast_to([128, 128, 16])
        t_it = []
        t_s_free = t_tr_free = None
        for q in range(4):
            t_sc = []
            for g in range(4):
                b = banks.get()
                PE.wait(b.free, s_key.ready)
                for i in range(4):
                    ii = g * 4 + i
                    tok = mms(b.ap[:, i * 128:(i + 1) * 128], [(QP[:, ii, q * 128:(q + 1) * 128], KEY[:, ii, :])], t_qp[ii])
                t_sc.append(act(SC1[:, g * 4:g * 4 + 4, :], b.ap.rearrange("p (i n) -> p i n", i=4), ACT.Copy, tok, t_s_free))
                banks.put(b, t_sc[-1])

            def top16(n, src, alt, val, idx, ready, *after):
                ta = [DVE.do(lambda i=i: v.max(val(i)[:, 0:8], src(i)), ready, *after) for i in range(n)]
                tb = [DVE.do(lambda i=i: v.max_index(idx(i)[:, 0:8], val(i)[:, 0:8], src(i)), ta[i]) for i in range(n)]
                tr = [DVE.do(lambda i=i: v.match_replace(alt(i), val(i)[:, 0:8], src(i), -3.0e38), ta[i]) for i in range(n)]
                ta = [DVE.do(lambda i=i: v.max(val(i)[:, 8:16], alt(i)), tr[i]) for i in range(n)]
                tb2 = [DVE.do(lambda i=i: v.max_index(idx(i)[:, 8:16], val(i)[:, 8:16], alt(i)), ta[i]) for i in range(n)]
                return tb2[-1]

            DVE.wait(DVE.last())
            t1 = top16(16, lambda i: SC1[:, i, :], lambda i: SC2[:, i, :], lambda i: VAL[:, i, :], lambda i: IDX[:, i, :], t_sc)
            t_s_free = t1
            t2 = vcopy(IDF, IDX, t1)
            V4 = VAL.rearrange("p (h s) k -> p h s k", s=2)
            F4 = IDF.rearrange("p (h s) k -> p h s k", s=2)
            t3 = None
            for h in range(8):
                t3 = tt(CD1[:, h, :, :], V4[:, h, 0, :].unsqueeze(2).broadcast_to([128, 16, 16]),
                        V4[:, h, 1, :].unsqueeze(1).broadcast_to([128, 16, 16]), ADD, t1)
            fl = lambda ap: ap.rearrange("p k j -> p (k j)")
            t4 = top16(8, lambda h: fl(CD1[:, h, :, :]), lambda h: fl(CD2[:, h, :, :]), lambda h: BST[:, h, :],
                       lambda h: POS[:, h, :], t3)
            t5 = DVE.do(lambda: v.tensor_scalar(out=PHI, in0=POS, scalar1=4, scalar2=None, op0=ALU.logical_shift_right), t4)
            t6 = DVE.do(lambda: v.tensor_scalar(out=PLO, in0=POS, scalar1=15, scalar2=None, op0=ALU.bitwise_and), t4)
            t5 = vcopy(PHF, PHI, t5)
            t6 = vcopy(PLF, PLO, t6)
            t9 = []
            for side, (pf, dst) in enumerate(((PHF, I1), (PLF, I2))):
                pfl = pf.rearrange("p h k -> p (h k)").unsqueeze(2).broadcast_to([128, 128, 16])
                eq = EQ.rearrange("p h k j -> p (h k) j")
                t7 = tt(eq, pfl, iota16, ALU.is_equal, t5, t6, t9[-1] if t9 else None)
                for h in range(8):
                    t8 = tt(EQ[:, h, :, :], EQ[:, h, :, :], F4[:, h, side, :].unsqueeze(1).broadcast_to([128, 16, 16]), MUL, t7, t2)
                t9.append(DVE.do(lambda dst=dst, eq=eq: v.tensor_reduce(out=dst.rearrange("p h k -> p (h k)"), in_=eq, axis=AX.X, op=ADD), t8, t_tr_free))
            u1 = tt(GW, BST, BST[:, :, 0:1].broadcast_to([128, 8, 16]), SUB, t4, t_tr_free)
            u2 = act(GW, GW, ACT.Exp, u1)
            u3 = DVE.do(lambda: v.tensor_reduce(out=GS, in_=GW, axis=AX.X, op=ADD), u2)
            u4 = DVE.do(lambda: v.reciprocal(GR, GS), u3)
            u5 = tt(GW, GW, GR.unsqueeze(2).broadcast_to([128, 8, 16]), MUL, u4)
            b = banks.get()
            PE.wait(b.free, t9, u5)
            for i, (src, dst) in enumerate(IT):
                tok = transpose(b.ap[:, i * 128:(i + 1) * 128], src.rearrange("p h k -> p (h k)"), sig=i == 2)
            t_tr_free = tok
            for i, (src, dst) in enumerate(IT):
                t_it.append(act(dst[:, q * 128:(q + 1) * 128], b.ap[:, i * 128:(i + 1) * 128], ACT.Copy, tok, t_x))
            banks.put(b, t_it[-1])
        slots.put(s_key, tok)

        WS = [reg(1, 16), reg(17, 16)]
        OH = reg(33, 8).rearrange("p (r s n) -> p r s n", r=16, s=2)
        oh_free = [None] * 4
        ws_free = [None, None]
        d_ws = [dsem("d_ws0"), dsem("d_ws1")]
        t_w = []
        for tb_ in range(8):
            wv = WS[tb_ % 2].rearrange("p (i t) -> p i t", t=64)
            for g in range(16):
                r0 = (g % 4) * 4
                toks = []
                for i in range(4):
                    n = tb_ * 64 + g * 4 + i
                    o2, o1 = OH[:, r0 + i, 0, :], OH[:, r0 + i, 1, :]
                    ts(o2, iota, I2T[:, n:n + 1], None, ALU.is_equal, None, t_it, oh_free[g % 4], t_tr_free)
                    toks.append(ts(o1, iota, I1T[:, n:n + 1], GT[:, n:n + 1], ALU.is_equal, MUL))
                b = banks.get()
                PE.wait(b.free, toks)
                for i in range(4):
                    tok = mms(b.ap[:, i * 128:(i + 1) * 128], [(OH[:, r0 + i, 0, :], OH[:, r0 + i, 1, :])])
                oh_free[g % 4] = tok
                t1 = act(wv[:, :, g * 4:g * 4 + 4].rearrange("p i t -> p t i"), b.ap.rearrange("p (t i) -> p t i", t=4), ACT.Copy,
                         tok, ws_free[tb_ % 2])
                banks.put(b, t1)
            ws_free[tb_ % 2] = dma(SC, nc.scalar, d_ws[tb_ % 2], Wd[tb_], WS[tb_ % 2], t1)
            t_w = [ws_free[0], ws_free[1]]

        Y = tiles(1, 8)
        GE = [tiles(9, 4), tiles(13, 4)]
        wring = Pool([Place(reg(17 + 4 * i, 4), sem(f"s_wr{i}")) for i in range(3)])
        for p_ in wring.q:
            p_.free = [t_w, tok]
        ge_free = [None, None]
        t_yy = [None] * 8

        def peer_up(c):
            s = load([(0, 4096, k8, A["u"][c])])
            wr = wring.get()
            wt = dma(SP, nc.sync, wr.counter, wr.ap.rearrange("p (b i) -> p b i", b=8),
                     Wd.rearrange("b p (c i) -> c p b i", c=32)[c], wr.free, t_w)
            ww = wr.ap.rearrange("p (b i t) -> p i b t", b=8, i=4)
            w = k8(s.ap)
            ge = GE[c % 2]
            toks = []
            for i in range(4):
                b = banks.get()
                tok = mms(b.ap, [(w[:, k, i * 128:(i + 1) * 128], H[:, k, :]) for k in range(8)], b.free, s.ready, t_h)
                t1 = act(ge[:, i, :], b.ap, ACT.Gelu_apprx_tanh, tok, ge_free[c % 2], t_w)
                banks.put(b, t1)
                g3 = ge[:, i, :].rearrange("p (b t) -> p b t", b=8)
                toks.append(tt(g3, g3, ww[:, i, :, :], MUL, t1, wt))
            slots.put(s, tok)
            wring.put(wr, toks[-1])
            return toks

        def peer_down(c, ready):
            s = load([(0, 4096, k4, A["v"][c * 512:(c + 1) * 512, :].rearrange("(k p) n -> p k n", p=128))])
            w = k4(s.ap)
            for d in range(8):
                b = banks.get()
                tok = mms(b.ap, [(w[:, k, d * 128:(d + 1) * 128], GE[c % 2][:, k, :]) for k in range(4)], b.free, s.ready, ready)
                if c == 0:
                    t_yy[d] = vcopy(Y[:, d, :], b.ap, tok, t_w)
                else:
                    t_yy[d] = tt(Y[:, d, :], Y[:, d, :], b.ap, ADD, tok, t_yy[d])
                banks.put(b, t_yy[d])
            ge_free[c % 2] = tok
            slots.put(s, tok)

        ready = peer_up(0)
        for c in range(32):
            nxt = peer_up(c + 1) if c < 31 else None
            peer_down(c, ready)
            ready = nxt

        for d in range(8):
            t_x = stt(X[:, d, :], Y[:, d, :], MOD[:, 40 + d, 0:1], X[:, d, :], MUL, ADD, t_yy[d])
        PE.wait(t_x)
        t_h = norm(X, lambda k: par("gfin", k), t_x, PE.last())
        t_o = dma(SP, nc.sync, d_o, out.rearrange("(k p) n -> p k n", p=128), H, t_h)
        SP.wait(t_o)

        block = ctx.enter_context(nc.Block())

        @block.sync
        def _(eng):
            SP.run(eng)

        @block.gpsimd
        def _(eng):
            GP.run(eng)

        @block.scalar
        def _(eng):
            SC.run(eng)

        @block.vector
        def _(eng):
            DVE.run(eng)

        @block.tensor
        def _(eng):
            PE.run(eng)


def constants():
    f = np.float32
    i = np.arange(128)
    c = {
        "ident": np.eye(128), "ones": np.ones((128, 128)),
        "blk": (i[:, None] // 64 == i[None] // 64),
        "linc": (i[:, None] >= i[None]), "smask": (i[None] > i[:, None]),
        "nmask": np.where(i[None] > i[:, None], 0.0, -BIG),
        "iota": np.broadcast_to(i, (128, 128)),
    }
    rot = np.zeros((128, 128))
    for d in range(128):
        if d % 32 < 16:
            rot[d + 16, d] = -1.0
        else:
            rot[d - 16, d] = 1.0
    c["rot"] = rot
    consts = np.concatenate([np.asarray(c[n], f) for n in CNAMES], axis=1)
    tpos = np.arange(S)
    row, col = (tpos // 64).astype(f), (tpos % 64).astype(f)
    inv = f(10000.0) ** (-np.arange(0, 32, 2, dtype=f) / f(32))
    ar, ac = row[:, None] * inv, col[:, None] * inv
    ang = np.concatenate([ar, ar, ac, ac], axis=-1).astype(f).T
    ang = np.concatenate([ang, ang], axis=0)
    rope = np.stack([np.cos(ang), np.sin(ang)]).astype(f)
    t01 = np.linspace(0.0, 1.0, S, dtype=f)[:, None]
    w = (f(2.0 * math.pi) * np.arange(S, dtype=f)[:, None] / f(S)).astype(f)
    fr = np.linspace(1e-4, 15, 16, dtype=f)[None]
    zf = np.concatenate([t01, np.cos(fr * w), -np.sin(fr * w)], axis=-1).astype(f).T
    deltas = np.abs(np.linspace(math.log(1e-2) / 1.5, math.log(1e-2) / 0.3, 512, dtype=f))
    dec = np.exp(-t01 * deltas).astype(f)
    n = np.arange(S)
    ph = (n[:, None] * n[None]) % 1024 * (2.0 * math.pi / 1024)
    fc, fs = np.cos(ph), np.sin(ph)
    fs[:, 0] = np.where(n % 2 == 0, 1.0, -1.0)
    dft = np.stack([fc, fs, fs.T, dec]).astype(f)
    return {"consts": consts, "rope": np.ascontiguousarray(rope), "zf": np.ascontiguousarray(zf), "dft": dft}


def layout(I):
    c = np.ascontiguousarray

    def cols(x):
        return np.asarray(x).reshape(-1, 128).T

    def twice(x):
        return np.concatenate([x, x]).reshape(128, 1)

    def pad(x):
        return np.concatenate([x, x]).reshape(128, 1)

    p = {
        "g1": cols(I["norm_mix_g"]), "gf1": cols(I["norm_ffn_g"]),
        "qg1": twice(I["q_norm_g"][0]), "kg1": twice(I["k_norm_g"][0]),
        "cw": cols(I["conv_w"]),
        "rb": np.broadcast_to(np.concatenate([I["b_router_group"][0], I["b_router_expert"][0]]), (128, 36)),
        "ab": cols(I["ada_b_2"]), "g2": cols(I["norm_mix_g_2"]), "gf2": cols(I["norm_ffn_g_2"]),
        "gfin": cols(I["final_norm_g_2"]), "qg2": twice(I["q_norm_g_2"][0]), "kg2": twice(I["k_norm_g_2"][0]),
        "hcw": cols(I["hy_conv_w_2"]), "hcb": cols(I["hy_conv_b_2"]),
        "hb1": pad(I["hf_b1_2"][0]), "hb2": pad(I["hf_b2_2"][0]), "hb3": pad(I["hf_b3_2"][0]), "hfr": pad(I["hf_freq_2"][0]),
        "cc": np.stack([cols(I["c_2"]), cols(I["c_ctx_2"])], axis=2).reshape(128, 16),
    }
    params = np.concatenate([p[n] for n in PCOLS], axis=1)
    w2 = I["w_in_2"][0]
    qc = w2[:, 0:512].reshape(D, 2, 4, 64).transpose(0, 2, 1, 3).reshape(D, 512)
    w_in_2 = np.concatenate([w2[:, 768:2304], qc, w2[:, 2304:4352], w2[:, 512:768]], axis=1)
    wa = I["w_attn_out_2"][0].reshape(2, 4, 64, D).transpose(1, 0, 2, 3).reshape(512, D)
    keys = np.stack([I["peer_keys1_2"][0], I["peer_keys2_2"][0]], axis=1)
    u = I["peer_u_2"][0].reshape(32, 512, 8, 128).transpose(0, 3, 2, 1)
    skip = np.broadcast_to(I["hy_skip_2"][0].reshape(1, 1024), (128, 1024))
    out = {
        "params": c(params), "x": c(I["x"][0].T), "ctx": c(I["ctx_2"][0].T),
        "w_in": I["w_in"][0], "w_sb": I["w_sb_branch"][0], "w_conv": I["w_conv_branch"][0], "w_out": I["w_out"][0],
        "w_router": c(np.concatenate([I["w_router_group"][0], I["w_router_expert"][0]], axis=1)),
        "w_gate": I["w_gate_e"][0], "w_up": I["w_up_e"][0], "w_down": I["w_down_e"][0],
        "ada_w": I["ada_w_2"][0], "w_in_2": c(w_in_2), "w_attn": c(wa), "w_hy": I["w_hy_out_2"][0],
        "w_out_2": I["w_out_2"][0], "wq": I["peer_wq_2"][0],
        "keys": c(keys.transpose(3, 0, 1, 2).reshape(128, 2048)),
        "u": c(u), "v": I["peer_v_2"][0], "skip": c(skip),
        "hf_w1": I["hf_w1_2"][0], "hf_w2": I["hf_w2_2"][0], "hf_w3": I["hf_w3_2"][0], "hf_w4": I["hf_w4_2"][0],
    }
    return {k: c(np.asarray(x)) for k, x in out.items()}


def kernel(**inputs):
    import concourse.bacc as bacc
    from concourse.bass_utils import run_bass_kernel_spmd

    arrays = layout({k: np.asarray(x) for k, x in inputs.items()})
    arrays.update(constants())
    nc = bacc.Bacc("TRN2", target_bir_lowering=False, num_devices=1)
    feeds, A = {}, {}
    for name, x in arrays.items():
        feeds[f"in_{name}"] = x
        A[name] = nc.dram_tensor(f"in_{name}", x.shape, mybir.dt.from_np(x.dtype), kind="ExternalInput").ap()
    if "u" in A:
        A["u"] = A["u"]
    out = nc.dram_tensor("out_0", (D, S), mybir.dt.float32, kind="ExternalOutput").ap()
    program(nc, A, out)
    r = run_bass_kernel_spmd(nc, [feeds], core_ids=[0])
    return np.ascontiguousarray(r.results[0]["out_0"].T)[None]
```

```python
import math

import numpy as np

import concourse.bass as bass
from concourse import mybir

S = 512
D = 1024
EPS = 1e-6
BIG = 1.0e30

PCOLS = {}
_n = 0
for _name, _w in [("g1", 8), ("gf1", 8), ("qg1", 1), ("kg1", 1), ("cw", 12), ("rb", 36), ("ab", 48),
                  ("g2", 8), ("gf2", 8), ("gfin", 8), ("qg2", 1), ("kg2", 1), ("hcw", 36), ("hcb", 12),
                  ("hb1", 1), ("hb2", 1), ("hb3", 1), ("hfr", 1), ("cc", 16)]:
    PCOLS[_name] = (_n, _n + _w)
    _n += _w
PTOTAL = _n
CNAMES = ["ident", "ones", "blk", "linc", "smask", "nmask", "iota", "rot"]


class Engine:

    def __init__(self, sem):
        self.sem, self.n, self.items, self.seen = sem, 0, [], {}

    def wait(self, *toks):
        for t in toks:
            if t is None:
                continue
            if isinstance(t, list):
                self.wait(*t)
                continue
            sem, val = t
            if self.seen.get(id(sem), 0) < val:
                self.seen[id(sem)] = val
                self.items.append((None, sem, val))

    def do(self, fn, *after, sig=True):
        self.wait(*after)
        if not sig:
            self.items.append((fn, None, 0))
            return None
        self.n += 1
        self.items.append((fn, self.sem, 1))
        return (self.sem, self.n)

    def last(self):
        return (self.sem, self.n) if self.n else None

    def run(self, eng):
        for fn, sem, val in self.items:
            if fn is None:
                eng.wait_ge(sem, val)
            else:
                ins = fn()
                if sem is not None:
                    ins.then_inc(sem, val)


class Counter:
    def __init__(self, sem):
        self.sem, self.n = sem, 0


class Place:

    def __init__(self, ap, sem=None):
        self.ap, self.free, self.counter = ap, [], Counter(sem)


class Pool:
    def __init__(self, places):
        self.q = list(places)

    def get(self):
        return self.q.pop(0)

    def put(self, place, *toks):
        place.free = list(toks)
        self.q.append(place)


def program(nc, A, out):
    f32 = mybir.dt.float32
    u32 = mybir.dt.uint32
    bf16 = mybir.dt.bfloat16
    f32r = mybir.dt.float32r
    ALU = mybir.AluOpType
    ACT = mybir.ActivationFunctionType
    AX = mybir.AxisListType
    from contextlib import ExitStack
    ctx = ExitStack()
    with ctx:
        def sb(name, cols, dt=f32, stack=None, side=None):
            return (stack or ctx).enter_context(nc.sbuf_tensor(name, [128, cols], dt, side=side))

        early, ring = ExitStack(), ExitStack()

        def sem(name):
            return ctx.enter_context(nc.semaphore(name))

        def dsem(name):
            return Counter(sem(name))

        v, a, t = nc.vector, nc.scalar, nc.tensor
        PE, DVE, SC, GP, SP = (Engine(sem(n)) for n in ("s_pe", "s_dve", "s_act", "s_pool", "s_sp"))

        def dma(queue, eng, counter, dst, src, *after):
            counter.n += 16
            sem_ = counter.sem
            queue.wait(*after)
            queue.items.append((lambda: eng.dma_start(dst, src), sem_, 16))
            return (sem_, counter.n)

        def dma_call(queue, counter, call, *after):
            counter.n += 16
            queue.wait(*after)
            queue.items.append((call, counter.sem, 16))
            return (counter.sem, counter.n)

        X = sb("X", 8 * S)[:, :].rearrange("p (k n) -> p k n", k=8)
        H = sb("H", 8 * S)[:, :].rearrange("p (k n) -> p k n", k=8)
        NSLOT = 4
        slots = Pool([Place(sb(f"W{i}", 4096, f32, ring, "right")[:, :], sem(f"s_w{i}")) for i in range(NSLOT)])
        NA = 46
        TMP = sb("tmp", 5 * S)
        CST = sb("cst", len(CNAMES) * 128)
        PAR = sb("par", PTOTAL)
        MODS = sb("mods", 136)
        TID = sb("tid", 4, u32)
        arena = sb("arena", NA * S, f32, early)
        banks = Pool([Place(ctx.enter_context(nc.psum_tensor(f"P{i}", [128, 512], f32))[:, :]) for i in range(8)])
        Wd = nc.dram_tensor("w_scratch", [16, 128, 128 * 32], f32).ap()
        NT = 39
        Hd = nc.dram_tensor("h_rows", [S, D], f32).ap()
        Ld = nc.dram_tensor("slot_list", [128 * NT, 1], u32).ap()
        Yd = nc.dram_tensor("y_rows", [128 * NT, D], f32).ap()

        def reg(at, n):
            assert at + n <= NA
            return arena[:, at * S:(at + n) * S]

        def tiles(at, n):
            return reg(at, n).rearrange("p (k n) -> p k n", k=n)

        def cst(name):
            i = CNAMES.index(name)
            return CST[:, i * 128:(i + 1) * 128]

        def par(name, i=None):
            lo, hi = PCOLS[name]
            return PAR[:, lo:hi] if i is None else PAR[:, lo + i:lo + i + 1]

        ident, ones, blk = cst("ident"), cst("ones"), cst("blk")
        tmp = [TMP[:, i * S:(i + 1) * S] for i in range(5)]

        def tt(out_, in0, in1, op, *after):
            return DVE.do(lambda: v.tensor_tensor(out=out_, in0=in0, in1=in1, op=op), *after)

        def ts(out_, in0, s1, s2, op0, op1, *after):
            if op1 is None:
                return DVE.do(lambda: v.tensor_scalar(out=out_, in0=in0, scalar1=s1, scalar2=None, op0=op0), *after)
            return DVE.do(lambda: v.tensor_scalar(out=out_, in0=in0, scalar1=s1, scalar2=s2, op0=op0, op1=op1), *after)

        def stt(out_, in0, s, in1, op0, op1, *after):
            return DVE.do(lambda: v.scalar_tensor_tensor(out=out_, in0=in0, scalar=s, in1=in1, op0=op0, op1=op1), *after)

        def vcopy(out_, in_, *after):
            return DVE.do(lambda: v.tensor_copy(out_, in_), *after)

        def act(out_, in_, fn, *after, bias=None, scale=None, acc=None):
            kw = {}
            if bias is not None:
                kw["bias"] = bias
            if scale is not None:
                kw["scale"] = scale
            if acc is not None:
                kw["accum_out"] = acc
            return SC.do(lambda: a.activation(out_, in_, fn, **kw), *after)

        def mms(out_, pairs, *after, start=True, stop=True):
            PE.wait(*after)
            n = len(pairs)
            tok = None
            for i, (l, r) in enumerate(pairs):
                st, sp = start and i == 0, stop and i == n - 1
                tok = PE.do(lambda l=l, r=r, st=st, sp=sp: t.matmul(out_, l, r, start=st, stop=sp), sig=i == n - 1)
            return tok

        def transpose(out_, in_, *after, sig=True):
            return PE.do(lambda: t.transpose(out_, in_, ident), *after, sig=sig)

        MUL, ADD, SUB = ALU.mult, ALU.add, ALU.subtract

        def split(hi, lo, x, *after):
            t1 = act(hi, x, ACT.Copy, *after)
            return tt(lo, x, hi.bitcast(f32), SUB, t1)

        def three(wh, wl, xh, xl):
            return [(wh, xh), (wh, xl), (wl, xh)]

        def load(pieces, *after):
            s = slots.get()
            tok = None
            for lo, hi, view, src in pieces:
                dst = s.ap[:, lo:hi]
                if view:
                    dst = view(dst)
                tok = dma(SP, nc.sync, s.counter, dst, src, s.free, *after)
            s.ready = tok
            return s

        k8 = lambda ap: ap.rearrange("p (k n) -> p k n", k=8)
        k4 = lambda ap: ap.rearrange("p (k n) -> p k n", k=4)
        k2 = lambda ap: ap.rearrange("p (k n) -> p k n", k=2)

        def load_cols(w, lo, hi):
            n = hi - lo
            return load([(0, 8 * n, k8, w[:, lo:hi].rearrange("(k p) n -> p k n", p=128))])

        def load_half(w):
            return load([(0, 4096, k4, w.rearrange("(k p) n -> p k n", p=128))])

        d_x, d_c, d_p, d_o = dsem("d_x"), dsem("d_c"), dsem("d_p"), dsem("d_o")
        t_c = dma(SC, nc.scalar, d_c, CST[:, :], A["consts"])
        t_p = dma(SC, nc.scalar, d_p, PAR[:, :], A["params"])
        t_tid = dma(SC, nc.scalar, dsem("d_t"), TID[:, :], A["tid"])
        t_x = dma(SP, nc.sync, d_x, X, A["x"].rearrange("(k p) n -> p k n", p=128))
        for e in (PE, DVE, SC, GP):
            e.wait(t_c, t_p)

        last_r = [None]

        def factor(srcs, lhs, inv, n, *after):
            b = banks.get()
            PE.wait(b.free)
            sq_free = factor_sq
            tok = None
            for i, s in enumerate(srcs):
                j = i % 2
                q = tmp[j][:, 0:n]
                tk = act(q, s, ACT.Square, sq_free[j], *after)
                tok = PE.do(lambda q=q, i=i: t.matmul(b.ap[:, 0:n], lhs, q, start=i == 0, stop=i == len(srcs) - 1), tk)
                sq_free[j] = tok
            m, r, w = tmp[2][:, 0:n], tmp[3][:, 0:n], tmp[4][:, 0:n]
            t1 = ts(m, b.ap[:, 0:n], inv, EPS, MUL, ADD, tok, last_r[0])
            banks.put(b, t1)
            t2 = act(r, m, ACT.Sqrt, t1)
            t3 = DVE.do(lambda: v.reciprocal(w, r), t2)
            t4 = tt(r, w, w, MUL, t3)
            t5 = tt(r, r, m, MUL, t4)
            t6 = ts(r, r, -0.5, 1.5, MUL, ADD, t5)
            t7 = tt(r, r, w, MUL, t6)
            return r, t7

        factor_sq = [None, None]

        def norm(src, gain, *after):
            r, tr = factor([src[:, k, :] for k in range(8)], ones, 1.0 / D, S, *after)
            toks = []
            for k in range(8):
                toks.append(stt(H[:, k, :], src[:, k, :], gain(k), r, MUL, MUL, tr))
            last_r[0] = toks[-1]
            return toks[-1]

        def proj(slot, c, h_tok, width=512):
            b = banks.get()
            w = slot.ap[:, 0:8 * width].rearrange("p (k n) -> p k n", k=8)
            tok = mms(b.ap, [(w[:, k, c * 128:(c + 1) * 128], H[:, k, :]) for k in range(8)], b.free, slot.ready, h_tok)
            return b, tok

        def drain(gen):
            for _ in gen:
                pass

        def mix(*gens):
            gens = list(gens)
            while gens:
                for g in list(gens):
                    try:
                        next(g)
                    except StopIteration:
                        gens.remove(g)

        t_h = norm(X, lambda k: par("g1", k), t_x)
        Q, K, V, AT = tiles(0, 4), tiles(4, 4), tiles(8, 4), tiles(12, 4)
        CB, CC, CU = tiles(16, 4), tiles(20, 4), tiles(24, 4)
        GA, GB = tiles(28, 8), tiles(36, 8)
        w_in = A["w_in"]

        def head_norm(dst, b, tok, gain):
            t0 = act(dst, b.ap, ACT.Copy, tok)
            r, tr = factor([dst], blk, 1.0 / 64, S, t0)
            banks.put(b, t0)
            t1 = stt(dst, dst, gain, r, MUL, MUL, tr)
            last_r[0] = t1
            return t1

        t_q, t_k, t_v = [None] * 4, [None] * 4, [None] * 4

        def project_qkv():
            for which, dst, gain, toks in ((0, Q, "qg1", t_q), (1, K, "kg1", t_k)):
                s = load_cols(w_in, which * 512, which * 512 + 512)
                held = []
                for c in range(4):
                    held.append(proj(s, c, t_h))
                slots.put(s, held[-1][1])
                for c in range(4):
                    toks[c] = head_norm(dst[:, c, :], *held[c], par(gain, 0))
            s = load_cols(w_in, 1024, 1536)
            w = k8(s.ap)
            for c in range(4):
                b = banks.get()
                tok = mms(b.ap, [(H[:, k, c * 128:(c + 1) * 128], w[:, k, :]) for k in range(8)], b.free, s.ready, t_h)
                t_v[c] = act(V[:, c, :], b.ap, ACT.Copy, tok)
                banks.put(b, t_v[c])
            slots.put(s, tok)

        project_qkv()

        OFF = [0, 512, 896, 1152]
        ZB = [reg(36, 10)[:, 0:1280], reg(36, 10)[:, 1280:2560]]
        EB = [reg(36, 10)[:, 2560:3840], reg(36, 10)[:, 3840:5120]]
        pv_tok = [None] * 8
        t_at = [None] * 8
        in_free = [None] * 8

        def attention():
            for h in range(8):
                j, po = h // 2, 64 * (h % 2)
                Z, E = ZB[h % 2], EB[h % 2]
                tz = None
                for i in range(4):
                    n = 512 - 128 * i
                    b = banks.get()
                    tok = mms(b.ap[:, 0:n], [(K[po:po + 64, j, i * 128:(i + 1) * 128], Q[po:po + 64, j, i * 128:512])],
                              b.free, t_q[j], t_k[j])
                    tz = act(Z[:, OFF[i]:OFF[i] + n], b.ap[:, 0:n], ACT.Copy, tok, pv_tok[h - 2] if h >= 2 else None, scale=0.125)
                    banks.put(b, tz)
                t1 = act(E, Z, ACT.Abs, tz, in_free[h - 2] if h >= 2 else None)
                t2 = act(E, E, ACT.Exp, t1, scale=-1.0)
                t3 = act(E, E, ACT.Ln, t2, bias=1.0)
                t4 = stt(E, Z, 0.0, E, ALU.max, ADD, t3)
                for i in range(4):
                    d = E[:, OFF[i]:OFF[i] + 128]
                    t5 = tt(d, d, cst("smask"), MUL, t4)
                yield
                te = None
                for i in range(4):
                    n = 512 - 128 * i
                    b = banks.get()
                    PE.wait(b.free, t5)
                    for jj in range(i, 4):
                        l = cst("linc") if jj == i else ones
                        o = (jj - i) * 128
                        tok = PE.do(lambda b=b, l=l, o=o, jj=jj, i=i, n=n, E=E: t.matmul(
                            b.ap[:, o:n], l, E[:, OFF[jj]:OFF[jj] + 512 - 128 * jj], start=jj == i, stop=jj == 3),
                            sig=jj == 3)
                    z = Z[:, OFF[i]:OFF[i] + n]
                    t6 = tt(z, z, b.ap[:, 0:n], SUB, tok, tz)
                    banks.put(b, t6)
                    t7 = tt(z[:, 0:128], z[:, 0:128], cst("nmask"), ADD, t6)
                in_free[h] = tok
                te = act(Z, Z, ACT.Exp, t7)
                yield
                b = banks.get()
                PE.wait(b.free, te, t_v)
                for i in range(4):
                    tok = PE.do(lambda i=i, b=b, Z=Z, h=h, po=po: t.matmul(
                        b.ap[po:po + 64, 128 * i:512], V[:, i, h * 64:(h + 1) * 64],
                        Z[:, OFF[i]:OFF[i] + 512 - 128 * i], start=i == 0, stop=i == 3), sig=i == 3)
                pv_tok[h] = tok
                t_at[h] = act(AT[po:po + 64, j, :], b.ap[po:po + 64, :], ACT.Copy, tok)
                banks.put(b, t_at[h])
                yield

        t_cv = [None] * 4
        t_ga = [None] * 8

        def conv_gates():
            t_cb, t_cc = [None] * 4, [None] * 4
            for dst, lo, toks in ((CB, 1536, t_cb), (CC, 2048, t_cc)):
                s = load_cols(w_in, lo, lo + 512)
                for c in range(4):
                    b, tok = proj(s, c, t_h)
                    toks[c] = act(dst[:, c, :], b.ap, ACT.Copy, tok)
                    banks.put(b, toks[c])
                    yield
                slots.put(s, tok)
            s = load_cols(w_in, 2560, 3072)
            for c in range(4):
                b, tok = proj(s, c, t_h)
                cu, y = CC[:, c, :], CU[:, c, :]
                cw = lambda j, c=c: par("cw", j * 4 + c)
                t1 = tt(cu, cu, b.ap, MUL, tok, t_cc[c])
                banks.put(b, t1)
                t2 = ts(y, cu, cw(2), None, MUL, None, t1)
                t3 = stt(y[:, 1:S], cu[:, 0:S - 1], cw(1), y[:, 1:S], MUL, ADD, t2)
                t4 = stt(y[:, 2:S], cu[:, 0:S - 2], cw(0), y[:, 2:S], MUL, ADD, t3)
                t_cv[c] = tt(y, y, CB[:, c, :], MUL, t4, t_cb[c])
                yield
            slots.put(s, tok)
            for half in range(2):
                s = load_cols(w_in, 3072 + half * 512, 3584 + half * 512)
                for c in range(4):
                    b, tok = proj(s, c, t_h)
                    i = half * 4 + c
                    t_ga[i] = act(GA[:, i, :], b.ap, ACT.Sigmoid, tok)
                    banks.put(b, t_ga[i])
                    yield
                slots.put(s, tok)

        mix(attention(), conv_gates())

        t_gb = [None] * 8

        def gates(dst, w, lo, toks, *after):
            for half in range(2):
                s = load_cols(w, lo + half * 512, lo + half * 512 + 512)
                for c in range(4):
                    b, tok = proj(s, c, t_h)
                    i = half * 4 + c
                    toks[i] = act(dst[:, i, :], b.ap, ACT.Sigmoid, tok, *after)
                    banks.put(b, toks[i])
                    yield
                slots.put(s, tok)

        drain(gates(GB, w_in, 4096, t_gb, pv_tok[6], pv_tok[7], in_free[6], in_free[7]))

        def merge(wa, wb, ATT, CONV, t_att, t_conv, t_g1, t_g2, ga, gb):
            toks = []
            for w, src, ready, g, tg in ((wa, ATT, t_att, ga, t_g1), (wb, CONV, t_conv, gb, t_g2)):
                s = load_half(w)
                wv = k4(s.ap)
                for c in range(8):
                    b = banks.get()
                    tok = mms(b.ap, [(wv[:, k, c * 128:(c + 1) * 128], src[:, k, :]) for k in range(4)], b.free, s.ready, ready)
                    t1 = tt(g[:, c, :], g[:, c, :], b.ap, MUL, tok, tg[c])
                    banks.put(b, t1)
                    if g is gb:
                        toks.append(tt(ga[:, c, :], ga[:, c, :], g[:, c, :], ADD, t1))
                slots.put(s, tok)
            return toks

        t_m = merge(A["w_sb"], A["w_conv"], AT, CU, t_at, t_cv, t_ga, t_gb, GA, GB)

        def out_proj(w, M, t_m, add):
            for half in range(2):
                s = load_cols(w, half * 512, half * 512 + 512)
                wv = k8(s.ap)
                for c in range(4):
                    b = banks.get()
                    tok = mms(b.ap, [(wv[:, k, c * 128:(c + 1) * 128], M[:, k, :]) for k in range(8)], b.free, s.ready, t_m)
                    t1 = add(half * 4 + c, b, tok)
                    banks.put(b, t1)
                slots.put(s, tok)
            return t1

        t_x = out_proj(A["w_out"], GA, t_m, lambda c, b, tok: tt(X[:, c, :], X[:, c, :], b.ap, ADD, tok))

        MOD, SCC = MODS[:, 0:96].rearrange("p (k n) -> p k n", n=2), MODS[:, 96:112].rearrange("p (k n) -> p k n", n=2)
        G2, GF2 = MODS[:, 112:128], MODS[:, 128:136]
        t_g2 = None

        def ada():
            nonlocal t_g2
            t_sc = act(SCC, par("cc").rearrange("p (k n) -> p k n", n=2), ACT.Silu)
            b = banks.get()
            PE.wait(b.free, t_sc)
            for i in range(12):
                s = load_cols(A["ada_w"], i * 512, i * 512 + 512)
                w = k8(s.ap)
                for c in range(4):
                    j = i * 4 + c
                    tok = mms(b.ap[:, 2 * j:2 * j + 2], [(w[:, k, c * 128:(c + 1) * 128], SCC[:, k, :]) for k in range(8)], s.ready)
                slots.put(s, tok)
            t_mod = tt(MOD, b.ap[:, 0:96].rearrange("p (k n) -> p k n", n=2), par("ab").unsqueeze(2).broadcast_to([128, 48, 2]),
                       ADD, tok)
            banks.put(b, t_mod)
            for w in range(2):
                t_g2 = stt(G2[:, 8 * w:8 * w + 8], MOD[:, 8:16, w], 1.0, par("g2"), ADD, MUL, t_mod)
            t_g2 = stt(GF2, MOD[:, 32:40, 0], 1.0, par("gf2"), ADD, MUL, t_mod, t_g2)
            return t_g2

        t_h = norm(X, lambda k: par("gf1", k), t_x)
        base = [0]
        scr = reg(0, 8)

        def small(n):
            base[0] += n
            return scr[:, base[0] - n:base[0]]

        WR = small(8 * 36).rearrange("p (k n) -> p k n", k=8)
        d_r = dsem("d_r")
        t_r = dma(SC, nc.scalar, d_r, WR, A["w_router"].rearrange("(k p) n -> p k n", p=128), t_x)
        b = banks.get()
        for q in range(4):
            tok = mms(b.ap[:, q * 36:(q + 1) * 36], [(H[:, k, q * 128:(q + 1) * 128], WR[:, k, :]) for k in range(8)],
                      b.free, t_r, t_h)
        LG = small(4 * 36).rearrange("p (k n) -> p k n", k=4)
        rb = par("rb").unsqueeze(1).broadcast_to([128, 4, 36])
        t_lg = tt(LG, b.ap[:, 0:144].rearrange("p (k n) -> p k n", k=4), rb, ADD, tok)
        banks.put(b, t_lg)
        L8 = small(32).rearrange("p (k n) -> p k n", k=4)
        t1 = DVE.do(lambda: v.memset(L8, -BIG), t_lg)
        t_l8 = vcopy(L8[:, :, 0:4], LG[:, :, 0:4], t1)
        M8, E8, V8, WI, NM, SM, EX, ND, W0, W1, OG, I8f, J8f = (
            small(32).rearrange("p (k n) -> p k n", k=4) for _ in range(13))
        UI = small(32).bitcast(u32).rearrange("p (k n) -> p k n", k=4)
        UJ = small(32).bitcast(u32).rearrange("p (k n) -> p k n", k=4)
        iota = cst("iota")
        R4 = range(4)

        def each(f, *after):
            return [f(q) for q in R4]

        ta = [DVE.do(lambda q=q: v.max(M8[:, q, :], L8[:, q, :]), t_l8) for q in R4]
        tb = [DVE.do(lambda q=q: v.max_index(UI[:, q, :], M8[:, q, :], L8[:, q, :]), ta[q]) for q in R4]
        tc = vcopy(I8f, UI, tb)
        td = ts(NM, M8, -1.0, None, MUL, None, ta)
        tex = [act(EX[:, q, 0:4], L8[:, q, 0:4], ACT.Exp, td, bias=NM[:, q, 0:1], acc=SM[:, q, 0:1]) for q in R4]
        tgw = DVE.do(lambda: v.reciprocal(SM[:, :, 1:2], SM[:, :, 0:1]), tex)
        tog = [ts(OG[:, q, 0:4], iota[:, 0:4], I8f[:, q, 0:1], None, ALU.is_equal, None, tc) for q in R4]
        te = [ts(E8[:, q, :], LG[:, q, 4:12], OG[:, q, 0:1], None, MUL, None, tog) for q in R4]
        for g in range(1, 4):
            te = [stt(E8[:, q, :], LG[:, q, 4 + 8 * g:12 + 8 * g], OG[:, q, g:g + 1], E8[:, q, :], MUL, ADD, te[q]) for q in R4]
        ta = [DVE.do(lambda q=q: v.max(V8[:, q, :], E8[:, q, :]), te[q]) for q in R4]
        tb = [DVE.do(lambda q=q: v.max_index(UJ[:, q, :], V8[:, q, :], E8[:, q, :]), ta[q]) for q in R4]
        tc = vcopy(J8f, UJ, tb)
        td = tt(ND[:, :, 0:1], V8[:, :, 1:2], V8[:, :, 0:1], SUB, ta)
        te = act(ND[:, :, 1:2], ND[:, :, 0:1], ACT.Exp, td)
        tf = ts(ND[:, :, 2:3], ND[:, :, 1:2], 1.0, None, ADD, None, te)
        tg = DVE.do(lambda: v.reciprocal(ND[:, :, 3:4], ND[:, :, 2:3]), tf)
        th = tt(ND[:, :, 4:5], ND[:, :, 3:4], ND[:, :, 1:2], MUL, tg)
        tw0 = [ts(W0[:, q, :], iota[:, 0:8], J8f[:, q, 0:1], ND[:, q, 3:4], ALU.is_equal, MUL, tc, tg) for q in R4]
        tw1 = [ts(W1[:, q, :], iota[:, 0:8], J8f[:, q, 1:2], ND[:, q, 4:5], ALU.is_equal, MUL, th) for q in R4]
        ti = tt(WI, W0, W1, ADD, tw0, tw1)
        ti = [ts(WI[:, q, :], WI[:, q, :], SM[:, q, 1:2], None, MUL, None, ti, tgw) for q in R4]
        OHK = [small(128).rearrange("p (k n) -> p k n", k=4) for _ in range(2)]
        tko = []
        for kk, src in ((0, J8f[:, :, 0:1]), (1, J8f[:, :, 1:2])):
            for q in R4:
                eq = (W0, W1)[kk]
                tko.append(ts(eq[:, q, :], iota[:, 0:8], src[:, q, :], None, ALU.is_equal, None, ti))
        tkk = []
        for kk in range(2):
            for q in R4:
                for g in range(4):
                    tkk.append(ts(OHK[kk][:, q, 8 * g:8 * g + 8], (W0, W1)[kk][:, q, :], OG[:, q, g:g + 1], None, MUL, None, tko))
        WK = small(8).rearrange("p (k q) -> p k q", k=2)
        twk = [tt(WK[:, kk, :], ND[:, :, 3 + kk], SM[:, :, 1], MUL, tgw, th) for kk in range(2)]
        MI = small(128).rearrange("p (k n) -> p k n", k=4)
        tmi = tt(MI, OHK[0], OHK[1], ADD, tkk)
        b = banks.get()
        PE.wait(b.free)
        for q in R4:
            mms(b.ap[:, q * 32:(q + 1) * 32], [(ones, MI[:, qq, :]) for qq in range(q)] + [(cst("smask"), MI[:, q, :])], tmi)
        tok = mms(b.ap[:, 128:160], [(ones, MI[:, qq, :]) for qq in R4])
        RK, NE = small(128).rearrange("p (k n) -> p k n", k=4), small(32)
        OVF, CUM, AA, SL, TL, PO, IX = small(32), small(32), *(small(128).rearrange("p (k n) -> p k n", k=4) for _ in range(5))
        t1 = vcopy(RK, b.ap[:, 0:128].rearrange("p (k n) -> p k n", k=4), tok)
        t2 = vcopy(NE, b.ap[:, 128:160], tok)
        banks.put(b, t1, t2)
        t3 = ts(OVF, NE, 128.5, None, ALU.is_gt, None, t2)
        t3 = stt(OVF, NE, 256.5, OVF, ALU.is_gt, ADD, t3)
        t3 = stt(OVF, NE, 384.5, OVF, ALU.is_gt, ADD, t3)
        t4 = DVE.do(lambda: v.tensor_tensor_scan(out=CUM, data0=ones[:, 0:32], data1=OVF, initial=0.0, op0=MUL, op1=ADD), t3)
        EI = small(7 * 32).rearrange("p (o n) -> p o n", o=7)
        EF, EU = small(8), small(8).bitcast(u32)
        t5 = tt(EI, CUM.unsqueeze(1).broadcast_to([128, 7, 32]), iota[:, 0:7].unsqueeze(2).broadcast_to([128, 7, 32]), ALU.is_le, t4)
        t5 = DVE.do(lambda: v.tensor_reduce(out=EF[:, 0:7], in_=EI, axis=AX.X, op=ADD), t5)
        t5 = ts(EF[:, 0:7], EF[:, 0:7], 31.0, None, ALU.min, None, t5)
        t_ei = vcopy(EU[:, 0:7], EF[:, 0:7], t5)
        t6 = ts(AA, RK, 127.5, None, ALU.is_gt, None, t1)
        t7 = ts(IX, RK, 127.5, None, ALU.is_gt, None, t1)
        t6 = stt(AA, RK, 255.5, AA, ALU.is_gt, ADD, t6)
        t6 = stt(AA, RK, 383.5, AA, ALU.is_gt, ADD, t6)
        t8 = stt(SL, AA, -128.0, RK, MUL, ADD, t6)
        t9 = tt(CUM, CUM, OVF, SUB, t5)
        t9 = stt(CUM, CUM, 31.0, iota[:, 0:32], ADD, SUB, t9)
        t9 = tt(TL, AA, CUM.unsqueeze(1).broadcast_to([128, 4, 32]), ADD, t9)
        t9 = tt(TL, TL, IX, MUL, t9, t7)
        t9 = tt(TL, TL, iota[:, 0:32].unsqueeze(1).broadcast_to([128, 4, 32]), ADD, t9)
        t10 = stt(PO, TL, 128.0, SL, MUL, ADD, t9, t8)
        t11 = stt(IX, SL, float(NT), TL, MUL, ADD, t9)
        PF, PU = small(16), small(16).bitcast(u32)
        tmpk = AA
        tl = t11
        for n_, (kk, src) in enumerate(((0, PO), (1, PO), (0, IX), (1, IX))):
            tl = tt(tmpk, OHK[kk], src, MUL, tl, t10)
            tl = DVE.do(lambda n_=n_: v.tensor_reduce(out=PF[:, 4 * n_:4 * n_ + 4], in_=tmpk, axis=AX.X, op=ADD), tl)
        t_pu = vcopy(PU, PF, tl)
        LST = small(40).bitcast(u32)[:, 0:NT]
        d_l, d_g, d_sc = dsem("d_l"), dsem("d_g"), dsem("d_sc")
        t_z = DVE.do(lambda: v.memset(LST, 0), t_pu)
        t_z = dma(GP, nc.gpsimd, d_l, Ld.rearrange("(p n) o -> p (n o)", p=128), LST, t_z)
        GP.wait(t_z, t_tid)
        for n_ in range(8):
            kk, q = n_ // 4, n_ % 4
            t_sc_ = dma_call(GP, d_sc, lambda kk=kk, q=q: nc.gpsimd.indirect_dma_start(
                out=Ld, out_offset=bass.IndirectOffsetOnAxis(ap=PU[:, 8 + 4 * kk + q:9 + 4 * kk + q], axis=0),
                in_=TID[:, q:q + 1], in_offset=None))
        t_lst = dma(GP, nc.gpsimd, d_l, LST, Ld.rearrange("(p n) o -> p (n o)", p=128), t_sc_)
        assert base[0] <= 8 * S

        HT = tiles(8, 8).rearrange("p (q c) n -> p q (c n)", q=4)
        d_ht = dsem("d_ht")
        for q in R4:
            tcp = []
            for c in range(2):
                b = banks.get()
                PE.wait(b.free)
                for i in range(4):
                    tok = transpose(b.ap[:, i * 128:(i + 1) * 128], H[:, 4 * c + i, q * 128:(q + 1) * 128], t_h, sig=i == 3)
                tcp.append(act(HT[:, q, c * 512:(c + 1) * 512], b.ap, ACT.Copy, tok))
                banks.put(b, tcp[-1])
            t_hd = dma(SC, nc.scalar, d_ht, Hd[q * 128:(q + 1) * 128, :], HT[:, q, :], tcp)

        t_ct = ada()

        GX = Pool([Place(reg(16 + 2 * i, 2), sem(f"s_gx{i}")) for i in range(3)])
        XTP = Pool([Place(reg(22 + 2 * i, 2).rearrange("p (k n) -> p k n", k=8)) for i in range(2)])
        SGP = Pool([Place(reg(26 + i, 1)) for i in range(2)])
        AVP = Pool([Place(reg(28 + i, 1)[:, 0:256].rearrange("p (k n) -> p k n", k=2)) for i in range(2)])
        YSP = Pool([Place(reg(30 + 2 * i, 2), sem(f"s_ys{i}")) for i in range(3)])
        eid = {}

        def expert(name, e):
            if e < 32:
                return lambda: A[name][e]
            return lambda: A[name][bass.ds(eid[e], 1)].rearrange("a d f -> (a d) f")

        def load_expert(i):
            if i >= 32:
                SP.wait(t_ei)

                def read():
                    eid[i] = nc.sync.value_load(EU[0:1, i - 32:i - 31], min_val=0, max_val=31)
                SP.items.append((read, None, 0))
            s = slots.get()
            for lo, name in ((0, "w_gate"), (256, "w_up")):
                src = expert(name, i)
                s.ready = dma_call(SP, s.counter, lambda s=s, lo=lo, src=src: nc.sync.dma_start(
                    k8(s.ap)[:, :, lo:lo + 256], src().rearrange("(k p) n -> p k n", p=128)), s.free)
            return s

        def load_down(i):
            s = slots.get()
            n = 2 if i < 31 else 1
            for j in range(n):
                src = expert("w_down", i + j)
                s.ready = dma_call(SP, s.counter, lambda s=s, j=j, src=src: nc.sync.dma_start(
                    s.ap[:, 2048 * j:2048 * j + 2048].rearrange("p (k n) -> p k n", k=2), src().rearrange("(k p) n -> p k n", p=128)), s.free)
            return s

        def tile_in(i):
            g = GX.get()
            tg = dma_call(GP, g.counter, lambda g=g, i=i: nc.gpsimd.indirect_dma_start(
                out=g.ap, out_offset=None, in_=Hd, in_offset=bass.IndirectOffsetOnAxis(ap=LST[:, i:i + 1], axis=0)),
                g.free, t_lst, t_hd)
            x = XTP.get()
            toks = []
            for c in range(2):
                b = banks.get()
                PE.wait(b.free, tg)
                for k in range(4):
                    tok = transpose(b.ap[:, k * 128:(k + 1) * 128], g.ap[:, (4 * c + k) * 128:(4 * c + k + 1) * 128], sig=k == 3)
                bv = b.ap.rearrange("p (k n) -> p k n", k=4)
                if c:
                    toks.append(vcopy(x.ap[:, 4 * c:4 * c + 4, :], bv, tok, x.free))
                else:
                    toks.append(act(x.ap[:, 4 * c:4 * c + 4, :], bv, ACT.Copy, tok, x.free))
                banks.put(b, toks[-1])
            GX.put(g, tok)
            return x, toks

        def tile_up(i, x, ready):
            s = load_expert(i)
            w = k8(s.ap)
            b = banks.get()
            tok = mms(b.ap, [(x.ap[:, k, :], w[:, k, :]) for k in range(8)], b.free, s.ready, ready)
            slots.put(s, tok)
            XTP.put(x, tok)
            g = SGP.get()
            t1 = act(g.ap[:, 0:256], b.ap[:, 0:256], ACT.Silu, tok, g.free)
            t2 = tt(g.ap[:, 256:512], g.ap[:, 0:256], b.ap[:, 256:512], MUL, t1, g.free)
            banks.put(b, t2)
            return g, t2

        def tile_mid(g, t2):
            b = banks.get()
            PE.wait(b.free, t2)
            for k in range(2):
                tok = transpose(b.ap[:, k * 128:(k + 1) * 128], g.ap[:, 256 + k * 128:384 + k * 128], sig=k == 1)
            SGP.put(g, tok)
            av = AVP.get()
            t3 = vcopy(av.ap, b.ap[:, 0:256].rearrange("p (k n) -> p k n", k=2), tok, av.free)
            banks.put(b, t3)
            return av, t3

        def tile_down(i, av, t3):
            if i >= 32 or i % 2 == 0:
                down[0] = load_down(i)
            s = down[0]
            o = 2048 * (i % 2) if i < 32 else 0
            w = s.ap[:, o:o + 2048].rearrange("p (k n) -> p k n", k=2)
            y = YSP.get()
            toks = []
            for c in range(2):
                b = banks.get()
                tok = mms(b.ap, [(av.ap[:, k, :], w[:, k, c * 512:(c + 1) * 512]) for k in range(2)], b.free, s.ready, t3)
                if c:
                    toks.append(vcopy(y.ap[:, 512:1024], b.ap, tok, y.free))
                else:
                    toks.append(act(y.ap[:, 0:512], b.ap, ACT.Copy, tok, y.free))
                banks.put(b, toks[-1])
            AVP.put(av, tok)
            if i >= 31 or i % 2 == 1:
                slots.put(s, tok)
            ty = dma(SC, nc.scalar, y.counter, Yd[i * 128:(i + 1) * 128, :], y.ap, toks)
            YSP.put(y, ty)
            return ty

        down = [None]
        ins = {0: tile_in(0), 1: tile_in(1)}
        ups = {0: tile_up(0, *ins.pop(0))}
        for i in range(NT):
            if i + 2 < NT:
                ins[i + 2] = tile_in(i + 2)
            mid = tile_mid(*ups.pop(i))
            if i + 1 < NT:
                ups[i + 1] = tile_up(i + 1, *ins.pop(i + 1))
            tile_down(i, *mid)
        t_yd = [p_.free for p_ in YSP.q]

        for q in R4:
            g0, g1 = GX.get(), GX.get()
            for kk, g in ((0, g0), (1, g1)):
                g.ready = dma_call(GP, g.counter, lambda g=g, kk=kk, q=q: nc.gpsimd.indirect_dma_start(
                    out=g.ap, out_offset=None, in_=Yd, in_offset=bass.IndirectOffsetOnAxis(ap=PU[:, 4 * kk + q:4 * kk + q + 1], axis=0)),
                    g.free, t_yd, t_pu)
            t1 = ts(g0.ap, g0.ap, WK[:, 0, q:q + 1], None, MUL, None, g0.ready, twk)
            t2 = stt(g0.ap, g1.ap, WK[:, 1, q:q + 1], g0.ap, MUL, ADD, t1, g1.ready)
            GX.put(g1, t2)
            for c in range(2):
                b = banks.get()
                PE.wait(b.free, t2)
                for k in range(4):
                    tok = transpose(b.ap[:, k * 128:(k + 1) * 128], g0.ap[:, (4 * c + k) * 128:(4 * c + k + 1) * 128], sig=k == 3)
                xs = X[:, 4 * c:4 * c + 4, q * 128:(q + 1) * 128]
                t_x = tt(xs, xs, b.ap.rearrange("p (k n) -> p k n", k=4), ADD, tok)
                banks.put(b, t_x)
            GX.put(g0, tok)

        def modulated(src, dst, n, gain, shift, *after):
            r, tr = factor([src[:, k, :] for k in range(8)], ones, 1.0 / D, n, *after)
            for k in range(8):
                t1 = stt(dst[:, k, :], src[:, k, :], gain(k), r, MUL, MUL, tr)
                t2 = ts(dst[:, k, :], dst[:, k, :], shift(k), None, ADD, None, t1)
            last_r[0] = t1
            return t2

        t_h = modulated(X, H, S, lambda k: G2[:, k:k + 1], lambda k: MOD[:, k, 0:1], t_x, t_g2)
        CX = reg(1, 4).rearrange("p (k n) -> p k n", k=8)
        HC = reg(5, 4).rearrange("p (k n) -> p k n", k=8)
        d_cx = dsem("d_cx")
        t_cx = dma(SC, nc.scalar, d_cx, CX, A["ctx"].rearrange("(k p) n -> p k n", p=128), t_x, t_ct)
        t_hc = modulated(CX, HC, 256, lambda k: G2[:, 8 + k:9 + k], lambda k: MOD[:, k, 1:2], t_cx, t_g2)

        w2 = A["w_in_2"]
        KK = reg(9, 2)[:, 0:768]
        VV = reg(11, 2)[:, 0:768].rearrange("p (k n) -> p k n", n=128)
        QQ = tiles(13, 4)
        COS, SIN = reg(17, 1), reg(18, 1)
        d_cs = dsem("d_cs")
        dma(SC, nc.scalar, d_cs, COS, A["rope"][0], t_x)
        t_cs = dma(SC, nc.scalar, d_cs, SIN, A["rope"][1], t_x)
        s = load_cols(w2, 4096, 4352)
        w = s.ap[:, 0:2048].rearrange("p (k n) -> p k n", k=8)

        def head_norm2(dst, b, tok, n, gain, rope):
            t0 = act(dst, b.ap[:, 0:n], ACT.Copy, tok)
            banks.put(b, t0)
            r, tr = factor([dst], blk, 1.0 / 64, n, t0)
            t1 = stt(dst, dst, gain, r, MUL, MUL, tr)
            last_r[0] = t1
            if rope:
                br = banks.get()
                tok = mms(br.ap, [(cst("rot"), dst)], br.free, t1)
                rt = tmp[0]
                t2 = tt(rt, br.ap, SIN, MUL, tok, t_cs, factor_sq[0])
                banks.put(br, t2)
                t3 = tt(dst, dst, COS, MUL, t2)
                t1 = tt(dst, dst, rt, ADD, t3)
                factor_sq[0] = t1
            return t1

        b = banks.get()
        tok = mms(b.ap, [(w[:, k, 0:128], H[:, k, :]) for k in range(8)], b.free, s.ready, t_h)
        t_k1 = head_norm2(KK[:, 0:512], b, tok, 512, par("kg2", 0), True)
        b = banks.get()
        tok = mms(b.ap[:, 0:256], [(w[:, k, 0:128], HC[:, k, :]) for k in range(8)], b.free, t_hc)
        t_k2 = head_norm2(KK[:, 512:768], b, tok, 256, par("kg2", 0), False)
        t_kk = [t_k1, t_k2]
        b = banks.get()
        b2 = banks.get()
        PE.wait(b.free, b2.free)
        for c in range(4):
            tok = mms(b.ap[:, c * 128:(c + 1) * 128], [(H[:, k, c * 128:(c + 1) * 128], w[:, k, 128:256]) for k in range(8)])
        for c in range(2):
            tok = mms(b2.ap[:, c * 128:(c + 1) * 128], [(HC[:, k, c * 128:(c + 1) * 128], w[:, k, 128:256]) for k in range(8)])
        slots.put(s, tok)
        t1 = act(VV[:, 0:4, :], b.ap.rearrange("p (k n) -> p k n", n=128), ACT.Copy, tok)
        t_vv = act(VV[:, 4:6, :], b2.ap[:, 0:256].rearrange("p (k n) -> p k n", n=128), ACT.Copy, tok)
        banks.put(b, t1)
        banks.put(b2, t_vv)
        t_qq = [None] * 4
        s = load_cols(w2, 1536, 2048)
        held = [proj(s, c, t_h) for c in range(4)]
        slots.put(s, held[-1][1])
        for c in range(4):
            t_qq[c] = head_norm2(QQ[:, c, :], *held[c], 512, par("qg2", 0), True)

        A2 = tiles(1, 4)
        PR = [reg(5, 2)[:, 0:768], reg(7, 2)[:, 0:768]]
        PT = reg(19, 6).rearrange("p (k n) -> p k n", k=6)
        STT = reg(25, 1)
        t_a2 = [None] * 8

        def attention2():
            pt_free = None
            pr_free = [None, None]
            it = 0
            for j in range(4):
                for g in range(2):
                    po = 64 * g
                    h = j * 2 + g
                    ready = []
                    for q in range(4):
                        c = (it % 2) * 8
                        st = lambda i, c=c: STT[:, c + i:c + i + 1]
                        Pb = PR[it % 2]
                        lq = QQ[po:po + 64, j, q * 128:(q + 1) * 128]
                        ba, bb = banks.get(), banks.get()
                        PE.wait(ba.free, bb.free)
                        t0 = mms(ba.ap, [(lq, KK[po:po + 64, 0:512])], t_qq[j], t_kk)
                        t1 = mms(bb.ap[:, 0:256], [(lq, KK[po:po + 64, 512:768])])
                        m0 = DVE.do(lambda st=st, ba=ba: v.tensor_reduce(out=st(0), in_=ba.ap, axis=AX.X, op=ALU.max), t0, pr_free[it % 2])
                        m1 = DVE.do(lambda st=st, bb=bb: v.tensor_reduce(out=st(1), in_=bb.ap[:, 0:256], axis=AX.X, op=ALU.max), t1)
                        m2 = tt(st(2), st(0), st(1), ALU.max, m0, m1)
                        m3 = ts(st(3), st(2), -0.125, None, MUL, None, m2)
                        e0 = act(Pb[:, 0:512], ba.ap, ACT.Exp, m3, pr_free[it % 2], t_hc, bias=st(3), scale=0.125, acc=st(4))
                        e1 = act(Pb[:, 512:768], bb.ap[:, 0:256], ACT.Exp, m3, bias=st(3), scale=0.125, acc=st(5))
                        banks.put(ba, e0)
                        banks.put(bb, e1)
                        m4 = tt(st(6), st(4), st(5), ADD, e0, e1)
                        m5 = DVE.do(lambda st=st: v.reciprocal(st(7), st(6)), m4)
                        m6 = ts(Pb, Pb, st(7), None, MUL, None, m5)
                        yield
                        ba, bb = banks.get(), banks.get()
                        PE.wait(ba.free, bb.free, m6)
                        for i in range(6):
                            o = (ba, bb)[i // 4].ap[:, (i % 4) * 128:(i % 4) * 128 + 128]
                            tok = transpose(o, Pb[:, i * 128:(i + 1) * 128], sig=i == 5)
                        pr_free[it % 2] = tok
                        r0 = act(PT[:, 0:4, q * 128:(q + 1) * 128], ba.ap.rearrange("p (k n) -> p k n", k=4), ACT.Copy, tok, pt_free)
                        r1 = vcopy(PT[:, 4:6, q * 128:(q + 1) * 128], bb.ap[:, 0:256].rearrange("p (k n) -> p k n", k=2), tok, pt_free)
                        banks.put(ba, r0)
                        banks.put(bb, r1)
                        ready += [r0, r1]
                        it += 1
                        yield
                    b = banks.get()
                    pt_free = mms(b.ap[po:po + 64, :], [(VV[:, i, po:po + 64], PT[:, i, :]) for i in range(6)], b.free, ready, t_vv)
                    t_a2[h] = act(A2[po:po + 64, j, :], b.ap[po:po + 64, :], ACT.Copy, pt_free, t_hc)
                    banks.put(b, t_a2[h])

        KF = tiles(26, 18)
        SB_, DB_ = tiles(10, 4), tiles(14, 4)
        DEC = None

        drain(attention2())
        PE_att = t_a2
        HM = reg(5, 1)
        FW = reg(19, 7)
        ZF, FW1, FW2, FW3, FW4, SKB = FW[:, 0:512], FW[:, 512:576], FW[:, 576:640], FW[:, 640:704], FW[:, 768:2816], FW[:, 2816 - 256:3584]
        SKB = reg(8, 2)
        d_f = dsem("d_f")
        dma(SP, nc.sync, d_f, ZF[0:33, :], A["zf"], t_a2, pt_last := PE.last())
        dma(SP, nc.sync, d_f, FW1[0:33, :], A["hf_w1"])
        dma(SP, nc.sync, d_f, FW2[0:64, :], A["hf_w2"])
        dma(SP, nc.sync, d_f, FW3[0:64, :], A["hf_w3"])
        dma(SP, nc.sync, d_f, FW4[0:64, :], A["hf_w4"])
        t_f = dma(SP, nc.sync, d_f, SKB, A["skip"])
        s_f1 = load([(0, 4096, lambda ap: ap.rearrange("p (t k n) -> p t k n", t=2, k=4), A["dft"][0:2].rearrange("t (k p) n -> p t k n", p=128))])
        s_f2 = load([(0, 4096, lambda ap: ap.rearrange("p (t k n) -> p t k n", t=2, k=4), A["dft"][2:4].rearrange("t (k p) n -> p t k n", p=128))])
        FC, FS = k4(s_f1.ap[:, 0:2048]), k4(s_f1.ap[:, 2048:4096])
        FST, DEC = k4(s_f2.ap[:, 0:2048]), k4(s_f2.ap[:, 2048:4096])
        MAGIC = 12582912.0
        C1, C2 = 6.28125, 2.0 * math.pi - 6.28125
        C2h = float(np.float32(np.round(C2 * 2 ** 21) / 2 ** 21))
        C3 = 2.0 * math.pi - C1 - C2h
        src, tok_s = ZF[0:33, :], t_f
        last_act = t_a2
        for li, (w, kk, bn) in enumerate(((FW1, 33, "hb1"), (FW2, 64, "hb2"), (FW3, 64, "hb3"))):
            b = banks.get()
            tok = mms(b.ap[0:64, :], [(w[0:kk, :], src)], b.free, t_f, tok_s)
            u, n_ = tmp[2][0:64, :], tmp[3][0:64, :]
            t1 = ts(u, b.ap[0:64, :], par(bn, 0)[0:64, :], par("hfr", 0)[0:64, :], ADD, MUL, tok, last_r[0])
            banks.put(b, t1)
            t2 = ts(n_, u, 1.0 / (2.0 * math.pi), MAGIC, MUL, ADD, t1)
            t3 = ts(n_, n_, -MAGIC, None, ADD, None, t2)
            t4 = stt(u, n_, -C1, u, MUL, ADD, t3)
            t5 = stt(u, n_, -C2h, u, MUL, ADD, t4)
            t6 = stt(u, n_, -C3, u, MUL, ADD, t5)
            t7 = ts(u, u, 3.1415925, -3.1415925, ALU.min, ALU.max, t6)
            hm = HM[0:64, :]
            tok_s = act(hm, u, ACT.Sin, t7, tok, t_a2)
            src = hm
        last_r[0] = t7
        t_hm = tok_s
        kf_tok = []
        sb_free = None
        for o in range(2):
            td = [None] * 4
            for c in range(4):
                bf, bb = banks.get(), banks.get()
                lh = HM[0:64, c * 128:(c + 1) * 128]
                t0 = mms(bf.ap, [(lh, FW4[0:64, o * 1024:o * 1024 + 512])], bf.free, t_hm)
                t1 = mms(bb.ap, [(lh, FW4[0:64, o * 1024 + 512:o * 1024 + 1024])], bb.free)
                fw, bw = SB_[:, c, :], DB_[:, c, :]
                t2 = tt(fw, bf.ap, DEC[:, c, :], MUL, t0, s_f2.ready, sb_free, t_hm)
                t3 = tt(bw, bb.ap, DEC[:, c, :], MUL, t1, sb_free)
                banks.put(bf, t2)
                banks.put(bb, t3)
                if c == 0:
                    t3 = DVE.do(lambda bw=bw: v.memset(bw[0:1, :], 0.0), t3)
                td[c] = [t2, t3]
            b = banks.get()
            PE.wait(b.free)
            nn = 0
            for c in range(4):
                for x in (SB_, DB_):
                    ab = tmp[nn % 2]
                    tk = act(ab, x[:, c, :], ACT.Abs, td[c], factor_sq[nn % 2])
                    factor_sq[nn % 2] = tok = PE.do(lambda ab=ab, nn=nn, b=b: t.matmul(b.ap, ones, ab, start=nn == 0, stop=nn == 7), tk)
                    nn += 1
            inv = tmp[2]
            t1 = ts(tmp[3], b.ap, EPS, None, ADD, None, tok, last_r[0])
            banks.put(b, t1)
            t_inv = DVE.do(lambda: v.reciprocal(tmp[2], tmp[3]), t1)
            last_r[0] = t_inv
            tsd = []
            for c in range(4):
                df = tmp[4]
                t1 = tt(df, SB_[:, c, :], DB_[:, c, :], SUB, td[c], tk, tsd[-1] if tsd else last_r[0])
                t2 = tt(SB_[:, c, :], SB_[:, c, :], DB_[:, c, :], ADD, t1, tk)
                t3 = vcopy(DB_[:, c, :], df, t2)
                tsd.append(t3)
            kc0 = 9 * o
            skip = SKB[:, o * 512:(o + 1) * 512]
            for f in range(4):
                b = banks.get()
                tok = mms(b.ap, [(FC[:, k, f * 128:(f + 1) * 128], SB_[:, k, :]) for k in range(4)], b.free, tsd, s_f1.ready)
                kc = KF[:, kc0 + f, :]
                t1 = tt(kc, b.ap, inv, MUL, tok, t_inv)
                banks.put(b, t1)
                t2 = tt(kc, kc, skip, ADD, t1)
                t3 = ts(kc, kc, 2.0 / 1024, None, MUL, None, t2)
                kf_tok.append(t3)
                b = banks.get()
                tok = mms(b.ap, [(FS[:, k, f * 128:(f + 1) * 128], DB_[:, k, :]) for k in range(4)], b.free)
                ks = KF[:, kc0 + 4 + f, :]
                t4 = tt(ks, b.ap, inv, MUL, tok)
                banks.put(b, t4)
                t5 = ts(ks, ks, 2.0 / 1024, None, MUL, None, t4)
                kf_tok.append(t5)
                if f == 0:
                    b = banks.get()
                    tok = mms(b.ap, [(FS[:, k, 0:128], SB_[:, k, :]) for k in range(4)], b.free)
                    kx = KF[:, kc0 + 8, :]
                    t6 = vcopy(kx, kc, t3)
                    t7 = ts(kc[0:1, :], kc[0:1, :], 0.5, None, MUL, None, t6)
                    t8 = DVE.do(lambda ks=ks: v.memset(ks[0:1, :], 0.0), t5)
                    t9 = tt(kx[0:1, :], b.ap[0:1, :], inv[0:1, :], MUL, tok, t6)
                    banks.put(b, t9)
                    t9 = tt(kx[0:1, :], kx[0:1, :], skip[0:1, :], ADD, t9)
                    t9 = ts(kx[0:1, :], kx[0:1, :], 1.0 / 1024, None, MUL, None, t9)
                    kf_tok += [t7, t8, t9]
            sb_free = tok
            last_r[0] = t5

        VF, X1, X2 = tiles(10, 4), tiles(14, 4), tiles(22, 4)
        UT, YC, YS = tiles(18, 4), tiles(5, 4), tiles(22, 4)

        def short(dst, c, tile, b, tok, *after):
            w = lambda j: par("hcw", j * 12 + c)
            raw = tmp[c % 2]
            t0 = act(raw, b.ap, ACT.Copy, tok, factor_sq[c % 2])
            banks.put(b, t0)
            t1 = ts(dst, raw, w(1), par("hcb", c), MUL, ADD, t0, *after)
            t2 = stt(dst[:, 1:S], raw[:, 0:S - 1], w(0), dst[:, 1:S], MUL, ADD, t1)
            t3 = stt(dst[:, 0:S - 1], raw[:, 1:S], w(2), dst[:, 0:S - 1], MUL, ADD, t2)
            factor_sq[c % 2] = t3
            return t3

        def hy_part(dst, i, *after):
            s = load_cols(w2, i * 512, i * 512 + 512)
            toks = []
            for c in range(4):
                b, tok = proj(s, c, t_h)
                toks.append(short(dst[:, c, :], i * 4 + c, c, b, tok, *after))
            slots.put(s, tok)
            return toks

        def to_tokens(dst, src, ready, *after):
            toks = []
            for q in range(4):
                b = banks.get()
                PE.wait(b.free, ready)
                for c in range(4):
                    tok = transpose(b.ap[:, c * 128:(c + 1) * 128], src[:, c, q * 128:(q + 1) * 128], sig=c == 3)
                toks.append(act(dst[:, q, :], b.ap, ACT.Copy, tok, *after))
                banks.put(b, toks[-1])
            return toks, tok

        def spectrum(U, ready, o, *after):
            toks = []
            for f in range(4):
                bc, bs = banks.get(), banks.get()
                tc_ = mms(bc.ap, [(FC[:, k, f * 128:(f + 1) * 128], U[:, k, :]) for k in range(4)], bc.free, ready)
                ts_ = mms(bs.ap, [(FS[:, k, f * 128:(f + 1) * 128], U[:, k, :]) for k in range(4)], bs.free)
                kc, ks = KF[:, 9 * o + f, :], KF[:, 9 * o + 4 + f, :]
                kx = KF[:, 9 * o + 8, :] if f == 0 else kc
                yc, ys, p = YC[:, f, :], YS[:, f, :], tmp[4]
                t1 = tt(yc, bc.ap, kc, MUL, tc_, kf_tok, *after)
                t2 = tt(p, bs.ap, ks, MUL, ts_, last_p[0])
                t3 = tt(yc, yc, p, SUB, t1, t2)
                t4 = tt(ys, bc.ap, ks, MUL, t3)
                t5 = tt(p, bs.ap, kx, MUL, t4)
                banks.put(bc, t4)
                banks.put(bs, t5)
                t6 = tt(ys, ys, p, ADD, t5)
                last_p[0] = t6
                toks += [t3, t6]
            return toks, ts_

        last_p = [last_r[0]]
        t_vf = hy_part(VF, 0, sb_free)
        t_x1 = hy_part(X1, 1, sb_free)
        t_ut, _ = to_tokens(UT, VF, t_vf, sb_free)
        t_y, t_u_free = spectrum(UT, t_ut, 0, sb_free)
        t_x1t, t_x1free = to_tokens(VF, X1, t_x1, t_ut[-1])
        t_y1 = []
        for q in range(4):
            b = banks.get()
            tok = mms(b.ap, [(FC[:, k, q * 128:(q + 1) * 128], YC[:, k, :]) for k in range(4)] +
                      [(FST[:, k, q * 128:(q + 1) * 128], YS[:, k, :]) for k in range(4)], b.free, t_y)
            t1 = tt(UT[:, q, :], b.ap, VF[:, q, :], MUL, tok, t_x1t, t_u_free)
            banks.put(b, t1)
            t_y1.append(t1)
        t_inv0 = tok
        t_y, t_u_free = spectrum(UT, t_y1, 1, t_inv0)
        t_x2 = hy_part(X1, 2, t_x1free)
        HY = X1
        t_hy = []
        for c in range(4):
            b = banks.get()
            tok = mms(b.ap, [(YC[:, k, c * 128:(c + 1) * 128], FC[:, k, :]) for k in range(4)] +
                      [(YS[:, k, c * 128:(c + 1) * 128], FST[:, k, :]) for k in range(4)], b.free, t_y)
            t1 = tt(HY[:, c, :], HY[:, c, :], b.ap, MUL, tok, t_x2[c])
            banks.put(b, t1)
            t_hy.append(t1)
        slots.put(s_f1, tok)
        slots.put(s_f2, tok)

        GA2, GB2 = tiles(18, 8), tiles(26, 8)
        t_ga2, t_gb2 = [None] * 8, [None] * 8
        drain(gates(GA2, w2, 2048, t_ga2, tok, t_hy))
        drain(gates(GB2, w2, 3072, t_gb2))
        t_m = merge(A["w_attn"], A["w_hy"], A2, HY, t_a2, t_hy, t_ga2, t_gb2, GA2, GB2)
        t_x = out_proj(A["w_out_2"], GA2, t_m,
                       lambda c, b, tok: stt(X[:, c, :], b.ap, MOD[:, 16 + c, 0:1], X[:, c, :], MUL, ADD, tok))
        t_h = modulated(X, H, S, lambda k: GF2[:, k:k + 1], lambda k: MOD[:, 24 + k, 0:1], t_x)

        QP = tiles(1, 16)
        t_qp = [None] * 16
        for i in range(4):
            s = load_cols(A["wq"], i * 512, i * 512 + 512)
            for c in range(4):
                b, tok = proj(s, c, t_h)
                t_qp[i * 4 + c] = act(QP[:, i * 4 + c, :], b.ap, ACT.Copy, tok, t_x)
                banks.put(b, t_qp[i * 4 + c])
            slots.put(s, tok)
        KEY = TMP[:, 0:2048].rearrange("p (i n) -> p i n", i=16)
        t_key = dma(SP, nc.sync, dsem("d_key"), KEY, A["keys"].rearrange("p (i n) -> p i n", i=16), t_h, DVE.last(), PE.last())
        t_ring = PE.last()
        ring.close()
        HR = [sb(f"hr{i}", 8 * S, f32r, None, "right")[:, :].rearrange("p (k n) -> p k n", k=8) for i in range(2)]
        raw = Pool([Place(sb(f"raw{i}", 2048, f32, None, "right")[:, :], sem(f"s_rw{i}")) for i in range(3)])
        for p_ in raw.q:
            p_.free = [t_ring]
        t_hr = [split(HR[0][:, k, :], HR[1][:, k, :], H[:, k, :], t_ring, t_h) for k in range(8)]
        SC1, SC2 = reg(17, 4).rearrange("p (i n) -> p i n", i=16), reg(21, 4).rearrange("p (i n) -> p i n", i=16)
        CD1, CD2 = reg(25, 4).rearrange("p (h k j) -> p h k j", h=8, k=16), reg(29, 4).rearrange("p (h k j) -> p h k j", h=8, k=16)
        EQ = reg(33, 4).rearrange("p (h k j) -> p h k j", h=8, k=16)
        SMALL = reg(37, 6)
        VAL = SMALL[:, 0:256].rearrange("p (i k) -> p i k", i=16)
        IDX = SMALL[:, 256:512].bitcast(u32).rearrange("p (i k) -> p i k", i=16)
        IDF = SMALL[:, 512:768].rearrange("p (i k) -> p i k", i=16)
        BST = SMALL[:, 768:896].rearrange("p (h k) -> p h k", h=8)
        POS = SMALL[:, 896:1024].bitcast(u32).rearrange("p (h k) -> p h k", h=8)
        PHI = SMALL[:, 1024:1152].bitcast(u32).rearrange("p (h k) -> p h k", h=8)
        PLO = SMALL[:, 1152:1280].bitcast(u32).rearrange("p (h k) -> p h k", h=8)
        PHF = SMALL[:, 1280:1408].rearrange("p (h k) -> p h k", h=8)
        PLF = SMALL[:, 1408:1536].rearrange("p (h k) -> p h k", h=8)
        I1 = SMALL[:, 1536:1664].rearrange("p (h k) -> p h k", h=8)
        I2 = SMALL[:, 1664:1792].rearrange("p (h k) -> p h k", h=8)
        GW = SMALL[:, 1792:1920].rearrange("p (h k) -> p h k", h=8)
        GS = SMALL[:, 1920:1928]
        GR = SMALL[:, 1928:1936]
        I1T, I2T = (reg(43, 1).bitcast(bf16)[:, i * 512:(i + 1) * 512] for i in range(2))
        GT = [reg(44, 2).bitcast(bf16)[:, i * 512:(i + 1) * 512] for i in range(3)]
        IT = [I1, I2, GW]
        iota16 = iota[:, 0:16].unsqueeze(1).broadcast_to([128, 128, 16])
        t_it = []
        t_s_free = t_tr_free = None
        for q in range(4):
            t_sc = []
            for g in range(4):
                b = banks.get()
                PE.wait(b.free, t_key)
                for i in range(4):
                    ii = g * 4 + i
                    tok = mms(b.ap[:, i * 128:(i + 1) * 128], [(QP[:, ii, q * 128:(q + 1) * 128], KEY[:, ii, :])], t_qp[ii])
                t_sc.append(act(SC1[:, g * 4:g * 4 + 4, :], b.ap.rearrange("p (i n) -> p i n", i=4), ACT.Copy, tok, t_s_free))
                banks.put(b, t_sc[-1])

            def top16(n, src, alt, val, idx, ready, *after):
                ta = [DVE.do(lambda i=i: v.max(val(i)[:, 0:8], src(i)), ready, *after) for i in range(n)]
                tb = [DVE.do(lambda i=i: v.max_index(idx(i)[:, 0:8], val(i)[:, 0:8], src(i)), ta[i]) for i in range(n)]
                tr = [DVE.do(lambda i=i: v.match_replace(alt(i), val(i)[:, 0:8], src(i), -3.0e38), ta[i]) for i in range(n)]
                ta = [DVE.do(lambda i=i: v.max(val(i)[:, 8:16], alt(i)), tr[i]) for i in range(n)]
                tb2 = [DVE.do(lambda i=i: v.max_index(idx(i)[:, 8:16], val(i)[:, 8:16], alt(i)), ta[i]) for i in range(n)]
                return tb2[-1]

            DVE.wait(DVE.last())
            t1 = top16(16, lambda i: SC1[:, i, :], lambda i: SC2[:, i, :], lambda i: VAL[:, i, :], lambda i: IDX[:, i, :], t_sc)
            t_s_free = t1
            t2 = vcopy(IDF, IDX, t1)
            V4 = VAL.rearrange("p (h s) k -> p h s k", s=2)
            F4 = IDF.rearrange("p (h s) k -> p h s k", s=2)
            t3 = None
            for h in range(8):
                t3 = tt(CD1[:, h, :, :], V4[:, h, 0, :].unsqueeze(2).broadcast_to([128, 16, 16]),
                        V4[:, h, 1, :].unsqueeze(1).broadcast_to([128, 16, 16]), ADD, t1)
            fl = lambda ap: ap.rearrange("p k j -> p (k j)")
            t4 = top16(8, lambda h: fl(CD1[:, h, :, :]), lambda h: fl(CD2[:, h, :, :]), lambda h: BST[:, h, :],
                       lambda h: POS[:, h, :], t3)
            t5 = DVE.do(lambda: v.tensor_scalar(out=PHI, in0=POS, scalar1=4, scalar2=None, op0=ALU.logical_shift_right), t4)
            t6 = DVE.do(lambda: v.tensor_scalar(out=PLO, in0=POS, scalar1=15, scalar2=None, op0=ALU.bitwise_and), t4)
            t5 = vcopy(PHF, PHI, t5)
            t6 = vcopy(PLF, PLO, t6)
            t9 = []
            for side, (pf, dst) in enumerate(((PHF, I1), (PLF, I2))):
                pfl = pf.rearrange("p h k -> p (h k)").unsqueeze(2).broadcast_to([128, 128, 16])
                eq = EQ.rearrange("p h k j -> p (h k) j")
                t7 = tt(eq, pfl, iota16, ALU.is_equal, t5, t6, t9[-1] if t9 else None)
                for h in range(8):
                    t8 = tt(EQ[:, h, :, :], EQ[:, h, :, :], F4[:, h, side, :].unsqueeze(1).broadcast_to([128, 16, 16]), MUL, t7, t2)
                t9.append(DVE.do(lambda dst=dst, eq=eq: v.tensor_reduce(out=dst.rearrange("p h k -> p (h k)"), in_=eq, axis=AX.X, op=ADD), t8, t_tr_free))
            u1 = tt(GW, BST, BST[:, :, 0:1].broadcast_to([128, 8, 16]), SUB, t4, t_tr_free)
            u2 = act(GW, GW, ACT.Exp, u1)
            u3 = DVE.do(lambda: v.tensor_reduce(out=GS, in_=GW, axis=AX.X, op=ADD), u2)
            u4 = DVE.do(lambda: v.reciprocal(GR, GS), u3)
            u5 = tt(GW, GW, GR.unsqueeze(2).broadcast_to([128, 8, 16]), MUL, u4)
            b = banks.get()
            PE.wait(b.free, t9, u5)
            for i, src in enumerate(IT):
                tok = transpose(b.ap[:, i * 128:(i + 1) * 128], src.rearrange("p h k -> p (h k)"), sig=i == 2)
            t_tr_free = tok
            qs = slice(q * 128, (q + 1) * 128)
            t_it.append(act(I1T[:, qs], b.ap[:, 0:128], ACT.Copy, tok, t_x))
            t_it.append(act(I2T[:, qs], b.ap[:, 128:256], ACT.Copy, tok))
            rest = EQ[:, 0:1, 0:8, :].rearrange("p h k j -> p (h k j)")
            w1 = vcopy(GT[0][:, qs], b.ap[:, 256:384], tok, t9, t_it)
            w2_ = tt(rest, b.ap[:, 256:384], GT[0][:, qs], SUB, w1)
            w3 = vcopy(GT[1][:, qs], rest, w2_)
            w4 = tt(rest, rest, GT[1][:, qs], SUB, w3)
            t_it.append(vcopy(GT[2][:, qs], rest, w4))
            banks.put(b, t_it[-1], t_it[-2], w2_)

        WS = [reg(1, 8), reg(9, 8)]
        OB = [[reg(17 + 10 * r, 10).bitcast(bf16)[:, 2048 * i:2048 * i + 2048].rearrange("p (i t) -> p i t", t=16) for i in range(5)]
              for r in range(2)]
        IOX = reg(37, 2).bitcast(bf16)[:, 0:2048].rearrange("p (i t) -> p i t", t=16)
        t_iox = vcopy(IOX, iota.unsqueeze(2).broadcast_to([128, 128, 16]), t_it, DVE.last())
        ob_free = [None, None]
        ws_free = [None, None]
        d_ws = [dsem("d_ws0"), dsem("d_ws1")]
        for g in range(32):
            tb_, wv = g // 2, WS[(g // 2) % 2].rearrange("p (i t) -> p i t", t=32)
            o2, o1, oa, ob, oc = OB[g % 2]
            ns = slice(g * 16, g * 16 + 16)
            rows = lambda ap: ap[:, ns].unsqueeze(1).broadcast_to([128, 128, 16])
            c1 = tt(o2, IOX, rows(I2T), ALU.is_equal, t_iox, t_it, ob_free[g % 2])
            c2 = tt(o1, IOX, rows(I1T), ALU.is_equal)
            c3 = [tt(x, o1, rows(GT[i]), MUL, c2) for i, x in enumerate((oa, ob, oc))]
            for f in range(4):
                b = banks.get()
                PE.wait(b.free, c1, c3)
                for i in range(4):
                    n = f * 4 + i
                    tok = mms(b.ap[:, i * 128:(i + 1) * 128], [(o2[:, :, n], x[:, :, n]) for x in (oa, ob, oc)])
                h0 = (g % 2) * 16 + f * 4
                t1 = act(wv[:, :, h0:h0 + 4].rearrange("p i t -> p t i"), b.ap.rearrange("p (t i) -> p t i", t=4), ACT.Copy,
                         tok, ws_free[tb_ % 2])
                banks.put(b, t1)
            ob_free[g % 2] = tok
            if g % 2:
                ws_free[tb_ % 2] = dma(SC, nc.scalar, d_ws[tb_ % 2], Wd[tb_], WS[tb_ % 2], t1)
        t_w = [ws_free[0], ws_free[1], tok, t1, c3[-1]]

        early.close()
        GE = [[sb(f"ge{i}{p}", 4 * S, f32r)[:, :].rearrange("p (k n) -> p k n", k=4) for p in range(2)] for i in range(2)]
        parts = Pool([Place([sb(f"part{i}{p}", 2048, f32r)[:, :] for p in range(2)]) for i in range(2)])
        Y = sb("y", 8 * S)[:, :].rearrange("p (k n) -> p k n", k=8)
        wring = Pool([Place(sb(f"wr{i}", 4 * S)[:, :], sem(f"s_wr{i}")) for i in range(2)])
        GTMP = [sb(f"gt{i}", S)[:, :] for i in range(2)]
        for p_ in wring.q + parts.q:
            p_.free = [t_w]
        ge_free = [None, None]
        gt_free = [None, None]
        t_yy = [None] * 8

        def load_split(src, k):
            r = raw.get()
            tok = dma(SP, nc.sync, r.counter, r.ap.rearrange("p (k n) -> p k n", k=k), src, r.free)
            s = parts.get()
            s.ready = split(s.ap[0], s.ap[1], r.ap, tok, s.free)
            raw.put(r, s.ready)
            return s, [x.rearrange("p (k n) -> p k n", k=k) for x in s.ap]

        order = [("u", 0, 0), ("u", 0, 1)]
        for c in range(32):
            order += [("u", c + 1, 0), ("u", c + 1, 1)] if c < 31 else []
            order += [("v", c, 0), ("v", c, 1)]
        ahead = []

        def next_slot():
            while order and len(ahead) < 2:
                which, c, half = order.pop(0)
                if which == "u":
                    ahead.append(load_split(A["u"][2 * c + half], 8))
                else:
                    vs = A["v"][c * 512:(c + 1) * 512, :].rearrange("(k p) n -> p k n", p=128)
                    ahead.append(load_split(vs[:, :, half * 512:half * 512 + 512], 4))
            return ahead.pop(0)

        def peer_up(c):
            wr = wring.get()
            wt = dma(SP, nc.sync, wr.counter, wr.ap.rearrange("p (b i) -> p b i", b=16),
                     Wd.rearrange("b p (c i) -> c p b i", c=32)[c], wr.free, t_w)
            ww = wr.ap.rearrange("p (b i t) -> p i b t", b=16, i=4)
            gh, gl = GE[c % 2]
            toks = []
            for half in range(2):
                s, (wh, wl) = next_slot()
                for j in range(2):
                    i = 2 * half + j
                    b = banks.get()
                    js = slice(j * 128, (j + 1) * 128)
                    tok = mms(b.ap, [p for k in range(8) for p in three(wh[:, k, js], wl[:, k, js], HR[0][:, k, :], HR[1][:, k, :])],
                              b.free, s.ready, t_hr)
                    g = GTMP[i % 2]
                    t1 = act(g, b.ap, ACT.Gelu_apprx_tanh, tok, gt_free[i % 2], t_w)
                    banks.put(b, t1)
                    g3 = g.rearrange("p (b t) -> p b t", b=16)
                    t2 = tt(g3, g3, ww[:, i, :, :], MUL, t1, wt)
                    t3 = split(gh[:, i, :], gl[:, i, :], g, t2, ge_free[c % 2])
                    gt_free[i % 2] = t3
                    toks.append(t3)
                parts.put(s, tok)
            wring.put(wr, t2)
            return toks

        def peer_down(c, ready):
            gh, gl = GE[c % 2]
            for half in range(2):
                s, (wh, wl) = next_slot()
                for j in range(4):
                    d = half * 4 + j
                    b = banks.get()
                    js = slice(j * 128, (j + 1) * 128)
                    tok = mms(b.ap, [p for k in range(4) for p in three(wh[:, k, js], wl[:, k, js], gh[:, k, :], gl[:, k, :])],
                              b.free, s.ready, ready)
                    if c == 0:
                        t_yy[d] = vcopy(Y[:, d, :], b.ap, tok, t_w)
                    else:
                        t_yy[d] = tt(Y[:, d, :], Y[:, d, :], b.ap, ADD, tok, t_yy[d])
                    banks.put(b, t_yy[d])
                parts.put(s, tok)
            ge_free[c % 2] = tok

        ready = peer_up(0)
        for c in range(32):
            nxt = peer_up(c + 1) if c < 31 else None
            peer_down(c, ready)
            ready = nxt

        for d in range(8):
            t_x = stt(X[:, d, :], Y[:, d, :], MOD[:, 40 + d, 0:1], X[:, d, :], MUL, ADD, t_yy[d])
        PE.wait(t_x)
        t_h = norm(X, lambda k: par("gfin", k), t_x, PE.last())
        t_o = dma(SP, nc.sync, d_o, out.rearrange("(k p) n -> p k n", p=128), H, t_h)
        SP.wait(t_o)

        block = ctx.enter_context(nc.Block())

        @block.sync
        def _(eng):
            SP.run(eng)

        @block.gpsimd
        def _(eng):
            GP.run(eng)

        @block.scalar
        def _(eng):
            SC.run(eng)

        @block.vector
        def _(eng):
            DVE.run(eng)

        @block.tensor
        def _(eng):
            PE.run(eng)


def constants():
    f = np.float32
    i = np.arange(128)
    c = {
        "ident": np.eye(128), "ones": np.ones((128, 128)),
        "blk": (i[:, None] // 64 == i[None] // 64),
        "linc": (i[:, None] >= i[None]), "smask": (i[None] > i[:, None]),
        "nmask": np.where(i[None] > i[:, None], 0.0, -BIG),
        "iota": np.broadcast_to(i, (128, 128)),
    }
    rot = np.zeros((128, 128))
    for d in range(128):
        if d % 32 < 16:
            rot[d + 16, d] = -1.0
        else:
            rot[d - 16, d] = 1.0
    c["rot"] = rot
    consts = np.concatenate([np.asarray(c[n], f) for n in CNAMES], axis=1)
    tpos = np.arange(S)
    row, col = (tpos // 64).astype(f), (tpos % 64).astype(f)
    inv = f(10000.0) ** (-np.arange(0, 32, 2, dtype=f) / f(32))
    ar, ac = row[:, None] * inv, col[:, None] * inv
    ang = np.concatenate([ar, ar, ac, ac], axis=-1).astype(f).T
    ang = np.concatenate([ang, ang], axis=0)
    rope = np.stack([np.cos(ang), np.sin(ang)]).astype(f)
    t01 = np.linspace(0.0, 1.0, S, dtype=f)[:, None]
    w = (f(2.0 * math.pi) * np.arange(S, dtype=f)[:, None] / f(S)).astype(f)
    fr = np.linspace(1e-4, 15, 16, dtype=f)[None]
    zf = np.concatenate([t01, np.cos(fr * w), -np.sin(fr * w)], axis=-1).astype(f).T
    deltas = np.abs(np.linspace(math.log(1e-2) / 1.5, math.log(1e-2) / 0.3, 512, dtype=f))
    dec = np.exp(-t01 * deltas).astype(f)
    n = np.arange(S)
    ph = (n[:, None] * n[None]) % 1024 * (2.0 * math.pi / 1024)
    fc, fs = np.cos(ph), np.sin(ph)
    fs[:, 0] = np.where(n % 2 == 0, 1.0, -1.0)
    dft = np.stack([fc, fs, fs.T, dec]).astype(f)
    tid = (np.arange(4, dtype=np.uint32)[None] * 128 + np.arange(128, dtype=np.uint32)[:, None])
    return {"tid": np.ascontiguousarray(tid), "consts": consts, "rope": np.ascontiguousarray(rope), "zf": np.ascontiguousarray(zf), "dft": dft}


def layout(I):
    c = np.ascontiguousarray

    def cols(x):
        return np.asarray(x).reshape(-1, 128).T

    def twice(x):
        return np.concatenate([x, x]).reshape(128, 1)

    def pad(x):
        return np.concatenate([x, x]).reshape(128, 1)

    p = {
        "g1": cols(I["norm_mix_g"]), "gf1": cols(I["norm_ffn_g"]),
        "qg1": twice(I["q_norm_g"][0]), "kg1": twice(I["k_norm_g"][0]),
        "cw": cols(I["conv_w"]),
        "rb": np.broadcast_to(np.concatenate([I["b_router_group"][0], I["b_router_expert"][0]]), (128, 36)),
        "ab": cols(I["ada_b_2"]), "g2": cols(I["norm_mix_g_2"]), "gf2": cols(I["norm_ffn_g_2"]),
        "gfin": cols(I["final_norm_g_2"]), "qg2": twice(I["q_norm_g_2"][0]), "kg2": twice(I["k_norm_g_2"][0]),
        "hcw": cols(I["hy_conv_w_2"]), "hcb": cols(I["hy_conv_b_2"]),
        "hb1": pad(I["hf_b1_2"][0]), "hb2": pad(I["hf_b2_2"][0]), "hb3": pad(I["hf_b3_2"][0]), "hfr": pad(I["hf_freq_2"][0]),
        "cc": np.stack([cols(I["c_2"]), cols(I["c_ctx_2"])], axis=2).reshape(128, 16),
    }
    params = np.concatenate([p[n] for n in PCOLS], axis=1)
    w2 = I["w_in_2"][0]
    qc = w2[:, 0:512].reshape(D, 2, 4, 64).transpose(0, 2, 1, 3).reshape(D, 512)
    w_in_2 = np.concatenate([w2[:, 768:2304], qc, w2[:, 2304:4352], w2[:, 512:768]], axis=1)
    wa = I["w_attn_out_2"][0].reshape(2, 4, 64, D).transpose(1, 0, 2, 3).reshape(512, D)
    keys = np.stack([I["peer_keys1_2"][0], I["peer_keys2_2"][0]], axis=1)
    u = I["peer_u_2"][0].reshape(64, 256, 8, 128).transpose(0, 3, 2, 1)
    skip = np.broadcast_to(I["hy_skip_2"][0].reshape(1, 1024), (128, 1024))
    out = {
        "params": c(params), "x": c(I["x"][0].T), "ctx": c(I["ctx_2"][0].T),
        "w_in": I["w_in"][0], "w_sb": I["w_sb_branch"][0], "w_conv": I["w_conv_branch"][0], "w_out": I["w_out"][0],
        "w_router": c(np.concatenate([I["w_router_group"][0], I["w_router_expert"][0]], axis=1)),
        "w_gate": I["w_gate_e"][0], "w_up": I["w_up_e"][0], "w_down": I["w_down_e"][0],
        "ada_w": I["ada_w_2"][0], "w_in_2": c(w_in_2), "w_attn": c(wa), "w_hy": I["w_hy_out_2"][0],
        "w_out_2": I["w_out_2"][0], "wq": I["peer_wq_2"][0],
        "keys": c(keys.transpose(3, 0, 1, 2).reshape(128, 2048)),
        "u": c(u), "v": I["peer_v_2"][0], "skip": c(skip),
        "hf_w1": I["hf_w1_2"][0], "hf_w2": I["hf_w2_2"][0], "hf_w3": I["hf_w3_2"][0], "hf_w4": I["hf_w4_2"][0],
    }
    return {k: c(np.asarray(x)) for k, x in out.items()}


def kernel(**inputs):
    import concourse.bacc as bacc
    from concourse.bass_utils import run_bass_kernel_spmd

    arrays = layout({k: np.asarray(x) for k, x in inputs.items()})
    arrays.update(constants())
    nc = bacc.Bacc("TRN2", target_bir_lowering=False, num_devices=1)
    feeds, A = {}, {}
    for name, x in arrays.items():
        feeds[f"in_{name}"] = x
        A[name] = nc.dram_tensor(f"in_{name}", x.shape, mybir.dt.from_np(x.dtype), kind="ExternalInput").ap()
    out = nc.dram_tensor("out_0", (D, S), mybir.dt.float32, kind="ExternalOutput").ap()
    program(nc, A, out)
    r = run_bass_kernel_spmd(nc, [feeds], core_ids=[0])
    return np.ascontiguousarray(r.results[0]["out_0"].T)[None]
```

```python
import math

import numpy as np

import concourse.bass as bass
from concourse import mybir

S = 512
D = 1024
EPS = 1e-6
BIG = 1.0e30

PCOLS = {}
_n = 0
for _name, _w in [("g1", 8), ("gf1", 8), ("qg1", 1), ("kg1", 1), ("cw", 12), ("rb", 36), ("ab", 48),
                  ("g2", 8), ("gf2", 8), ("gfin", 8), ("qg2", 1), ("kg2", 1), ("hcw", 36), ("hcb", 12),
                  ("hb1", 1), ("hb2", 1), ("hb3", 1), ("hfr", 1), ("cc", 16)]:
    PCOLS[_name] = (_n, _n + _w)
    _n += _w
PTOTAL = _n
CNAMES = ["ident", "ones", "blk", "linc", "smask", "nmask", "iota", "rot"]


class Engine:

    def __init__(self, sem):
        self.sem, self.n, self.items, self.seen = sem, 0, [], {}

    def wait(self, *toks):
        for t in toks:
            if t is None:
                continue
            if isinstance(t, list):
                self.wait(*t)
                continue
            sem, val = t
            if self.seen.get(id(sem), 0) < val:
                self.seen[id(sem)] = val
                self.items.append((None, sem, val))

    def do(self, fn, *after, sig=True):
        self.wait(*after)
        if not sig:
            self.items.append((fn, None, 0))
            return None
        self.n += 1
        self.items.append((fn, self.sem, 1))
        return (self.sem, self.n)

    def last(self):
        return (self.sem, self.n) if self.n else None

    def enter(self, sem):
        self.outer = (self.sem, self.n, self.items, self.seen)
        self.sem, self.n, self.items, self.seen = sem, 0, [], dict(self.seen)

    def leave(self, count):
        inner = self.items
        self.sem, self.n, self.items, self.seen = self.outer
        self.items.append((inner, count, 0))

    def run(self, eng, items=None):
        for fn, sem, val in self.items if items is None else items:
            if isinstance(fn, list):
                n = eng.value_load(sem, min_val=0, max_val=7)
                with eng.If(n > 0):
                    self.run(eng, fn)
            elif fn is None:
                eng.wait_ge(sem, val)
            else:
                ins = fn()
                if sem is not None:
                    ins.then_inc(sem, val)


class Counter:
    def __init__(self, sem):
        self.sem, self.n = sem, 0


class Place:

    def __init__(self, ap, sem=None):
        self.ap, self.free, self.counter = ap, [], Counter(sem)


class Pool:
    def __init__(self, places):
        self.q = list(places)

    def get(self):
        return self.q.pop(0)

    def put(self, place, *toks):
        place.free = list(toks)
        self.q.append(place)


def program(nc, A, out):
    f32 = mybir.dt.float32
    u32 = mybir.dt.uint32
    bf16 = mybir.dt.bfloat16
    f32r = mybir.dt.float32r
    ALU = mybir.AluOpType
    ACT = mybir.ActivationFunctionType
    AX = mybir.AxisListType
    from contextlib import ExitStack
    ctx = ExitStack()
    with ctx:
        def sb(name, cols, dt=f32, stack=None, side=None):
            return (stack or ctx).enter_context(nc.sbuf_tensor(name, [128, cols], dt, side=side))

        early, ring = ExitStack(), ExitStack()

        def sem(name):
            return ctx.enter_context(nc.semaphore(name))

        def dsem(name):
            return Counter(sem(name))

        v, a, t = nc.vector, nc.scalar, nc.tensor
        PE, DVE, SC, GP, SP = (Engine(sem(n)) for n in ("s_pe", "s_dve", "s_act", "s_pool", "s_sp"))

        def dma(queue, eng, counter, dst, src, *after):
            counter.n += 16
            sem_ = counter.sem
            queue.wait(*after)
            queue.items.append((lambda: eng.dma_start(dst, src), sem_, 16))
            return (sem_, counter.n)

        def dma_call(queue, counter, call, *after):
            counter.n += 16
            queue.wait(*after)
            queue.items.append((call, counter.sem, 16))
            return (counter.sem, counter.n)

        X = sb("X", 8 * S)[:, :].rearrange("p (k n) -> p k n", k=8)
        NSLOT = 4
        slots = Pool([Place(sb(f"W{i}", 4096, f32, ring, "right")[:, :], sem(f"s_w{i}")) for i in range(NSLOT)])
        NA = 46
        TMP = sb("tmp", 5 * S)
        CST = sb("cst", len(CNAMES) * 128)
        PAR = sb("par", PTOTAL)
        MODS = sb("mods", 136)
        TID = sb("tid", 4, u32)
        NX = sb("nx", 1, u32)
        H = sb("H", 8 * S, f32, early)[:, :].rearrange("p (k n) -> p k n", k=8)
        arena = sb("arena", NA * S, f32, early)
        area = [NA, arena]
        banks = Pool([Place(ctx.enter_context(nc.psum_tensor(f"P{i}", [128, 512], f32))[:, :]) for i in range(8)])
        Wd = nc.dram_tensor("w_scratch", [16, 128, 128 * 32], f32).ap()
        FA, FB = 1.2, 1.6
        NT = 39
        Hd = nc.dram_tensor("h_rows", [S, D], f32).ap()
        Ad = nc.dram_tensor("a_scratch", [32, 128, 4 * S], f32).ap()
        Yd = nc.dram_tensor("y_rows", [128 * NT, D], f32).ap()

        def reg(at, n):
            assert at + n <= area[0]
            return area[1][:, at * S:(at + n) * S]

        def tiles(at, n):
            return reg(at, n).rearrange("p (k n) -> p k n", k=n)

        def cst(name):
            i = CNAMES.index(name)
            return CST[:, i * 128:(i + 1) * 128]

        def par(name, i=None):
            lo, hi = PCOLS[name]
            return PAR[:, lo:hi] if i is None else PAR[:, lo + i:lo + i + 1]

        ident, ones, blk = cst("ident"), cst("ones"), cst("blk")
        tmp = [TMP[:, i * S:(i + 1) * S] for i in range(5)]

        def tt(out_, in0, in1, op, *after):
            return DVE.do(lambda: v.tensor_tensor(out=out_, in0=in0, in1=in1, op=op), *after)

        def ts(out_, in0, s1, s2, op0, op1, *after):
            if op1 is None:
                return DVE.do(lambda: v.tensor_scalar(out=out_, in0=in0, scalar1=s1, scalar2=None, op0=op0), *after)
            return DVE.do(lambda: v.tensor_scalar(out=out_, in0=in0, scalar1=s1, scalar2=s2, op0=op0, op1=op1), *after)

        def stt(out_, in0, s, in1, op0, op1, *after):
            return DVE.do(lambda: v.scalar_tensor_tensor(out=out_, in0=in0, scalar=s, in1=in1, op0=op0, op1=op1), *after)

        def vcopy(out_, in_, *after):
            return DVE.do(lambda: v.tensor_copy(out_, in_), *after)

        def act(out_, in_, fn, *after, bias=None, scale=None, acc=None):
            kw = {}
            if bias is not None:
                kw["bias"] = bias
            if scale is not None:
                kw["scale"] = scale
            if acc is not None:
                kw["accum_out"] = acc
            return SC.do(lambda: a.activation(out_, in_, fn, **kw), *after)

        def mms(out_, pairs, *after, start=True, stop=True):
            PE.wait(*after)
            n = len(pairs)
            tok = None
            for i, (l, r, *ready) in enumerate(pairs):
                PE.wait(*ready)
                st, sp = start and i == 0, stop and i == n - 1
                tok = PE.do(lambda l=l, r=r, st=st, sp=sp: t.matmul(out_, l, r, start=st, stop=sp), sig=i == n - 1)
            return tok

        def transpose(out_, in_, *after, sig=True):
            return PE.do(lambda: t.transpose(out_, in_, ident), *after, sig=sig)

        MUL, ADD, SUB = ALU.mult, ALU.add, ALU.subtract

        def split(hi, lo, x, *after, on=None):
            t1 = act(hi, x, ACT.Copy, *after)
            if on is GP:
                return GP.do(lambda: nc.gpsimd.tensor_tensor(out=lo, in0=x, in1=hi.bitcast(f32), op=SUB), t1)
            return tt(lo, x, hi.bitcast(f32), SUB, t1)

        def three(wh, wl, xh, xl):
            return [(wh, xh), (wh, xl), (wl, xh)]

        def load(pieces, *after):
            s = slots.get()
            tok = None
            for lo, hi, view, src in pieces:
                dst = s.ap[:, lo:hi]
                if view:
                    dst = view(dst)
                tok = dma(SP, nc.sync, s.counter, dst, src, s.free, *after)
            s.ready = tok
            return s

        k8 = lambda ap: ap.rearrange("p (k n) -> p k n", k=8)
        k4 = lambda ap: ap.rearrange("p (k n) -> p k n", k=4)
        k2 = lambda ap: ap.rearrange("p (k n) -> p k n", k=2)

        def load_cols(w, lo, hi):
            n = hi - lo
            return load([(0, 8 * n, k8, w[:, lo:hi].rearrange("(k p) n -> p k n", p=128))])

        def load_half(w):
            return load([(0, 4096, k4, w.rearrange("(k p) n -> p k n", p=128))])

        d_c, d_p, d_o = dsem("d_c"), dsem("d_p"), dsem("d_o")
        t_c = dma(SC, nc.scalar, d_c, CST[:, :], A["consts"])
        t_p = dma(SC, nc.scalar, d_p, PAR[:, :], A["params"])
        t_tid = dma(SC, nc.scalar, dsem("d_t"), TID[:, :], A["tid"])
        t_x = []
        for k in range(0, 8, 2):
            t_x += 2 * [dma(SP, nc.sync, dsem(f"d_x{k}"), X[:, k:k + 2, :], A["x"][k * 128:k * 128 + 256, :].rearrange("(k p) n -> p k n", p=128))]
        for e in (PE, DVE, SC, GP):
            e.wait(t_c, t_p)

        last_r = [None]

        def factor(srcs, lhs, inv, n, *after, each=None):
            b = banks.get()
            PE.wait(b.free)
            sq_free = factor_sq
            tok = None
            for i, s in enumerate(srcs):
                j = i % 2
                q = tmp[j][:, 0:n]
                tk = act(q, s, ACT.Square, sq_free[j], *after, each[i] if each else None)
                tok = PE.do(lambda q=q, i=i: t.matmul(b.ap[:, 0:n], lhs, q, start=i == 0, stop=i == len(srcs) - 1), tk)
                sq_free[j] = tok
            m, r, w = tmp[2][:, 0:n], tmp[3][:, 0:n], tmp[4][:, 0:n]
            t1 = ts(m, b.ap[:, 0:n], inv, EPS, MUL, ADD, tok, last_r[0])
            banks.put(b, t1)
            t2 = act(r, m, ACT.Ln, t1)
            t3 = act(w, r, ACT.Exp, t2, scale=-0.5)
            t4 = tt(r, w, w, MUL, t3)
            t5 = stt(r, r, -0.5, m, MUL, MUL, t4)
            t7 = stt(r, r, 1.5, w, ADD, MUL, t5)
            return r, t7

        factor_sq = [None, None]

        def norm(src, gain, each):
            r, tr = factor([src[:, k, :] for k in range(8)], ones, 1.0 / D, S, each=each)
            toks = []
            for k in range(8):
                toks.append(stt(H[:, k, :], src[:, k, :], gain(k), r, MUL, MUL, tr))
            last_r[0] = toks[-1]
            return toks

        def proj(slot, c, h_tok, width=512):
            b = banks.get()
            w = slot.ap[:, 0:8 * width].rearrange("p (k n) -> p k n", k=8)
            tok = mms(b.ap, [(w[:, k, c * 128:(c + 1) * 128], H[:, k, :], h_tok[k]) for k in range(8)], b.free, slot.ready)
            return b, tok

        def drain(gen):
            for _ in gen:
                pass

        def mixed(*gens):
            gens = list(gens)
            while gens:
                for g in list(gens):
                    try:
                        yield next(g)
                    except StopIteration:
                        gens.remove(g)

        def mix(*gens):
            drain(mixed(*gens))

        def beside(main, other, n):
            k = 0
            for _ in main:
                k += n
                while k >= 1:
                    k -= 1
                    next(other, None)

        nil = reg(36, 2)
        t_z = DVE.do(lambda: v.memset(nil, 0.0))
        d_z = dsem("d_z")

        t_h = norm(X, lambda k: par("g1", k), t_x)
        GP.wait(t_h)
        for i in range(32, NT):
            t_zd = dma(GP, nc.gpsimd, d_z, Yd[i * 128:(i + 1) * 128, :], nil, t_z)
        Q, K, V, AT = tiles(0, 4), tiles(4, 4), tiles(8, 4), tiles(12, 4)
        CB, CC, CU = tiles(16, 4), tiles(20, 4), tiles(24, 4)
        GA, GB = tiles(28, 8), tiles(36, 8)
        w_in = A["w_in"]

        def head_norm(dst, t0, gain):
            r, tr = factor([dst], blk, 1.0 / 64, S, t0)
            t1 = stt(dst, dst, gain, r, MUL, MUL, tr)
            last_r[0] = t1
            return t1

        t_q, t_k, t_v = [None] * 4, [None] * 4, [None] * 4

        def project_qkv():
            raw_q, raw_k = [None] * 4, [None] * 4
            for which, dst, raw_ in ((0, Q, raw_q), (1, K, raw_k)):
                s = load_cols(w_in, which * 512, which * 512 + 512)
                for c in range(4):
                    b, tok = proj(s, c, t_h)
                    raw_[c] = act(dst[:, c, :], b.ap, ACT.Copy, tok)
                    banks.put(b, raw_[c])
                    if which:
                        t_q[c] = head_norm(Q[:, c, :], raw_q[c], par("qg1", 0))
                slots.put(s, tok)
            s = load_cols(w_in, 1024, 1536)
            w = k8(s.ap)
            for c in range(4):
                b = banks.get()
                tok = mms(b.ap, [(H[:, k, c * 128:(c + 1) * 128], w[:, k, :]) for k in range(8)], b.free, s.ready, t_h)
                t_v[c] = act(V[:, c, :], b.ap, ACT.Copy, tok)
                banks.put(b, t_v[c])
                t_k[c] = head_norm(K[:, c, :], raw_k[c], par("kg1", 0))
            slots.put(s, tok)

        project_qkv()

        MOD, SCC = MODS[:, 0:96].rearrange("p (k n) -> p k n", n=2), MODS[:, 96:112].rearrange("p (k n) -> p k n", n=2)
        G2, GF2 = MODS[:, 112:128], MODS[:, 128:136]
        ft = [sb(f"ft{i}", S, f32, early)[:, :] for i in range(2)]
        t_g2 = None

        def ada():
            nonlocal t_g2
            t_sc = act(SCC, par("cc").rearrange("p (k n) -> p k n", n=2), ACT.Silu)
            eye = ident.unsqueeze(1).broadcast_to([128, 4, 128])
            red = [None, None]
            for i in range(12):
                s = load_cols(A["ada_w"], i * 512, i * 512 + 512)
                w = k8(s.ap)
                end = []
                for x in range(2):
                    t1 = ts(ft[x], w[:, 0, :], SCC[:, 0, x:x + 1], None, MUL, None, s.ready, t_sc, red[x])
                    for k in range(1, 8):
                        t1 = stt(ft[x], w[:, k, :], SCC[:, k, x:x + 1], ft[x], MUL, ADD, t1)
                        if k == 4:
                            yield
                    end.append(t1)
                    yield
                    b = banks.get()
                    tok = mms(b.ap, [(ones, ft[x])], b.free, t1)
                    f4 = ft[x].rearrange("p (c n) -> p c n", c=4)
                    t2 = tt(f4, b.ap.rearrange("p (c n) -> p c n", c=4), eye, MUL, tok)
                    banks.put(b, t2)
                    red[x] = DVE.do(lambda i=i, x=x, f4=f4: v.tensor_reduce(out=MOD[:, 4 * i:4 * i + 4, x:x + 1].rearrange("p k n -> p (k n)"),
                                                                  in_=f4, axis=AX.X, op=ADD), t2)
                slots.put(s, end)
            t_mod = tt(MOD, MOD, par("ab").unsqueeze(2).broadcast_to([128, 48, 2]), ADD, red)
            for w in range(2):
                t_g2 = stt(G2[:, 8 * w:8 * w + 8], MOD[:, 8:16, w], 1.0, par("g2"), ADD, MUL, t_mod)
            t_g2 = stt(GF2, MOD[:, 32:40, 0], 1.0, par("gf2"), ADD, MUL, t_mod, t_g2)

        OFF = [0, 512, 896, 1152]
        ZB = [reg(36, 10)[:, 0:1280], reg(36, 10)[:, 1280:2560]]
        EB = [reg(36, 10)[:, 2560:3840], reg(36, 10)[:, 3840:5120]]
        pv_tok = [None] * 8
        t_at = [None] * 8
        in_free = [None] * 8

        def attention():
            for h in range(8):
                j, po = h // 2, 64 * (h % 2)
                Z, E = ZB[h % 2], EB[h % 2]
                tz = None
                for i in range(4):
                    n = 512 - 128 * i
                    b = banks.get()
                    tok = mms(b.ap[:, 0:n], [(K[po:po + 64, j, i * 128:(i + 1) * 128], Q[po:po + 64, j, i * 128:512])],
                              b.free, t_q[j], t_k[j])
                    tz = act(Z[:, OFF[i]:OFF[i] + n], b.ap[:, 0:n], ACT.Copy, tok, pv_tok[h - 2] if h >= 2 else t_zd, scale=0.125)
                    banks.put(b, tz)
                t1 = act(E, Z, ACT.Abs, tz, in_free[h - 2] if h >= 2 else None)
                t2 = act(E, E, ACT.Exp, t1, scale=-1.0)
                t3 = act(E, E, ACT.Ln, t2, bias=1.0)
                t4 = stt(E, Z, 0.0, E, ALU.max, ADD, t3)
                for i in range(4):
                    d = E[:, OFF[i]:OFF[i] + 128]
                    t5 = tt(d, d, cst("smask"), MUL, t4)
                yield
                te = None
                for i in range(4):
                    n = 512 - 128 * i
                    b = banks.get()
                    PE.wait(b.free, t5)
                    for jj in range(i, 4):
                        l = cst("linc") if jj == i else ones
                        o = (jj - i) * 128
                        tok = PE.do(lambda b=b, l=l, o=o, jj=jj, i=i, n=n, E=E: t.matmul(
                            b.ap[:, o:n], l, E[:, OFF[jj]:OFF[jj] + 512 - 128 * jj], start=jj == i, stop=jj == 3),
                            sig=jj == 3)
                    z = Z[:, OFF[i]:OFF[i] + n]
                    t6 = tt(z, z, b.ap[:, 0:n], SUB, tok, tz)
                    banks.put(b, t6)
                    t7 = tt(z[:, 0:128], z[:, 0:128], cst("nmask"), ADD, t6)
                in_free[h] = tok
                te = act(Z, Z, ACT.Exp, t7)
                yield
                b = banks.get()
                PE.wait(b.free, te, t_v)
                for i in range(4):
                    tok = PE.do(lambda i=i, b=b, Z=Z, h=h, po=po: t.matmul(
                        b.ap[po:po + 64, 128 * i:512], V[:, i, h * 64:(h + 1) * 64],
                        Z[:, OFF[i]:OFF[i] + 512 - 128 * i], start=i == 0, stop=i == 3), sig=i == 3)
                pv_tok[h] = tok
                t_at[h] = act(AT[po:po + 64, j, :], b.ap[po:po + 64, :], ACT.Copy, tok)
                banks.put(b, t_at[h])
                yield

        t_cv = [None] * 4
        t_ga = [None] * 8

        def conv_gates():
            t_cb, t_cc = [None] * 4, [None] * 4
            for dst, lo, toks in ((CB, 1536, t_cb), (CC, 2048, t_cc)):
                s = load_cols(w_in, lo, lo + 512)
                for c in range(4):
                    b, tok = proj(s, c, t_h)
                    toks[c] = act(dst[:, c, :], b.ap, ACT.Copy, tok)
                    banks.put(b, toks[c])
                    yield
                slots.put(s, tok)
            s = load_cols(w_in, 2560, 3072)
            for c in range(4):
                b, tok = proj(s, c, t_h)
                cu, y = CC[:, c, :], CU[:, c, :]
                cw = lambda j, c=c: par("cw", j * 4 + c)
                t1 = tt(cu, cu, b.ap, MUL, tok, t_cc[c])
                banks.put(b, t1)
                t2 = ts(y, cu, cw(2), None, MUL, None, t1)
                t3 = stt(y[:, 1:S], cu[:, 0:S - 1], cw(1), y[:, 1:S], MUL, ADD, t2)
                t4 = stt(y[:, 2:S], cu[:, 0:S - 2], cw(0), y[:, 2:S], MUL, ADD, t3)
                t_cv[c] = tt(y, y, CB[:, c, :], MUL, t4, t_cb[c])
                yield
            slots.put(s, tok)
            for half in range(2):
                s = load_cols(w_in, 3072 + half * 512, 3584 + half * 512)
                for c in range(4):
                    b, tok = proj(s, c, t_h)
                    i = half * 4 + c
                    t_ga[i] = act(GA[:, i, :], b.ap, ACT.Sigmoid, tok)
                    banks.put(b, t_ga[i])
                    yield
                slots.put(s, tok)

        modulation = ada()
        beside(mixed(attention(), conv_gates()), modulation, 0.55)

        t_gb = [None] * 8

        def gates(dst, w, lo, toks, *after):
            for half in range(2):
                s = load_cols(w, lo + half * 512, lo + half * 512 + 512)
                for c in range(4):
                    b, tok = proj(s, c, t_h)
                    i = half * 4 + c
                    toks[i] = act(dst[:, i, :], b.ap, ACT.Sigmoid, tok, *after)
                    banks.put(b, toks[i])
                    yield
                slots.put(s, tok)

        beside(gates(GB, w_in, 4096, t_gb, pv_tok[6], pv_tok[7], in_free[6], in_free[7]), modulation, 1)

        def merge(wa, wb, ATT, CONV, t_att, t_conv, t_g1, t_g2, ga, gb, toks):
            for w, src, ready, g, tg in ((wa, ATT, t_att, ga, t_g1), (wb, CONV, t_conv, gb, t_g2)):
                s = load_half(w)
                wv = k4(s.ap)
                for c in range(8):
                    b = banks.get()
                    tok = mms(b.ap, [(wv[:, k, c * 128:(c + 1) * 128], src[:, k, :]) for k in range(4)], b.free, s.ready, ready)
                    t1 = tt(g[:, c, :], g[:, c, :], b.ap, MUL, tok, tg[c])
                    banks.put(b, t1)
                    if g is gb:
                        toks.append(tt(ga[:, c, :], ga[:, c, :], g[:, c, :], ADD, t1))
                    yield
                slots.put(s, tok)

        t_m = []
        beside(merge(A["w_sb"], A["w_conv"], AT, CU, t_at, t_cv, t_ga, t_gb, GA, GB, t_m), modulation, 1)
        drain(modulation)

        def out_proj(w, M, t_m, add):
            toks = []
            for half in range(2):
                s = load_cols(w, half * 512, half * 512 + 512)
                wv = k8(s.ap)
                for c in range(4):
                    b = banks.get()
                    tok = mms(b.ap, [(wv[:, k, c * 128:(c + 1) * 128], M[:, k, :], t_m[k]) for k in range(8)], b.free, s.ready)
                    toks.append(add(half * 4 + c, b, tok))
                    banks.put(b, toks[-1])
                slots.put(s, tok)
            return toks

        t_x = out_proj(A["w_out"], GA, t_m, lambda c, b, tok: tt(X[:, c, :], X[:, c, :], b.ap, ADD, tok))

        t_h = norm(X, lambda k: par("gf1", k), t_x)
        base = [0]
        scr = reg(0, 8)

        def small(n):
            base[0] += n
            return scr[:, base[0] - n:base[0]]

        WR = small(8 * 36).rearrange("p (k n) -> p k n", k=8)
        d_r = dsem("d_r")
        t_r = dma(SC, nc.scalar, d_r, WR, A["w_router"].rearrange("(k p) n -> p k n", p=128), t_x)
        b = banks.get()
        for q in range(4):
            tok = mms(b.ap[:, q * 36:(q + 1) * 36], [(H[:, k, q * 128:(q + 1) * 128], WR[:, k, :]) for k in range(8)],
                      b.free, t_r, t_h)
        LG = small(4 * 36).rearrange("p (k n) -> p k n", k=4)
        rb = par("rb").unsqueeze(1).broadcast_to([128, 4, 36])
        t_lg = tt(LG, b.ap[:, 0:144].rearrange("p (k n) -> p k n", k=4), rb, ADD, tok)
        banks.put(b, t_lg)
        HT = tiles(8, 8).rearrange("p (q c) n -> p q (c n)", q=4)
        d_ht = dsem("d_ht")
        for q in range(4):
            tcp = []
            for c in range(2):
                b = banks.get()
                PE.wait(b.free)
                for i in range(4):
                    tok = transpose(b.ap[:, i * 128:(i + 1) * 128], H[:, 4 * c + i, q * 128:(q + 1) * 128], t_h, sig=i == 3)
                tcp.append(act(HT[:, q, c * 512:(c + 1) * 512], b.ap, ACT.Copy, tok))
                banks.put(b, tcp[-1])
            t_hd = dma(SC, nc.scalar, d_ht, Hd[q * 128:(q + 1) * 128, :], HT[:, q, :], tcp)

        L8 = small(32).rearrange("p (k n) -> p k n", k=4)
        t1 = DVE.do(lambda: v.memset(L8, -BIG), t_lg)
        t_l8 = vcopy(L8[:, :, 0:4], LG[:, :, 0:4], t1)
        M8, E8, V8, WI, NM, SM, EX, ND, W0, W1, OG, I8f, J8f = (
            small(32).rearrange("p (k n) -> p k n", k=4) for _ in range(13))
        UI = small(32).bitcast(u32).rearrange("p (k n) -> p k n", k=4)
        UJ = small(32).bitcast(u32).rearrange("p (k n) -> p k n", k=4)
        iota = cst("iota")
        R4 = range(4)

        def each(f, *after):
            return [f(q) for q in R4]

        ta = [DVE.do(lambda q=q: v.max(M8[:, q, :], L8[:, q, :]), t_l8) for q in R4]
        tb = [DVE.do(lambda q=q: v.max_index(UI[:, q, :], M8[:, q, :], L8[:, q, :]), ta[q]) for q in R4]
        tc = vcopy(I8f, UI, tb)
        td = ts(NM, M8, -1.0, None, MUL, None, ta)
        tex = [act(EX[:, q, 0:4], L8[:, q, 0:4], ACT.Exp, td, bias=NM[:, q, 0:1], acc=SM[:, q, 0:1]) for q in R4]
        tgw = DVE.do(lambda: v.reciprocal(SM[:, :, 1:2], SM[:, :, 0:1]), tex)
        tog = [ts(OG[:, q, 0:4], iota[:, 0:4], I8f[:, q, 0:1], None, ALU.is_equal, None, tc) for q in R4]
        te = [ts(E8[:, q, :], LG[:, q, 4:12], OG[:, q, 0:1], None, MUL, None, tog) for q in R4]
        for g in range(1, 4):
            te = [stt(E8[:, q, :], LG[:, q, 4 + 8 * g:12 + 8 * g], OG[:, q, g:g + 1], E8[:, q, :], MUL, ADD, te[q]) for q in R4]
        ta = [DVE.do(lambda q=q: v.max(V8[:, q, :], E8[:, q, :]), te[q]) for q in R4]
        tb = [DVE.do(lambda q=q: v.max_index(UJ[:, q, :], V8[:, q, :], E8[:, q, :]), ta[q]) for q in R4]
        tc = vcopy(J8f, UJ, tb)
        td = tt(ND[:, :, 0:1], V8[:, :, 1:2], V8[:, :, 0:1], SUB, ta)
        te = act(ND[:, :, 1:2], ND[:, :, 0:1], ACT.Exp, td)
        tf = ts(ND[:, :, 2:3], ND[:, :, 1:2], 1.0, None, ADD, None, te)
        tg = DVE.do(lambda: v.reciprocal(ND[:, :, 3:4], ND[:, :, 2:3]), tf)
        th = tt(ND[:, :, 4:5], ND[:, :, 3:4], ND[:, :, 1:2], MUL, tg)
        tw0 = [ts(W0[:, q, :], iota[:, 0:8], J8f[:, q, 0:1], ND[:, q, 3:4], ALU.is_equal, MUL, tc, tg) for q in R4]
        tw1 = [ts(W1[:, q, :], iota[:, 0:8], J8f[:, q, 1:2], ND[:, q, 4:5], ALU.is_equal, MUL, th) for q in R4]
        ti = tt(WI, W0, W1, ADD, tw0, tw1)
        ti = [ts(WI[:, q, :], WI[:, q, :], SM[:, q, 1:2], None, MUL, None, ti, tgw) for q in R4]
        OHK = [small(128).rearrange("p (k n) -> p k n", k=4) for _ in range(2)]
        tko = []
        for kk, src in ((0, J8f[:, :, 0:1]), (1, J8f[:, :, 1:2])):
            for q in R4:
                eq = (W0, W1)[kk]
                tko.append(ts(eq[:, q, :], iota[:, 0:8], src[:, q, :], None, ALU.is_equal, None, ti))
        tkk = []
        for kk in range(2):
            for q in R4:
                for g in range(4):
                    tkk.append(ts(OHK[kk][:, q, 8 * g:8 * g + 8], (W0, W1)[kk][:, q, :], OG[:, q, g:g + 1], None, MUL, None, tko))
        WK = small(8).rearrange("p (k q) -> p k q", k=2)
        twk = [tt(WK[:, kk, :], ND[:, :, 3 + kk], SM[:, :, 1], MUL, tgw, th) for kk in range(2)]
        MI = small(128).rearrange("p (k n) -> p k n", k=4)
        tmi = tt(MI, OHK[0], OHK[1], ADD, tkk)
        b = banks.get()
        PE.wait(b.free)
        for q in R4:
            mms(b.ap[:, q * 32:(q + 1) * 32], [(ones, MI[:, qq, :]) for qq in range(q)] + [(cst("smask"), MI[:, q, :])], tmi)
        tok = mms(b.ap[:, 128:160], [(ones, MI[:, qq, :]) for qq in R4])
        RK, NE = small(128).rearrange("p (k n) -> p k n", k=4), small(32)
        OVF, CUM, AA, SL, TL, PO, IX = small(32), small(32), *(small(128).rearrange("p (k n) -> p k n", k=4) for _ in range(5))
        t1 = vcopy(RK, b.ap[:, 0:128].rearrange("p (k n) -> p k n", k=4), tok)
        t2 = vcopy(NE, b.ap[:, 128:160], tok)
        banks.put(b, t1, t2)
        t3 = ts(OVF, NE, 128.5, None, ALU.is_gt, None, t2)
        t3 = stt(OVF, NE, 256.5, OVF, ALU.is_gt, ADD, t3)
        t3 = stt(OVF, NE, 384.5, OVF, ALU.is_gt, ADD, t3)
        t4 = DVE.do(lambda: v.tensor_tensor_scan(out=CUM, data0=ones[:, 0:32], data1=OVF, initial=0.0, op0=MUL, op1=ADD), t3)
        t6 = ts(AA, RK, 127.5, None, ALU.is_gt, None, t1)
        t7 = ts(IX, RK, 127.5, None, ALU.is_gt, None, t1)
        t6 = stt(AA, RK, 255.5, AA, ALU.is_gt, ADD, t6)
        t6 = stt(AA, RK, 383.5, AA, ALU.is_gt, ADD, t6)
        t8 = stt(SL, AA, -128.0, RK, MUL, ADD, t6)
        CU2 = small(32)
        t9 = tt(CU2, CUM, OVF, SUB, t4)
        t9 = stt(CU2, CU2, 31.0, iota[:, 0:32], ADD, SUB, t9)
        t9 = tt(TL, AA, CU2.unsqueeze(1).broadcast_to([128, 4, 32]), ADD, t9)
        t9 = tt(TL, TL, IX, MUL, t9, t7)
        t9 = tt(TL, TL, iota[:, 0:32].unsqueeze(1).broadcast_to([128, 4, 32]), ADD, t9)
        PF, PU = small(24), small(8).bitcast(u32)
        tmpk = AA
        tl = t9
        for n_, (kk, src) in enumerate(((0, SL), (1, SL), (0, TL), (1, TL))):
            tl = tt(tmpk, OHK[kk], src, MUL, tl, t8)
            tl = DVE.do(lambda n_=n_: v.tensor_reduce(out=PF[:, 4 * n_:4 * n_ + 4], in_=tmpk, axis=AX.X, op=ADD), tl)
        tl = stt(PF[:, 16:24], PF[:, 8:16], 128.0, PF[:, 0:8], MUL, ADD, tl)
        t_pu = vcopy(PU, PF[:, 16:24], tl)
        LST = small(40).bitcast(u32)[:, 0:NT]
        OS = tiles(16, 2).rearrange("p k (j n) -> p (k j) n", n=128)
        OT = reg(18, 1)[:, 0:320].rearrange("p (k n) -> p k n", k=8)
        d_g = dsem("d_g")
        TIF = small(4)
        t_tf = vcopy(TIF, TID[:, :], t_tid, t_pu)
        los = []
        for n_ in range(8):
            kk, q = n_ // 4, n_ % 4
            los.append(ts(OS[:, n_, :], iota, PF[:, 4 * kk + q:4 * kk + q + 1], None, ALU.is_equal, None, t_pu))
            los.append(ts(OT[:, n_, 0:NT], iota[:, 0:NT], PF[:, 8 + 4 * kk + q:9 + 4 * kk + q], TIF[:, q:q + 1], ALU.is_equal, MUL, t_tf))
        b = banks.get()
        tok = mms(b.ap[:, 0:NT], [(OS[:, n_, :], OT[:, n_, 0:NT]) for n_ in range(8)], b.free, los)
        t_lst = vcopy(LST, b.ap[:, 0:NT], tok)
        banks.put(b, t_lst)
        t_nx = vcopy(NX[:, 0:1], CUM[:, 31:32], t4)
        EI = small(7 * 32).rearrange("p (o n) -> p o n", o=7)
        EF, EU = small(8), small(8).bitcast(u32)
        t5 = tt(EI, CUM.unsqueeze(1).broadcast_to([128, 7, 32]), iota[:, 0:7].unsqueeze(2).broadcast_to([128, 7, 32]), ALU.is_le, t4)
        t5 = DVE.do(lambda: v.tensor_reduce(out=EF[:, 0:7], in_=EI, axis=AX.X, op=ADD), t5)
        t5 = ts(EF[:, 0:7], EF[:, 0:7], 31.0, None, ALU.min, None, t5)
        t_ei = vcopy(EU[:, 0:7], EF[:, 0:7], t5)
        assert base[0] <= 8 * S

        GX = Pool([Place(reg(16 + 2 * i, 2), sem(f"s_gx{i}")) for i in range(3)])
        XTP = Pool([Place(reg(22 + 2 * i, 2).rearrange("p (k n) -> p k n", k=8)) for i in range(2)])
        SGP = Pool([Place(reg(26 + i, 1)) for i in range(2)])
        AVP = Pool([Place(reg(28 + i, 1)[:, 0:256].rearrange("p (k n) -> p k n", k=2)) for i in range(2)])
        YSP = Pool([Place(reg(30 + 2 * i, 2), sem(f"s_ys{i}")) for i in range(3)])
        eid = {}

        def expert(name, e):
            if e < 32:
                return lambda: A[name][e]
            return lambda: A[name][bass.ds(eid[e], 1)].rearrange("a d f -> (a d) f")

        def load_expert(i):
            if i >= 32:
                SP.wait(t_ei)

                def read():
                    eid[i] = nc.sync.value_load(EU[0:1, i - 32:i - 31], min_val=0, max_val=31)
                SP.items.append((read, None, 0))
            s = slots.get()
            for lo, name in ((0, "w_gate"), (256, "w_up")):
                src = expert(name, i)
                s.ready = dma_call(SP, s.counter, lambda s=s, lo=lo, src=src: nc.sync.dma_start(
                    k8(s.ap)[:, :, lo:lo + 256], src().rearrange("(k p) n -> p k n", p=128)), s.free)
            return s

        def load_down(i):
            s = slots.get()
            n = 2 if i < 31 else 1
            for j in range(n):
                src = expert("w_down", i + j)
                s.ready = dma_call(SP, s.counter, lambda s=s, j=j, src=src: nc.sync.dma_start(
                    s.ap[:, 2048 * j:2048 * j + 2048].rearrange("p (k n) -> p k n", k=2), src().rearrange("(k p) n -> p k n", p=128)), s.free)
            return s

        def tile_in(i):
            g = GX.get()
            tg = dma_call(GP, g.counter, lambda g=g, i=i: nc.gpsimd.indirect_dma_start(
                out=g.ap, out_offset=None, in_=Hd, in_offset=bass.IndirectOffsetOnAxis(ap=LST[:, i:i + 1], axis=0)),
                g.free, t_lst, t_hd)
            x = XTP.get()
            toks = []
            for c in range(2):
                b = banks.get()
                PE.wait(b.free, tg)
                for k in range(4):
                    tok = transpose(b.ap[:, k * 128:(k + 1) * 128], g.ap[:, (4 * c + k) * 128:(4 * c + k + 1) * 128], sig=k == 3)
                bv = b.ap.rearrange("p (k n) -> p k n", k=4)
                if c:
                    toks.append(vcopy(x.ap[:, 4 * c:4 * c + 4, :], bv, tok, x.free))
                else:
                    toks.append(act(x.ap[:, 4 * c:4 * c + 4, :], bv, ACT.Copy, tok, x.free))
                banks.put(b, toks[-1])
            GX.put(g, tok)
            return x, toks

        def tile_up(i, x, ready):
            s = load_expert(i)
            w = k8(s.ap)
            b = banks.get()
            tok = mms(b.ap, [(x.ap[:, k, :], w[:, k, :]) for k in range(8)], b.free, s.ready, ready)
            slots.put(s, tok)
            XTP.put(x, tok)
            g = SGP.get()
            t1 = act(g.ap[:, 0:256], b.ap[:, 0:256], ACT.Silu, tok, g.free)
            t2 = tt(g.ap[:, 256:512], g.ap[:, 0:256], b.ap[:, 256:512], MUL, t1, g.free)
            banks.put(b, t2)
            return g, t2

        def tile_mid(g, t2):
            b = banks.get()
            PE.wait(b.free, t2)
            for k in range(2):
                tok = transpose(b.ap[:, k * 128:(k + 1) * 128], g.ap[:, 256 + k * 128:384 + k * 128], sig=k == 1)
            SGP.put(g, tok)
            av = AVP.get()
            t3 = vcopy(av.ap, b.ap[:, 0:256].rearrange("p (k n) -> p k n", k=2), tok, av.free)
            banks.put(b, t3)
            return av, t3

        def tile_down(i, av, t3):
            if i >= 32 or i % 2 == 0:
                down[0] = load_down(i)
            s = down[0]
            o = 2048 * (i % 2) if i < 32 else 0
            w = s.ap[:, o:o + 2048].rearrange("p (k n) -> p k n", k=2)
            y = YSP.get()
            toks = []
            for c in range(2):
                b = banks.get()
                tok = mms(b.ap, [(av.ap[:, k, :], w[:, k, c * 512:(c + 1) * 512]) for k in range(2)], b.free, s.ready, t3)
                if c:
                    toks.append(vcopy(y.ap[:, 512:1024], b.ap, tok, y.free))
                else:
                    toks.append(act(y.ap[:, 0:512], b.ap, ACT.Copy, tok, y.free))
                banks.put(b, toks[-1])
            AVP.put(av, tok)
            if i >= 31 or i % 2 == 1:
                slots.put(s, tok)
            ty = dma(SC, nc.scalar, y.counter, Yd[i * 128:(i + 1) * 128, :], y.ap, toks)
            YSP.put(y, ty)
            return ty

        def modulated(src, dst, n, gain, shift, *after, each=None):
            r, tr = factor([src[:, k, :] for k in range(8)], ones, 1.0 / D, n, *after, each=each)
            toks = []
            for k in range(8):
                t1 = stt(dst[:, k, :], src[:, k, :], gain(k), r, MUL, MUL, tr)
                toks.append(act(dst[:, k, :], dst[:, k, :], ACT.Identity, t1, bias=shift(k)))
            last_r[0] = t1
            return toks

        CX = HC = reg(38, 4).rearrange("p (k n) -> p k n", k=8)
        HM, ZF, FW = reg(37, 1), reg(42, 1), reg(43, 1)
        FW1, FW2, FW3 = FW[:, 0:64], FW[:, 64:128], FW[:, 128:192]
        COS, SIN, SKB = reg(44, 1), reg(45, 1), reg(42, 2)
        t_hc = t_hm = t_cs = t_sk = None
        MAGIC = 12582912.0
        C1, C2 = 6.28125, 2.0 * math.pi - 6.28125
        C2h = float(np.float32(np.round(C2 * 2 ** 21) / 2 ** 21))
        C3 = 2.0 * math.pi - C1 - C2h

        def context_and_layers():
            nonlocal t_hc, t_hm, t_cs, t_sk
            t_cx = dma(SC, nc.scalar, dsem("d_cx"), CX, A["ctx"].rearrange("(k p) n -> p k n", p=128), t_x)
            d_f = dsem("d_f")
            dma(SC, nc.scalar, d_f, ZF[0:33, :], A["zf"])
            dma(SC, nc.scalar, d_f, FW1[0:33, :], A["hf_w1"])
            dma(SC, nc.scalar, d_f, FW2[0:64, :], A["hf_w2"])
            t_f = dma(SC, nc.scalar, d_f, FW3[0:64, :], A["hf_w3"])
            yield
            t_hc = modulated(CX, HC, 256, lambda k: G2[:, 8 + k:9 + k], lambda k: MOD[:, k, 1:2], t_cx, t_g2)
            yield
            f_last = t_g2
            src, tok_s = ZF[0:33, :], t_f
            for li, (w, kk, bn) in enumerate(((FW1, 33, "hb1"), (FW2, 64, "hb2"), (FW3, 64, "hb3"))):
                b = banks.get()
                tok = mms(b.ap[0:64, :], [(w[0:kk, :], src)], b.free, t_f, tok_s)
                u, n_ = ft[0][0:64, :], ft[1][0:64, :]
                yield
                t1 = ts(u, b.ap[0:64, :], par(bn, 0)[0:64, :], par("hfr", 0)[0:64, :], ADD, MUL, tok, f_last)
                banks.put(b, t1)
                t2 = ts(n_, u, 1.0 / (2.0 * math.pi), MAGIC, MUL, ADD, t1)
                t3 = ts(n_, n_, -MAGIC, None, ADD, None, t2)
                t4 = stt(u, n_, -C1, u, MUL, ADD, t3)
                t5 = stt(u, n_, -C2h, u, MUL, ADD, t4)
                t6 = stt(u, n_, -C3, u, MUL, ADD, t5)
                t7 = ts(u, u, 3.1415925, -3.1415925, ALU.min, ALU.max, t6)
                hm = HM[0:64, :]
                yield
                f_last = tok_s = act(hm, u, ACT.Sin, t7, tok)
                src = hm
                yield
            t_hm = tok_s
            d_cs = dsem("d_cs")
            dma(SC, nc.scalar, d_cs, COS, A["rope"][0])
            t_cs = dma(SC, nc.scalar, d_cs, SIN, A["rope"][1])
            t_sk = dma(SC, nc.scalar, dsem("d_sk"), SKB, A["skip"], t_hm)

        down = [None]

        def run_tiles(lo, hi, other=()):
            other = iter(other)
            ins = {lo: tile_in(lo), lo + 1: tile_in(lo + 1)}
            ups = {lo: tile_up(lo, *ins.pop(lo))}
            for i in range(lo, hi):
                if i + 2 < hi:
                    ins[i + 2] = tile_in(i + 2)
                mid = tile_mid(*ups.pop(i))
                if i + 1 < hi:
                    ups[i + 1] = tile_up(i + 1, *ins.pop(i + 1))
                tile_down(i, *mid)
                if i % 2:
                    next(other, None)

        run_tiles(0, 32, context_and_layers())
        engines = (PE, DVE, SC, GP, SP)
        pools = (banks, slots, GX, XTP, SGP, AVP, YSP)
        kept = [(p_, list(p_.q), [(x, x.free, x.counter) for x in p_.q]) for p_ in pools]
        inner_sems = []
        SC.wait(t_zd)
        for e in engines:
            e.wait(t_nx)
            inner_sems.append(sem(f"s_more{len(inner_sems)}"))
            e.enter(inner_sems[-1])
        counters = []
        for pool, prefix in ((slots, "w"), (GX, "gx"), (YSP, "ys")):
            for n_, x in enumerate(pool.q):
                x.counter = Counter(sem(f"s_more_{prefix}{n_}"))
                counters.append(x.counter)
        run_tiles(32, NT)
        ends = [e.last() for e in engines] + [(x.sem, x.n) for x in counters if x.n]
        for e in engines:
            e.wait(ends)
            e.leave(NX[0:1, 0:1])
        for pool, q, places in kept:
            pool.q = q
            for x, free, counter in places:
                x.free, x.counter = free, counter
        t_yd = [p_.free for p_ in YSP.q]

        for i in range(4):
            more = Place(reg(8 + 2 * i, 2), sem(f"s_gy{i}"))
            more.free = [t_hd]
            GX.q.append(more)
        got = {}

        def fetch(q):
            got[q] = g0, g1 = GX.get(), GX.get()
            for kk, g in ((0, g0), (1, g1)):
                g.ready = dma_call(GP, g.counter, lambda g=g, kk=kk, q=q: nc.gpsimd.indirect_dma_start(
                    out=g.ap, out_offset=None, in_=Yd, in_offset=bass.IndirectOffsetOnAxis(ap=PU[:, 4 * kk + q:4 * kk + q + 1], axis=0)),
                    g.free, t_yd, t_pu)

        for q in range(3):
            fetch(q)
        def combine():
            nonlocal t_x
            for q in R4:
                g0, g1 = got[q]
                t1 = ts(g0.ap, g0.ap, WK[:, 0, q:q + 1], None, MUL, None, g0.ready, twk)
                t2 = stt(g0.ap, g1.ap, WK[:, 1, q:q + 1], g0.ap, MUL, ADD, t1, g1.ready)
                GX.put(g1, t2)
                for c in range(2):
                    b = banks.get()
                    PE.wait(b.free, t2)
                    for k in range(4):
                        tok = transpose(b.ap[:, k * 128:(k + 1) * 128], g0.ap[:, (4 * c + k) * 128:(4 * c + k + 1) * 128], sig=k == 3)
                    xs = X[:, 4 * c:4 * c + 4, q * 128:(q + 1) * 128]
                    t_x = tt(xs, xs, b.ap.rearrange("p (k n) -> p k n", k=4), ADD, tok)
                    banks.put(b, t_x)
                GX.put(g0, tok)
                if q == 0:
                    fetch(3)
                yield

        t_moe = [PE.last(), DVE.last(), SC.last(), t_yd]
        w2 = A["w_in_2"]
        KK = reg(0, 2)[:, 0:768]
        VV = reg(2, 2)[:, 0:768].rearrange("p (k n) -> p k n", n=128)
        QQ = tiles(38, 4)
        t_kk = t_vv = hc_free = None
        t_qq = [None] * 4

        def head_norm2(dst, b, tok, n, gain):
            t0 = act(dst, b.ap[:, 0:n], ACT.Copy, tok, t_x, hc_free)
            banks.put(b, t0)
            r, tr = factor([dst], blk, 1.0 / 64, n, t0)
            last_r[0] = stt(dst, dst, gain, r, MUL, MUL, tr)
            return last_r[0]

        def rotate(dst, t1):
            br = banks.get()
            tok = mms(br.ap, [(cst("rot"), dst)], br.free, t1)
            rt = tmp[0]
            t2 = tt(rt, br.ap, SIN, MUL, tok, t_cs, factor_sq[0])
            banks.put(br, t2)
            t3 = tt(dst, dst, COS, MUL, t2)
            factor_sq[0] = tt(dst, dst, rt, ADD, t3)
            return factor_sq[0]

        s_kv = load_cols(w2, 4096, 4352)

        def keys_queries():
            nonlocal t_h, t_kk, t_vv, hc_free
            s = s_kv
            w = s.ap[:, 0:2048].rearrange("p (k n) -> p k n", k=8)
            b, b2 = banks.get(), banks.get()
            tok = mms(b.ap[:, 0:256], [(w[:, k, 0:128], HC[:, k, :]) for k in range(8)], b.free, s.ready, t_hc)
            PE.wait(b2.free)
            for c in range(2):
                hc_free = mms(b2.ap[:, c * 128:(c + 1) * 128], [(HC[:, k, c * 128:(c + 1) * 128], w[:, k, 128:256]) for k in range(8)])
            yield
            yield from combine()
            t_k2 = head_norm2(KK[:, 512:768], b, tok, 256, par("kg2", 0))
            t_vc = act(VV[:, 4:6, :], b2.ap[:, 0:256].rearrange("p (k n) -> p k n", n=128), ACT.Copy, hc_free, t_moe, t_x)
            banks.put(b2, t_vc)
            t_h = modulated(X, H, S, lambda k: G2[:, k:k + 1], lambda k: MOD[:, k, 0:1], t_x, t_g2)
            yield
            b = banks.get()
            tok = mms(b.ap, [(w[:, k, 0:128], H[:, k, :], t_h[k]) for k in range(8)], b.free)
            t_k1 = head_norm2(KK[:, 0:512], b, tok, 512, par("kg2", 0))
            yield
            b = banks.get()
            PE.wait(b.free)
            for c in range(4):
                tok = mms(b.ap[:, c * 128:(c + 1) * 128], [(H[:, k, c * 128:(c + 1) * 128], w[:, k, 128:256]) for k in range(8)])
            slots.put(s, tok)
            t1 = act(VV[:, 0:4, :], b.ap.rearrange("p (k n) -> p k n", n=128), ACT.Copy, tok, t_moe)
            t_vv = [t_vc, t1]
            banks.put(b, t1)
            t_kk = [rotate(KK[:, 0:512], t_k1), t_k2]
            yield
            s = load_cols(w2, 1536, 2048)
            held, normed = [], []
            for c in range(6):
                if c < 4:
                    held.append(proj(s, c, t_h))
                if 1 <= c < 5:
                    normed.append(head_norm2(QQ[:, c - 1, :], *held[c - 1], 512, par("qg2", 0)))
                if c >= 2:
                    t_qq[c - 2] = rotate(QQ[:, c - 2, :], normed[c - 2])
                yield
            slots.put(s, held[-1][1])

        KF = tiles(4, 18)
        SB_, DB_ = tiles(22, 4), tiles(26, 4)
        FW4 = reg(30, 4)
        d_f4 = dsem("d_f4")
        t_f4 = dma(SP, nc.sync, d_f4, FW4[0:64, :], A["hf_w4"], t_moe)
        s_f2 = load([(0, 4096, lambda ap: ap.rearrange("p (t k n) -> p t k n", t=2, k=4), A["dft"][2:4].rearrange("t (k p) n -> p t k n", p=128))], got[0][1].ready)
        s_f1 = load([(0, 4096, lambda ap: ap.rearrange("p (t k n) -> p t k n", t=2, k=4), A["dft"][0:2].rearrange("t (k p) n -> p t k n", p=128))], got[2][1].ready)
        FC, FS = k4(s_f1.ap[:, 0:2048]), k4(s_f1.ap[:, 2048:4096])
        FST, DEC = k4(s_f2.ap[:, 0:2048]), k4(s_f2.ap[:, 2048:4096])
        ft += [reg(36, 1), ft[1]]
        kf_tok = []
        sb_free = None

        def filters():
            nonlocal sb_free
            ab_free = [t_hm, t_hm]
            inv_free = ab_free
            for o in range(2):
                td = [None] * 4
                for c in range(4):
                    yield
                    bf, bb = banks.get(), banks.get()
                    lh = HM[0:64, c * 128:(c + 1) * 128]
                    t0 = mms(bf.ap, [(lh, FW4[0:64, o * 1024:o * 1024 + 512])], bf.free, t_hm, t_f4)
                    t1 = mms(bb.ap, [(lh, FW4[0:64, o * 1024 + 512:o * 1024 + 1024])], bb.free)
                    fw, bw = SB_[:, c, :], DB_[:, c, :]
                    t2 = tt(fw, bf.ap, DEC[:, c, :], MUL, t0, s_f2.ready, sb_free, t_moe)
                    t3 = tt(bw, bb.ap, DEC[:, c, :], MUL, t1, sb_free)
                    banks.put(bf, t2)
                    banks.put(bb, t3)
                    if c == 0:
                        t3 = DVE.do(lambda bw=bw: v.memset(bw[0:1, :], 0.0), t3)
                    td[c] = [t2, t3]
                b = banks.get()
                PE.wait(b.free)
                nn = 0
                for c in range(4):
                    for x in (SB_, DB_):
                        ab = ft[nn % 2]
                        tk = act(ab, x[:, c, :], ACT.Abs, td[c], ab_free[nn % 2])
                        ab_free[nn % 2] = tok = PE.do(lambda ab=ab, nn=nn, b=b: t.matmul(b.ap, ones, ab, start=nn == 0, stop=nn == 7), tk)
                        nn += 1
                inv = ft[2]
                t1 = ts(ft[3], b.ap, EPS, None, ADD, None, tok, inv_free)
                banks.put(b, t1)
                t_l = act(ft[2], ft[3], ACT.Ln, t1)
                t_l = act(ft[2], ft[2], ACT.Exp, t_l, scale=-1.0)
                t_l = stt(ft[3], ft[3], -1.0, ft[2], MUL, MUL, t_l)
                t_inv = stt(ft[2], ft[3], 2.0, ft[2], ADD, MUL, t_l)
                tsd = []
                for c in range(4):
                    t1 = tt(DB_[:, c, :], SB_[:, c, :], DB_[:, c, :], SUB, td[c], tk)
                    tsd.append(stt(SB_[:, c, :], SB_[:, c, :], 2.0, DB_[:, c, :], MUL, SUB, t1))
                kc0 = 9 * o
                skip = SKB[:, o * 512:(o + 1) * 512]
                for f in range(4):
                    yield
                    b = banks.get()
                    tok = mms(b.ap, [(FC[:, k, f * 128:(f + 1) * 128], SB_[:, k, :]) for k in range(4)], b.free, tsd, s_f1.ready)
                    kc = KF[:, kc0 + f, :]
                    t1 = tt(kc, b.ap, inv, MUL, tok, t_inv, t_x)
                    banks.put(b, t1)
                    t2 = tt(kc, kc, skip, ADD, t1, t_sk)
                    t3 = ts(kc, kc, 2.0 / 1024, None, MUL, None, t2)
                    kf_tok.append(t3)
                    b = banks.get()
                    tok = mms(b.ap, [(FS[:, k, f * 128:(f + 1) * 128], DB_[:, k, :]) for k in range(4)], b.free)
                    ks = KF[:, kc0 + 4 + f, :]
                    t4 = tt(ks, b.ap, inv, MUL, tok)
                    banks.put(b, t4)
                    t5 = ts(ks, ks, 2.0 / 1024, None, MUL, None, t4)
                    kf_tok.append(t5)
                    if f == 0:
                        b = banks.get()
                        tok = mms(b.ap, [(FS[:, k, 0:128], SB_[:, k, :]) for k in range(4)], b.free)
                        kx = KF[:, kc0 + 8, :]
                        t6 = vcopy(kx, kc, t3)
                        t7 = ts(kc[0:1, :], kc[0:1, :], 0.5, None, MUL, None, t6)
                        t8 = DVE.do(lambda ks=ks: v.memset(ks[0:1, :], 0.0), t5)
                        t9 = tt(kx[0:1, :], b.ap[0:1, :], inv[0:1, :], MUL, tok, t6)
                        banks.put(b, t9)
                        t9 = tt(kx[0:1, :], kx[0:1, :], skip[0:1, :], ADD, t9)
                        t9 = ts(kx[0:1, :], kx[0:1, :], 1.0 / 1024, None, MUL, None, t9)
                        kf_tok.extend([t7, t8, t9])
                sb_free = tok
                inv_free = [t5, t9]
                yield

        def chain(*gens):
            for g in gens:
                yield from g

        keys_, filters_ = keys_queries(), filters()
        beside((next(keys_) for _ in range(5)), filters_, FA)
        beside(keys_, filters_, FB)
        drain(filters_)

        VF, X1 = tiles(22, 4), tiles(26, 4)
        UT, YC, YS = tiles(30, 4), tiles(34, 4), tiles(42, 4)

        def short(dst, c, tile, b, tok, *after):
            w = lambda j: par("hcw", j * 12 + c)
            raw = tmp[c % 2]
            t0 = act(raw, b.ap, ACT.Copy, tok, factor_sq[c % 2])
            banks.put(b, t0)
            t1 = ts(dst, raw, w(1), par("hcb", c), MUL, ADD, t0, *after)
            t2 = stt(dst[:, 1:S], raw[:, 0:S - 1], w(0), dst[:, 1:S], MUL, ADD, t1)
            t3 = stt(dst[:, 0:S - 1], raw[:, 1:S], w(2), dst[:, 0:S - 1], MUL, ADD, t2)
            factor_sq[c % 2] = t3
            return t3

        def hy_part(dst, i, *after):
            s = load_cols(w2, i * 512, i * 512 + 512)
            toks = []
            for c in range(4):
                b, tok = proj(s, c, t_h)
                toks.append(short(dst[:, c, :], i * 4 + c, c, b, tok, *after))
            slots.put(s, tok)
            return toks

        def to_tokens(dst, src, ready, *after):
            toks = []
            for q in range(4):
                b = banks.get()
                PE.wait(b.free, ready)
                for c in range(4):
                    tok = transpose(b.ap[:, c * 128:(c + 1) * 128], src[:, c, q * 128:(q + 1) * 128], sig=c == 3)
                toks.append(act(dst[:, q, :], b.ap, ACT.Copy, tok, *after))
                banks.put(b, toks[-1])
            return toks, tok

        def spectrum(U, ready, o, *after):
            toks = []
            for f in range(4):
                bc, bs = banks.get(), banks.get()
                tc_ = mms(bc.ap, [(FC[:, k, f * 128:(f + 1) * 128], U[:, k, :]) for k in range(4)], bc.free, ready)
                ts_ = mms(bs.ap, [(FS[:, k, f * 128:(f + 1) * 128], U[:, k, :]) for k in range(4)], bs.free)
                kc, ks = KF[:, 9 * o + f, :], KF[:, 9 * o + 4 + f, :]
                kx = KF[:, 9 * o + 8, :] if f == 0 else kc
                yc, ys, p = YC[:, f, :], YS[:, f, :], tmp[4]
                t1 = tt(yc, bc.ap, kc, MUL, tc_, kf_tok, *after)
                t2 = tt(p, bs.ap, ks, MUL, ts_, last_p[0])
                t3 = tt(yc, yc, p, SUB, t1, t2)
                t4 = tt(ys, bc.ap, ks, MUL, t3)
                t5 = tt(p, bs.ap, kx, MUL, t4)
                banks.put(bc, t4)
                banks.put(bs, t5)
                t6 = tt(ys, ys, p, ADD, t5)
                last_p[0] = t6
                toks += [t3, t6]
            return toks, ts_

        last_p = [last_r[0]]
        t_vf = hy_part(VF, 0, sb_free)
        t_x1 = hy_part(X1, 1, sb_free)
        t_ut, _ = to_tokens(UT, VF, t_vf, sb_free)
        t_y, t_u_free = spectrum(UT, t_ut, 0, sb_free)
        t_x1t, t_x1free = to_tokens(VF, X1, t_x1, t_ut[-1])
        t_y1 = []
        for q in range(4):
            b = banks.get()
            tok = mms(b.ap, [(FC[:, k, q * 128:(q + 1) * 128], YC[:, k, :]) for k in range(4)] +
                      [(FST[:, k, q * 128:(q + 1) * 128], YS[:, k, :]) for k in range(4)], b.free, t_y)
            t1 = tt(UT[:, q, :], b.ap, VF[:, q, :], MUL, tok, t_x1t, t_u_free)
            banks.put(b, t1)
            t_y1.append(t1)
        t_inv0 = tok
        t_y, t_u_free = spectrum(UT, t_y1, 1, t_inv0)
        t_x2 = hy_part(X1, 2, t_x1free)
        HY = X1
        t_hy = []
        for c in range(4):
            b = banks.get()
            tok = mms(b.ap, [(YC[:, k, c * 128:(c + 1) * 128], FC[:, k, :]) for k in range(4)] +
                      [(YS[:, k, c * 128:(c + 1) * 128], FST[:, k, :]) for k in range(4)], b.free, t_y)
            t1 = tt(HY[:, c, :], HY[:, c, :], b.ap, MUL, tok, t_x2[c])
            banks.put(b, t1)
            t_hy.append(t1)
        slots.put(s_f1, tok)
        slots.put(s_f2, tok)

        GA2, GB2 = tiles(30, 8), tiles(18, 8)
        t_ga2, t_gb2 = [None] * 8, [None] * 8
        t_hy.append(tok)

        def both_gates():
            for dst, lo, toks in ((GA2, 2048, t_ga2), (GB2, 3072, t_gb2)):
                for half in range(2):
                    s = load_cols(w2, lo + half * 512, lo + half * 512 + 512)
                    w = k8(s.ap)
                    for c in range(4):
                        b = banks.get()
                        pairs = [(w[:, k, c * 128:(c + 1) * 128], H[:, k, :]) for k in range(8)]
                        mms(b.ap, pairs[0:4], b.free, s.ready, t_h, stop=False)
                        yield
                        tok = mms(b.ap, pairs[4:8], start=False)
                        i = half * 4 + c
                        toks[i] = act(dst[:, i, :], b.ap, ACT.Sigmoid, tok, t_hy)
                        banks.put(b, toks[i])
                        yield
                    slots.put(s, tok)

        A2 = tiles(14, 4)
        PR = [reg(10, 2)[:, 0:768], reg(12, 2)[:, 0:768]]
        PT = reg(4, 6).rearrange("p (k n) -> p k n", k=6)
        STT = reg(42, 1)
        t_a2 = [None] * 8

        def attention2():
            steps = [(j, g, q) for j in range(4) for g in range(2) for q in range(4)]
            scaled = [None] * 32
            pr_free = [t_hy, t_hy]
            pt_free = t_hy
            ready = []
            for it in range(33):
                if it < 32:
                    j, g, q = steps[it]
                    po = 64 * g
                    c = (it % 2) * 8
                    st = lambda i, c=c: STT[:, c + i:c + i + 1]
                    Pb = PR[it % 2]
                    lq = QQ[po:po + 64, j, q * 128:(q + 1) * 128]
                    ba, bb = banks.get(), banks.get()
                    PE.wait(ba.free, bb.free)
                    t0 = mms(ba.ap, [(lq, KK[po:po + 64, 0:512])], t_qq[j], t_kk)
                    t1 = mms(bb.ap[:, 0:256], [(lq, KK[po:po + 64, 512:768])])
                    m0 = DVE.do(lambda st=st, ba=ba: v.tensor_reduce(out=st(0), in_=ba.ap, axis=AX.X, op=ALU.max), t0, pr_free[it % 2])
                    m1 = DVE.do(lambda st=st, bb=bb: v.tensor_reduce(out=st(1), in_=bb.ap[:, 0:256], axis=AX.X, op=ALU.max), t1)
                    m2 = tt(st(2), st(0), st(1), ALU.max, m0, m1)
                    m3 = ts(st(3), st(2), -0.125, None, MUL, None, m2)
                    e0 = act(Pb[:, 0:512], ba.ap, ACT.Exp, m3, pr_free[it % 2], bias=st(3), scale=0.125, acc=st(4))
                    e1 = act(Pb[:, 512:768], bb.ap[:, 0:256], ACT.Exp, m3, bias=st(3), scale=0.125, acc=st(5))
                    banks.put(ba, e0)
                    banks.put(bb, e1)
                    m4 = tt(st(6), st(4), st(5), ADD, e0, e1)
                    m5 = DVE.do(lambda st=st: v.reciprocal(st(7), st(6)), m4)
                    scaled[it] = ts(Pb, Pb, st(7), None, MUL, None, m5)
                yield
                if it:
                    j, g, q = steps[it - 1]
                    po, h = 64 * g, 2 * j + g
                    Pb = PR[(it - 1) % 2]
                    ba, bb = banks.get(), banks.get()
                    PE.wait(ba.free, bb.free, scaled[it - 1])
                    for i in range(6):
                        o = (ba, bb)[i // 4].ap[:, (i % 4) * 128:(i % 4) * 128 + 128]
                        tok = transpose(o, Pb[:, i * 128:(i + 1) * 128], sig=i == 5)
                    pr_free[(it - 1) % 2] = tok
                    r0 = act(PT[:, 0:4, q * 128:(q + 1) * 128], ba.ap.rearrange("p (k n) -> p k n", k=4), ACT.Copy, tok, pt_free)
                    r1 = vcopy(PT[:, 4:6, q * 128:(q + 1) * 128], bb.ap[:, 0:256].rearrange("p (k n) -> p k n", k=2), tok, pt_free)
                    banks.put(ba, r0)
                    banks.put(bb, r1)
                    ready += [r0, r1]
                    if q == 3:
                        b = banks.get()
                        pt_free = mms(b.ap[po:po + 64, :], [(VV[:, i, po:po + 64], PT[:, i, :]) for i in range(6)], b.free, ready, t_vv)
                        t_a2[h] = act(A2[po:po + 64, j, :], b.ap[po:po + 64, :], ACT.Copy, pt_free, t_hy)
                        banks.put(b, t_a2[h])
                        ready = []

        mix(attention2(), both_gates())

        t_m = []
        drain(merge(A["w_attn"], A["w_hy"], A2, HY, t_a2, t_hy, t_ga2, t_gb2, GA2, GB2, t_m))
        t_x = out_proj(A["w_out_2"], GA2, t_m,
                       lambda c, b, tok: stt(X[:, c, :], b.ap, MOD[:, 16 + c, 0:1], X[:, c, :], MUL, ADD, tok))

        t_ring = [PE.last(), DVE.last(), SC.last()]
        ring.close()
        HR = [sb(f"hr{i}", 8 * S, f32r, None, "right")[:, :].rearrange("p (k n) -> p k n", k=8) for i in range(2)]
        raw = Pool([Place(sb(f"raw{i}", 2048, f32, None, "right")[:, :], sem(f"s_rw{i}")) for i in range(3)])
        for p_ in raw.q:
            p_.free = [t_x]
        H2 = tiles(38, 8)
        early.close()
        parts = Pool([Place([sb(f"part{i}{p}", 2048, f32r)[:, :] for p in range(2)]) for i in range(2)])
        GTMP = Pool([Place(sb(f"gt{i}", S)[:, :], sem(f"s_gt{i}")) for i in range(4)])
        for p_ in parts.q:
            p_.free = [t_x]
        window = ExitStack()
        WA = sb("window", 39 * S, f32, window)

        area[0:2] = [39, WA]
        def load_split(src, k, on=None):
            r = raw.get()
            tok = dma(SP, nc.sync, r.counter, r.ap.rearrange("p (k n) -> p k n", k=k), src, r.free)
            s = parts.get()
            s.ready = split(s.ap[0], s.ap[1], r.ap, tok, s.free, on=on)
            raw.put(r, s.ready)
            return s, [x.rearrange("p (k n) -> p k n", k=k) for x in s.ap]

        SPILL, RATIO = 24, (0.7, 0.6)
        spilled = list(range(SPILL))
        rest_ = list(range(SPILL, 32))
        sequence = []
        while spilled or rest_:
            if rest_:
                sequence.append(rest_.pop(0))
            for _ in range(2 if len(spilled) > len(rest_) else 1):
                if spilled:
                    sequence.append(spilled.pop(0))
        order = [("q", i, 0) for i in range(8)]
        order += [("u", c, h) for c in range(SPILL) for h in range(2)]
        for n_, c in enumerate(sequence):
            if n_ == 0:
                order += [("u", c, 0), ("u", c, 1)]
            if n_ + 1 < 32 and sequence[n_ + 1] >= SPILL:
                order += [("u", sequence[n_ + 1], 0), ("u", sequence[n_ + 1], 1)]
            order += [("v", c, 0), ("v", c, 1)]
        ahead = []

        def look_ahead():
            while order and len(ahead) < 2:
                which, c, half = order.pop(0)
                if which == "q":
                    sp_ = load_split(A["wq"][:, c * 256:c * 256 + 256].rearrange("(k p) n -> p k n", p=128), 8)
                elif which == "u":
                    sp_ = load_split(A["u"][2 * c + half], 8, GP if c < SPILL else None)
                else:
                    vs = A["v"][c * 512:(c + 1) * 512, :].rearrange("(k p) n -> p k n", p=128)
                    sp_ = load_split(vs[:, :, half * 512:half * 512 + 512], 4)
                ahead.append((which, c, sp_))

        def next_slot(which_, c_):
            look_ahead()
            which, c, sp_ = ahead.pop(0)
            assert (which, c) == (which_, c_)
            return sp_

        r_, tr_ = factor([X[:, k, :] for k in range(8)], ones, 1.0 / D, S, each=t_x)
        look_ahead()
        t_hr = []
        for k in range(9):
            if k < 8:
                t1 = stt(H2[:, k, :], X[:, k, :], GF2[:, k:k + 1], r_, MUL, MUL, tr_, t_ring)
                hi_ = act(HR[0][:, k, :], H2[:, k, :], ACT.Identity, t1, bias=MOD[:, 24 + k, 0:1])
            if k:
                t_hr.append(stt(HR[1][:, k - 1, :], H2[:, k - 1, :], MOD[:, 23 + k, 0:1], HR[0][:, k - 1, :].bitcast(f32), ADD, SUB, hi_before))
            hi_before = hi_
        last_r[0] = t1
        t_early = [t_ring, t_hr]
        for p_ in GTMP.q:
            p_.free = [t_early]

        def from_features(s, wh, wl, j):
            b = banks.get()
            js = slice(j * 128, (j + 1) * 128)
            return b, mms(b.ap, [(*p, t_hr[k]) for k in range(8)
                                 for p in three(wh[:, k, js], wl[:, k, js], HR[0][:, k, :], HR[1][:, k, :])], b.free, s.ready)

        QP = tiles(0, 16)
        t_qp = [None] * 16
        KEY = TMP[:, 0:2048].rearrange("p (i n) -> p i n", i=16)
        t_key = dma(SC, nc.scalar, dsem("d_key"), KEY, A["keys"].rearrange("p (i n) -> p i n", i=16), t_early)
        for i in range(8):
            s, (wh, wl) = next_slot("q", i)
            for j in range(2):
                b, tok = from_features(s, wh, wl, j)
                t_qp[2 * i + j] = act(QP[:, 2 * i + j, :], b.ap, ACT.Copy, tok, t_early)
                banks.put(b, t_qp[2 * i + j])
            parts.put(s, tok)
        SC1, SC2 = reg(16, 4).rearrange("p (i n) -> p i n", i=16), reg(20, 4).rearrange("p (i n) -> p i n", i=16)
        CD1, CD2 = reg(16, 4).rearrange("p (h k j) -> p h k j", h=8, k=16), reg(20, 4).rearrange("p (h k j) -> p h k j", h=8, k=16)
        EQ = reg(24, 4).rearrange("p (h k j) -> p h k j", h=8, k=16)
        SMALL = reg(28, 6)
        VAL = SMALL[:, 0:256].rearrange("p (i k) -> p i k", i=16)
        IDX = SMALL[:, 256:512].bitcast(u32).rearrange("p (i k) -> p i k", i=16)
        IDF = SMALL[:, 512:768].rearrange("p (i k) -> p i k", i=16)
        BST = SMALL[:, 768:896].rearrange("p (h k) -> p h k", h=8)
        POS = SMALL[:, 896:1024].bitcast(u32).rearrange("p (h k) -> p h k", h=8)
        PHI = SMALL[:, 1024:1152].bitcast(u32).rearrange("p (h k) -> p h k", h=8)
        PLO = SMALL[:, 1152:1280].bitcast(u32).rearrange("p (h k) -> p h k", h=8)
        PHF = SMALL[:, 1280:1408].rearrange("p (h k) -> p h k", h=8)
        PLF = SMALL[:, 1408:1536].rearrange("p (h k) -> p h k", h=8)
        I1 = SMALL[:, 1536:1664].rearrange("p (h k) -> p h k", h=8)
        I2 = SMALL[:, 1664:1792].rearrange("p (h k) -> p h k", h=8)
        GW = SMALL[:, 1792:1920].rearrange("p (h k) -> p h k", h=8)
        GS = SMALL[:, 1920:1928]
        GR = SMALL[:, 1928:1936]
        I1T, I2T = (reg(34, 1).bitcast(bf16)[:, i * 512:(i + 1) * 512] for i in range(2))
        GT = [reg(35, 2).bitcast(bf16)[:, i * 512:(i + 1) * 512] for i in range(3)]
        IT = [I1, I2, GW]
        iota16 = iota[:, 0:16].unsqueeze(1).broadcast_to([128, 128, 16])
        t_it = []

        def best_pairs():
            t_s_free = t_early
            t_tr_free = None
            for q in range(4):
                t_sc = []
                for g in range(4):
                    b = banks.get()
                    PE.wait(b.free, t_key)
                    for i in range(4):
                        ii = g * 4 + i
                        tok = mms(b.ap[:, i * 128:(i + 1) * 128], [(QP[:, ii, q * 128:(q + 1) * 128], KEY[:, ii, :])], t_qp[ii])
                    t_sc.append(act(SC1[:, g * 4:g * 4 + 4, :], b.ap.rearrange("p (i n) -> p i n", i=4), ACT.Copy, tok, t_s_free))
                    banks.put(b, t_sc[-1])

                def top16(n, src, alt, val, idx, ready, *after):
                    steps = [lambda i: v.max(val(i)[:, 0:8], src(i)),
                             lambda i: v.max_index(idx(i)[:, 0:8], val(i)[:, 0:8], src(i)),
                             lambda i: v.match_replace(alt(i), val(i)[:, 0:8], src(i), -3.0e38),
                             lambda i: v.max(val(i)[:, 8:16], alt(i)),
                             lambda i: v.max_index(idx(i)[:, 8:16], val(i)[:, 8:16], alt(i))]
                    before = [[ready, *after]] * n
                    for step in steps:
                        now = []
                        for i in range(n):
                            now.append(DVE.do(lambda step=step, i=i: step(i), before[i]))
                            if i % 8 == 7:
                                yield
                        before = now
                    return before[-1]

                DVE.wait(DVE.last())
                t1 = yield from top16(16, lambda i: SC1[:, i, :], lambda i: SC2[:, i, :], lambda i: VAL[:, i, :], lambda i: IDX[:, i, :], t_sc)
                t2 = vcopy(IDF, IDX, t1)
                yield
                V4 = VAL.rearrange("p (h s) k -> p h s k", s=2)
                F4 = IDF.rearrange("p (h s) k -> p h s k", s=2)
                t3 = None
                for h in range(8):
                    t3 = tt(CD1[:, h, :, :], V4[:, h, 0, :].unsqueeze(2).broadcast_to([128, 16, 16]),
                            V4[:, h, 1, :].unsqueeze(1).broadcast_to([128, 16, 16]), ADD, t1)
                fl = lambda ap: ap.rearrange("p k j -> p (k j)")
                t4 = yield from top16(8, lambda h: fl(CD1[:, h, :, :]), lambda h: fl(CD2[:, h, :, :]), lambda h: BST[:, h, :],
                           lambda h: POS[:, h, :], t3)
                t_s_free = t4
                yield
                t5 = DVE.do(lambda: v.tensor_scalar(out=PHI, in0=POS, scalar1=4, scalar2=None, op0=ALU.logical_shift_right), t4)
                t6 = DVE.do(lambda: v.tensor_scalar(out=PLO, in0=POS, scalar1=15, scalar2=None, op0=ALU.bitwise_and), t4)
                t5 = vcopy(PHF, PHI, t5)
                t6 = vcopy(PLF, PLO, t6)
                t9 = []
                for side, (pf, dst) in enumerate(((PHF, I1), (PLF, I2))):
                    pfl = pf.rearrange("p h k -> p (h k)").unsqueeze(2).broadcast_to([128, 128, 16])
                    eq = EQ.rearrange("p h k j -> p (h k) j")
                    t7 = tt(eq, pfl, iota16, ALU.is_equal, t5, t6, t9[-1] if t9 else None)
                    for h in range(8):
                        t8 = tt(EQ[:, h, :, :], EQ[:, h, :, :], F4[:, h, side, :].unsqueeze(1).broadcast_to([128, 16, 16]), MUL, t7, t2)
                    yield
                    t9.append(DVE.do(lambda dst=dst, eq=eq: v.tensor_reduce(out=dst.rearrange("p h k -> p (h k)"), in_=eq, axis=AX.X, op=ADD), t8, t_tr_free))
                u1 = tt(GW, BST, BST[:, :, 0:1].broadcast_to([128, 8, 16]), SUB, t4, t_tr_free)
                u2 = act(GW, GW, ACT.Exp, u1)
                u3 = DVE.do(lambda: v.tensor_reduce(out=GS, in_=GW, axis=AX.X, op=ADD), u2)
                u4 = DVE.do(lambda: v.reciprocal(GR, GS), u3)
                u5 = tt(GW, GW, GR.unsqueeze(2).broadcast_to([128, 8, 16]), MUL, u4)
                b = banks.get()
                PE.wait(b.free, t9, u5)
                for i, src in enumerate(IT):
                    tok = transpose(b.ap[:, i * 128:(i + 1) * 128], src.rearrange("p h k -> p (h k)"), sig=i == 2)
                t_tr_free = tok
                qs = slice(q * 128, (q + 1) * 128)
                t_it.append(act(I1T[:, qs], b.ap[:, 0:128], ACT.Copy, tok, t_x))
                t_it.append(act(I2T[:, qs], b.ap[:, 128:256], ACT.Copy, tok))
                rest = EQ[:, 0:1, 0:8, :].rearrange("p h k j -> p (h k j)")
                w1 = vcopy(GT[0][:, qs], b.ap[:, 256:384], tok, t9, t_it)
                w2_ = tt(rest, b.ap[:, 256:384], GT[0][:, qs], SUB, w1)
                w3 = vcopy(GT[1][:, qs], rest, w2_)
                w4 = tt(rest, rest, GT[1][:, qs], SUB, w3)
                t_it.append(vcopy(GT[2][:, qs], rest, w4))
                banks.put(b, t_it[-1], t_it[-2], w2_)
                yield

        WS = [reg(0, 8), reg(8, 8)]
        OB = [[reg(16 + 8 * r, 8).bitcast(bf16)[:, 2048 * i:2048 * i + 2048].rearrange("p (i t) -> p i t", t=16) for i in range(4)]
              for r in range(2)]
        O1 = reg(32, 2).bitcast(bf16)[:, 0:2048].rearrange("p (i t) -> p i t", t=16)
        IOX = reg(37, 2).bitcast(bf16)[:, 0:2048].rearrange("p (i t) -> p i t", t=16)
        d_ws = [dsem("d_ws0"), dsem("d_ws1")]
        t_w = []

        def weights():
            t_iox = vcopy(IOX, iota.unsqueeze(2).broadcast_to([128, 128, 16]), t_it, DVE.last(), t_early)
            ob_free = [None, None]
            ws_free = [None, None]
            for g in range(32):
                tb_, wv = g // 2, WS[(g // 2) % 2].rearrange("p (i t) -> p i t", t=32)
                o2, oa, ob, oc = OB[g % 2]
                ns = slice(g * 16, g * 16 + 16)
                rows = lambda ap: ap[:, ns].unsqueeze(1).broadcast_to([128, 128, 16])
                c0 = DVE.last()
                c1 = tt(o2, IOX, rows(I2T), ALU.is_equal, t_iox, t_it, ob_free[g % 2])
                c2 = tt(O1, IOX, rows(I1T), ALU.is_equal, c0)
                yield
                c3 = [tt(x, O1, rows(GT[i]), MUL, c2) for i, x in enumerate((oa, ob, oc))]
                yield
                for f in range(4):
                    b = banks.get()
                    PE.wait(b.free, c1, c3)
                    for i in range(4):
                        n = f * 4 + i
                        tok = mms(b.ap[:, i * 128:(i + 1) * 128], [(o2[:, :, n], x[:, :, n]) for x in (oa, ob, oc)])
                    h0 = (g % 2) * 16 + f * 4
                    t1 = act(wv[:, :, h0:h0 + 4].rearrange("p i t -> p t i"), b.ap.rearrange("p (t i) -> p t i", t=4), ACT.Copy,
                             tok, ws_free[tb_ % 2])
                    banks.put(b, t1)
                ob_free[g % 2] = tok
                if g % 2:
                    ws_free[tb_ % 2] = dma(SC, nc.scalar, d_ws[tb_ % 2], Wd[tb_], WS[tb_ % 2], t1)
            t_w.extend([ws_free[0], ws_free[1], tok, t1, c3[-1]])

        t_ad = [None] * SPILL

        def ahead_products():
            for c in range(SPILL):
                t_ad[c] = []
                for half in range(2):
                    s, (wh, wl) = next_slot("u", c)
                    for j in range(2):
                        i = 2 * half + j
                        b, tok = from_features(s, wh, wl, j)
                        g = GTMP.get()
                        t1 = act(g.ap, b.ap, ACT.Gelu_apprx_tanh, tok, g.free)
                        banks.put(b, t1)
                        t2 = dma(SC, nc.scalar, g.counter, Ad[c][:, i * S:(i + 1) * S], g.ap, t1)
                        GTMP.put(g, t2)
                        t_ad[c].append(t2)
                        if j == 1:
                            parts.put(s, tok)
                        yield

        others = ahead_products()
        beside(best_pairs(), others, RATIO[0])
        beside(weights(), others, RATIO[1])
        drain(others)

        window.close()
        GE = [[sb(f"ge{i}{p}", 4 * S, f32r)[:, :].rearrange("p (k n) -> p k n", k=4) for p in range(2)] for i in range(2)]
        Y = sb("y", 8 * S)[:, :].rearrange("p (k n) -> p k n", k=8)
        wring = Pool([Place(sb(f"wr{i}", 4 * S)[:, :], sem(f"s_wr{i}")) for i in range(2)])
        GIN = Pool([Place(sb(f"gin{i}", 4 * S)[:, :].rearrange("p (k n) -> p k n", k=4), sem(f"s_gin{i}")) for i in range(2)])
        for p_ in wring.q + GIN.q:
            p_.free = [t_w]
        ge_free = [t_w, t_w]
        t_yy = [None] * 8

        def peer_up(n_):
            c = sequence[n_]
            wr = wring.get()
            wt = dma(SP, nc.sync, wr.counter, wr.ap.rearrange("p (b i) -> p b i", b=16),
                     Wd.rearrange("b p (c i) -> c p b i", c=32)[c], wr.free, t_w)
            ww = wr.ap.rearrange("p (b i t) -> p i b t", b=16, i=4)
            gh, gl = GE[n_ % 2]
            gin = GIN.get()
            if c < SPILL:
                tg = dma(SP, nc.sync, gin.counter, gin.ap, Ad[c].rearrange("p (k n) -> p k n", k=4), gin.free, t_ad[c])
            toks = []
            for i in range(4):
                g = gin.ap[:, i, :]
                if c >= SPILL:
                    if i % 2 == 0:
                        s, (wh, wl) = next_slot("u", c)
                    b, tok = from_features(s, wh, wl, i % 2)
                    tg = act(g, b.ap, ACT.Gelu_apprx_tanh, tok, gin.free)
                    banks.put(b, tg)
                    if i % 2:
                        parts.put(s, tok)
                g3 = g.rearrange("p (b t) -> p b t", b=16)
                t2 = tt(g3, g3, ww[:, i, :, :], MUL, tg, wt)
                toks.append(split(gh[:, i, :], gl[:, i, :], g, t2, ge_free[n_ % 2]))
            GIN.put(gin, toks[-1])
            wring.put(wr, t2)
            return toks

        def peer_down(n_, ready, first):
            c = sequence[n_]
            gh, gl = GE[n_ % 2]
            for half in range(2):
                s, (wh, wl) = first if first and not half else next_slot("v", c)
                for j in range(4):
                    d = half * 4 + j
                    b = banks.get()
                    js = slice(j * 128, (j + 1) * 128)
                    tok = mms(b.ap, [p for k in range(4) for p in three(wh[:, k, js], wl[:, k, js], gh[:, k, :], gl[:, k, :])],
                              b.free, s.ready, ready)
                    if n_ == 0:
                        t_yy[d] = vcopy(Y[:, d, :], b.ap, tok, t_w)
                    else:
                        t_yy[d] = tt(Y[:, d, :], Y[:, d, :], b.ap, ADD, tok, t_yy[d])
                    banks.put(b, t_yy[d])
                    if n_ == 31:
                        t_x[d] = stt(X[:, d, :], Y[:, d, :], MOD[:, 40 + d, 0:1], X[:, d, :], MUL, ADD, t_yy[d])
                parts.put(s, tok)
            ge_free[n_ % 2] = tok

        ready = peer_up(0)
        for n_ in range(32):
            first = next_slot("v", sequence[n_]) if n_ == 31 or sequence[n_ + 1] < SPILL else None
            nxt = peer_up(n_ + 1) if n_ < 31 else None
            peer_down(n_, ready, first)
            ready = nxt

        r, tr = factor([X[:, k, :] for k in range(8)], ones, 1.0 / D, S, each=t_x)
        for k in range(8):
            t1 = stt(Y[:, k, :], X[:, k, :], par("gfin", k), r, MUL, MUL, tr)
            t_o = dma(SP, nc.sync, d_o, out[k * 128:(k + 1) * 128, :], Y[:, k, :], t1)
        SP.wait(t_o)

        block = ctx.enter_context(nc.Block())

        @block.sync
        def _(eng):
            SP.run(eng)

        @block.gpsimd
        def _(eng):
            GP.run(eng)

        @block.scalar
        def _(eng):
            SC.run(eng)

        @block.vector
        def _(eng):
            DVE.run(eng)

        @block.tensor
        def _(eng):
            PE.run(eng)


def constants():
    f = np.float32
    i = np.arange(128)
    c = {
        "ident": np.eye(128), "ones": np.ones((128, 128)),
        "blk": (i[:, None] // 64 == i[None] // 64),
        "linc": (i[:, None] >= i[None]), "smask": (i[None] > i[:, None]),
        "nmask": np.where(i[None] > i[:, None], 0.0, -BIG),
        "iota": np.broadcast_to(i, (128, 128)),
    }
    rot = np.zeros((128, 128))
    for d in range(128):
        if d % 32 < 16:
            rot[d + 16, d] = -1.0
        else:
            rot[d - 16, d] = 1.0
    c["rot"] = rot
    consts = np.concatenate([np.asarray(c[n], f) for n in CNAMES], axis=1)
    tpos = np.arange(S)
    row, col = (tpos // 64).astype(f), (tpos % 64).astype(f)
    inv = f(10000.0) ** (-np.arange(0, 32, 2, dtype=f) / f(32))
    ar, ac = row[:, None] * inv, col[:, None] * inv
    ang = np.concatenate([ar, ar, ac, ac], axis=-1).astype(f).T
    ang = np.concatenate([ang, ang], axis=0)
    rope = np.stack([np.cos(ang), np.sin(ang)]).astype(f)
    t01 = np.linspace(0.0, 1.0, S, dtype=f)[:, None]
    w = (f(2.0 * math.pi) * np.arange(S, dtype=f)[:, None] / f(S)).astype(f)
    fr = np.linspace(1e-4, 15, 16, dtype=f)[None]
    zf = np.concatenate([t01, np.cos(fr * w), -np.sin(fr * w)], axis=-1).astype(f).T
    deltas = np.abs(np.linspace(math.log(1e-2) / 1.5, math.log(1e-2) / 0.3, 512, dtype=f))
    dec = np.exp(-t01 * deltas).astype(f)
    n = np.arange(S)
    ph = (n[:, None] * n[None]) % 1024 * (2.0 * math.pi / 1024)
    fc, fs = np.cos(ph), np.sin(ph)
    fs[:, 0] = np.where(n % 2 == 0, 1.0, -1.0)
    dft = np.stack([fc, fs, fs.T, dec]).astype(f)
    tid = (np.arange(4, dtype=np.uint32)[None] * 128 + np.arange(128, dtype=np.uint32)[:, None])
    return {"tid": np.ascontiguousarray(tid), "consts": consts, "rope": np.ascontiguousarray(rope), "zf": np.ascontiguousarray(zf), "dft": dft}


def layout(I):
    c = np.ascontiguousarray

    def cols(x):
        return np.asarray(x).reshape(-1, 128).T

    def twice(x):
        return np.concatenate([x, x]).reshape(128, 1)

    def pad(x):
        return np.concatenate([x, x]).reshape(128, 1)

    p = {
        "g1": cols(I["norm_mix_g"]), "gf1": cols(I["norm_ffn_g"]),
        "qg1": twice(I["q_norm_g"][0]), "kg1": twice(I["k_norm_g"][0]),
        "cw": cols(I["conv_w"]),
        "rb": np.broadcast_to(np.concatenate([I["b_router_group"][0], I["b_router_expert"][0]]), (128, 36)),
        "ab": cols(I["ada_b_2"]), "g2": cols(I["norm_mix_g_2"]), "gf2": cols(I["norm_ffn_g_2"]),
        "gfin": cols(I["final_norm_g_2"]), "qg2": twice(I["q_norm_g_2"][0]), "kg2": twice(I["k_norm_g_2"][0]),
        "hcw": cols(I["hy_conv_w_2"]), "hcb": cols(I["hy_conv_b_2"]),
        "hb1": pad(I["hf_b1_2"][0]), "hb2": pad(I["hf_b2_2"][0]), "hb3": pad(I["hf_b3_2"][0]), "hfr": pad(I["hf_freq_2"][0]),
        "cc": np.stack([cols(I["c_2"]), cols(I["c_ctx_2"])], axis=2).reshape(128, 16),
    }
    params = np.concatenate([p[n] for n in PCOLS], axis=1)
    w2 = I["w_in_2"][0]
    qc = w2[:, 0:512].reshape(D, 2, 4, 64).transpose(0, 2, 1, 3).reshape(D, 512)
    w_in_2 = np.concatenate([w2[:, 768:2304], qc, w2[:, 2304:4352], w2[:, 512:768]], axis=1)
    wa = I["w_attn_out_2"][0].reshape(2, 4, 64, D).transpose(1, 0, 2, 3).reshape(512, D)
    keys = np.stack([I["peer_keys1_2"][0], I["peer_keys2_2"][0]], axis=1)
    u = I["peer_u_2"][0].reshape(64, 256, 8, 128).transpose(0, 3, 2, 1)
    skip = np.broadcast_to(I["hy_skip_2"][0].reshape(1, 1024), (128, 1024))
    out = {
        "params": c(params), "x": c(I["x"][0].T), "ctx": c(I["ctx_2"][0].T),
        "w_in": I["w_in"][0], "w_sb": I["w_sb_branch"][0], "w_conv": I["w_conv_branch"][0], "w_out": I["w_out"][0],
        "w_router": c(np.concatenate([I["w_router_group"][0], I["w_router_expert"][0]], axis=1)),
        "w_gate": I["w_gate_e"][0], "w_up": I["w_up_e"][0], "w_down": I["w_down_e"][0],
        "ada_w": I["ada_w_2"][0], "w_in_2": c(w_in_2), "w_attn": c(wa), "w_hy": I["w_hy_out_2"][0],
        "w_out_2": I["w_out_2"][0], "wq": I["peer_wq_2"][0],
        "keys": c(keys.transpose(3, 0, 1, 2).reshape(128, 2048)),
        "u": c(u), "v": I["peer_v_2"][0], "skip": c(skip),
        "hf_w1": I["hf_w1_2"][0], "hf_w2": I["hf_w2_2"][0], "hf_w3": I["hf_w3_2"][0], "hf_w4": I["hf_w4_2"][0],
    }
    return {k: c(np.asarray(x)) for k, x in out.items()}


def kernel(**inputs):
    import concourse.bacc as bacc
    from concourse.bass_utils import run_bass_kernel_spmd

    arrays = layout({k: np.asarray(x) for k, x in inputs.items()})
    arrays.update(constants())
    nc = bacc.Bacc("TRN2", target_bir_lowering=False, num_devices=1)
    feeds, A = {}, {}
    for name, x in arrays.items():
        feeds[f"in_{name}"] = x
        A[name] = nc.dram_tensor(f"in_{name}", x.shape, mybir.dt.from_np(x.dtype), kind="ExternalInput").ap()
    out = nc.dram_tensor("out_0", (D, S), mybir.dt.float32, kind="ExternalOutput").ap()
    program(nc, A, out)
    r = run_bass_kernel_spmd(nc, [feeds], core_ids=[0])
    return np.ascontiguousarray(r.results[0]["out_0"].T)[None]
```
